# Optimizing a Trainium2 kernel written in Bass

```python
import jax
import jax.numpy as jnp
from jax import lax
import numpy as np

D_MODEL = 1024
BATCH = 1
SEQ = 256
DEPTH = 2

GRID_W = 64
CTX_LEN = 256
EPS = 1e-6
LRU_WIDTH = D_MODEL // 2
LRU_BLOCKS = 8
LRU_BLOCK = LRU_WIDTH // LRU_BLOCKS
CONV_W = 4
LRU_C = 8.0
ATT_HEADS = 8
ATT_KV_HEADS = 2
HEAD_DIM = 64
WINDOW = 128
ATT_BLOCK = 128
ROPE_BASE = 10000.0
ATT_Q_WIDTH = ATT_HEADS * HEAD_DIM
ATT_KV_WIDTH = ATT_KV_HEADS * HEAD_DIM
EVEN_IN = 2 * LRU_WIDTH + ATT_Q_WIDTH + 2 * ATT_KV_WIDTH
EVEN_MIX = LRU_WIDTH + ATT_Q_WIDTH
GLA_HEADS = 4
GLA_DK = D_MODEL // 2 // GLA_HEADS
GLA_DV = D_MODEL // GLA_HEADS
GLA_LOWRANK = 16
GLA_TAU = 16.0
GLA_CHUNK = 64
GLA_K_WIDTH = GLA_HEADS * GLA_DK
GLA_V_WIDTH = GLA_HEADS * GLA_DV
ODD_IN = 2 * GLA_K_WIDTH + 2 * GLA_V_WIDTH + 2 * GLA_LOWRANK
ODD_MIX = GLA_V_WIDTH
N_EXPERTS = 16
N_GROUPS = 4
EXPERTS_PER_GROUP = N_EXPERTS // N_GROUPS
TOP_K = 2
D_EXPERT = 512

kernel_name = 'hybrid_rglru_swa_gla_moe_prefix_dit'

def rms_norm(x, g):
    x32 = x.astype(jnp.float32)
    y = x32 * lax.rsqrt(jnp.mean(x32 * x32, axis=-1, keepdims=True) + EPS)
    return y.astype(x.dtype) * g

def modulate(h, g, shift, scale):
    return rms_norm(h, g) * (1.0 + scale) + shift

def axial_rope_tables(n_tokens):
    rows = n_tokens // GRID_W
    row = jnp.repeat(jnp.arange(rows), GRID_W).astype(jnp.float32)
    col = jnp.tile(jnp.arange(GRID_W), rows).astype(jnp.float32)
    n_freq = HEAD_DIM // 4
    inv_freq = ROPE_BASE ** (-jnp.arange(n_freq, dtype=jnp.float32) / n_freq)
    ang_r = row[:, None] * inv_freq
    ang_c = col[:, None] * inv_freq
    return (jnp.cos(ang_r), jnp.sin(ang_r), jnp.cos(ang_c), jnp.sin(ang_c))

def _rotate(x, cos, sin):
    x1, x2 = jnp.split(x, 2, axis=-1)
    return jnp.concatenate([x1 * cos - x2 * sin, x2 * cos + x1 * sin], axis=-1)

def apply_axial_rope(x, tables):
    cr, sr, cc, sc = (t.astype(x.dtype)[:, None, :] for t in tables)
    xr, xc = jnp.split(x, 2, axis=-1)
    return jnp.concatenate([_rotate(xr, cr, sr), _rotate(xc, cc, sc)], axis=-1)

def centred_depthwise_conv(u, w, b):
    left = (CONV_W - 1) // 2
    y = lax.conv_general_dilated(u, w[:, None, :], window_strides=(1,),
                                 padding=[(left, CONV_W - 1 - left)],
                                 dimension_numbers=('NWC', 'WIO', 'NWC'),
                                 feature_group_count=u.shape[-1])
    return y + b

def block_diagonal(u, w, b):
    ub = u.reshape(u.shape[:-1] + (LRU_BLOCKS, LRU_BLOCK))
    return jnp.einsum('btnc,ncd->btnd', ub, w).reshape(u.shape) + b

def linear_recurrence(a, b, h0, reverse):
    if h0 is not None:
        edge = -1 if reverse else 0
        b = b.at[:, edge].add(a[:, edge] * h0)

    def combine(left, right):
        a_l, b_l = left
        a_r, b_r = right
        return a_l * a_r, a_r * b_l + b_r

    return lax.associative_scan(combine, (a, b), reverse=reverse, axis=1)[1]

def rglru_direction(u, w_r, b_r, w_i, b_i, lam, h0, reverse):
    r = jax.nn.sigmoid(block_diagonal(u, w_r, b_r).astype(jnp.float32))
    i = jax.nn.sigmoid(block_diagonal(u, w_i, b_i).astype(jnp.float32))
    log_a = -LRU_C * r * jax.nn.softplus(-lam.astype(jnp.float32))
    x_in = jnp.sqrt(-jnp.expm1(2.0 * log_a)) * (i * u.astype(jnp.float32))
    return linear_recurrence(jnp.exp(log_a), x_in, h0, reverse)

def rglru_group(u_lat, u_ctx, g_lat, g_ctx, conv_w, conv_b, w_r, b_r, w_i, b_i, lam, need_ctx_out):
    u_lat = centred_depthwise_conv(u_lat, conv_w, conv_b)
    u_ctx = centred_depthwise_conv(u_ctx, conv_w, conv_b)
    h_lat = 0.0
    h_ctx = 0.0
    for d, reverse in enumerate((False, True)):
        hc = rglru_direction(u_ctx, w_r[d], b_r[d], w_i[d], b_i[d], lam[d], None, reverse)
        h0 = hc[:, 0] if reverse else hc[:, -1]
        h_lat = h_lat + rglru_direction(u_lat, w_r[d], b_r[d], w_i[d], b_i[d], lam[d], h0, reverse)
        if need_ctx_out:
            h_ctx = h_ctx + hc
    y_lat = h_lat.astype(u_lat.dtype) * jax.nn.gelu(g_lat)
    y_ctx = h_ctx.astype(u_ctx.dtype) * jax.nn.gelu(g_ctx) if need_ctx_out else None
    return y_lat, y_ctx

def windowed_attention(q, k, v, k_ctx, v_ctx, sink):
    B, T, H, hd = q.shape
    KV = k.shape[2]
    G = H // KV
    nb = T // ATT_BLOCK
    scale = hd ** -0.5
    qb = q.reshape(B, nb, ATT_BLOCK, KV, G, hd)
    pad = ((0, 0), (ATT_BLOCK, ATT_BLOCK), (0, 0), (0, 0))
    kp = jnp.pad(k, pad).reshape(B, nb + 2, ATT_BLOCK, KV, hd)
    vp = jnp.pad(v, pad).reshape(B, nb + 2, ATT_BLOCK, KV, hd)

    def band(t):
        return jnp.concatenate([t[:, :-2], t[:, 1:-1], t[:, 2:]], axis=2)

    kw, vw = band(kp), band(vp)
    qi = jnp.arange(ATT_BLOCK)[:, None]
    ks = jnp.arange(3 * ATT_BLOCK)[None, :]
    kpos = (jnp.arange(nb) * ATT_BLOCK - ATT_BLOCK)[:, None, None] + ks[None]
    mask = (jnp.abs(ks - ATT_BLOCK - qi) <= WINDOW)[None] & (kpos >= 0) & (kpos < T)
    s_win = jnp.einsum('bnikgd,bnskd->bnkgis', qb, kw).astype(jnp.float32) * scale
    s_win = jnp.where(mask[None, :, None, None], s_win, -1e30)
    s_ctx = jnp.einsum('bnikgd,blkd->bnkgil', qb, k_ctx).astype(jnp.float32) * scale
    s_sink = sink.astype(jnp.float32).reshape(1, 1, KV, G, 1, 1)
    m = jnp.maximum(jnp.maximum(s_win.max(-1, keepdims=True), s_ctx.max(-1, keepdims=True)), s_sink)
    e_win = jnp.exp(s_win - m)
    e_ctx = jnp.exp(s_ctx - m)
    denom = e_win.sum(-1, keepdims=True) + e_ctx.sum(-1, keepdims=True) + jnp.exp(s_sink - m)
    o = (jnp.einsum('bnkgis,bnskd->bnkgid', e_win.astype(v.dtype), vw)
         + jnp.einsum('bnkgil,blkd->bnkgid', e_ctx.astype(v.dtype), v_ctx)) / denom.astype(v.dtype)
    return jnp.transpose(o, (0, 1, 4, 2, 3, 5)).reshape(B, T, H * hd)

def context_attention(q, k, v, sink):
    B, L, H, hd = q.shape
    KV = k.shape[2]
    G = H // KV
    qg = q.reshape(B, L, KV, G, hd)
    s = jnp.einsum('blkgd,bmkd->bkglm', qg, k).astype(jnp.float32) * hd ** -0.5
    s_sink = jnp.broadcast_to(sink.astype(jnp.float32).reshape(1, KV, G, 1, 1), s.shape[:-1] + (1,))
    p = jax.nn.softmax(jnp.concatenate([s, s_sink], axis=-1), axis=-1)[..., :L].astype(v.dtype)
    return jnp.einsum('bkglm,bmkd->blkgd', p, v).reshape(B, L, H * hd)

def rglru_swa_layer(n_lat, n_ctx, rope, w_in, w_out, conv_w, conv_b, rg_w, rg_b, ig_w, ig_b,
                    lam, q_g, k_g, sink, need_ctx_out):
    splits = [LRU_WIDTH, 2 * LRU_WIDTH, 2 * LRU_WIDTH + ATT_Q_WIDTH,
              2 * LRU_WIDTH + ATT_Q_WIDTH + ATT_KV_WIDTH]

    def project(n):
        B, L = n.shape[:2]
        u, gate, q, k, v = jnp.split(n @ w_in, splits, axis=-1)
        q = rms_norm(q.reshape(B, L, ATT_HEADS, HEAD_DIM), q_g)
        k = rms_norm(k.reshape(B, L, ATT_KV_HEADS, HEAD_DIM), k_g)
        return u, gate, q, k, v.reshape(B, L, ATT_KV_HEADS, HEAD_DIM)

    u_l, g_l, q_l, k_l, v_l = project(n_lat)
    u_c, g_c, q_c, k_c, v_c = project(n_ctx)
    q_l = apply_axial_rope(q_l, rope)
    k_l = apply_axial_rope(k_l, rope)
    a_lat, a_ctx = rglru_group(u_l, u_c, g_l, g_c, conv_w, conv_b, rg_w, rg_b, ig_w, ig_b, lam,
                               need_ctx_out)
    b_lat = windowed_attention(q_l, k_l, v_l, k_c, v_c, sink)
    y_lat = jnp.concatenate([a_lat, b_lat], axis=-1) @ w_out
    if not need_ctx_out:
        return y_lat, None
    b_ctx = context_attention(q_c, k_c, v_c, sink)
    y_ctx = jnp.concatenate([a_ctx, b_ctx], axis=-1) @ w_out
    return y_lat, y_ctx

def gla_chunked(q, k, v, log_a, s0, with_output):
    B, T, H, dk = k.shape
    dv = v.shape[-1]
    nc = T // GLA_CHUNK
    kc = k.astype(jnp.float32).reshape(B, nc, GLA_CHUNK, H, dk)
    vc = v.astype(jnp.float32).reshape(B, nc, GLA_CHUNK, H, dv)
    b = jnp.cumsum(log_a.reshape(B, nc, GLA_CHUNK, H, dk), axis=2)
    g = b[:, :, -1]
    k_end = kc * jnp.exp(g[:, :, None] - b)
    if s0 is None:
        s0 = jnp.zeros((B, H, dk, dv), jnp.float32)

    def chunk_major(t):
        return jnp.moveaxis(t, 1, 0)

    if not with_output:
        def carry_only(S, xs):
            k_n, v_n, g_n = xs
            return jnp.exp(g_n)[..., None] * S + jnp.einsum('bshd,bshv->bhdv', k_n, v_n), None

        s_final, _ = lax.scan(carry_only, s0, (chunk_major(k_end), chunk_major(vc), chunk_major(g)))
        return None, s_final
    q_dec = q.astype(jnp.float32).reshape(B, nc, GLA_CHUNK, H, dk) * jnp.exp(b)

    def step(S, xs):
        q_n, k_n, v_n, g_n = xs
        o_n = jnp.einsum('bthd,bhdv->bthv', q_n, S)
        S = jnp.exp(g_n)[..., None] * S + jnp.einsum('bshd,bshv->bhdv', k_n, v_n)
        return S, o_n

    s_final, o_inter = lax.scan(step, s0, (chunk_major(q_dec), chunk_major(k_end),
                                           chunk_major(vc), chunk_major(g)))
    k_inc = kc * jnp.exp(-b)
    intra = jnp.einsum('bnthd,bnshd->bnhts', q_dec, k_inc)
    intra = jnp.where(jnp.tril(jnp.ones((GLA_CHUNK, GLA_CHUNK), bool)), intra, 0.0)
    o = jnp.einsum('bnhts,bnshv->bnthv', intra, vc) + jnp.moveaxis(o_inter, 0, 1)
    return o.reshape(B, T, H, dv), s_final

def gla_direction(q, k, v, log_a, s0, reverse, with_output):
    if not reverse:
        return gla_chunked(q, k, v, log_a, s0, with_output)
    flip = lambda t: jnp.flip(t, axis=1)
    o, s = gla_chunked(flip(q), flip(k), flip(v), flip(log_a), s0, with_output)
    return (flip(o) if o is not None else None), s

def gla_layer(n_lat, n_ctx, w_in, w_out, gate_up, gate_b, out_norm_g, need_ctx_out):
    splits = [GLA_K_WIDTH, 2 * GLA_K_WIDTH, 2 * GLA_K_WIDTH + GLA_V_WIDTH,
              2 * GLA_K_WIDTH + 2 * GLA_V_WIDTH, 2 * GLA_K_WIDTH + 2 * GLA_V_WIDTH + GLA_LOWRANK]

    def project(n):
        B, L = n.shape[:2]
        q, k, v, r, a_f, a_b = jnp.split(n @ w_in, splits, axis=-1)
        q = q.reshape(B, L, GLA_HEADS, GLA_DK) * GLA_DK ** -0.5
        k = k.reshape(B, L, GLA_HEADS, GLA_DK)
        v = v.reshape(B, L, GLA_HEADS, GLA_DV)
        log_a = [(jax.nn.log_sigmoid((a_d @ gate_up[d] + gate_b[d]).astype(jnp.float32)) / GLA_TAU)
                 .reshape(B, L, GLA_HEADS, GLA_DK) for d, a_d in enumerate((a_f, a_b))]
        return q, k, v, r, log_a

    ql, kl, vl, rl, la_l = project(n_lat)
    qc, kc, vc, rc, la_c = project(n_ctx)
    o_lat = 0.0
    o_ctx = 0.0
    for d, reverse in enumerate((False, True)):
        oc, s_ctx = gla_direction(qc, kc, vc, la_c[d], None, reverse, need_ctx_out)
        ol, _ = gla_direction(ql, kl, vl, la_l[d], s_ctx, reverse, True)
        o_lat = o_lat + ol
        if need_ctx_out:
            o_ctx = o_ctx + oc

    def finish(o, r, n):
        B, L = n.shape[:2]
        o = rms_norm(o.astype(n.dtype), out_norm_g).reshape(B, L, GLA_V_WIDTH)
        return (o * jax.nn.silu(r)) @ w_out

    y_lat = finish(o_lat, rl, n_lat)
    y_ctx = finish(o_ctx, rc, n_ctx) if need_ctx_out else None
    return y_lat, y_ctx

def grouped_top2_moe(h, router_w, router_bias, w_gate, w_up, w_down):
    scores = jax.nn.sigmoid(h.astype(jnp.float32) @ router_w.astype(jnp.float32))
    sel = scores + router_bias.astype(jnp.float32)
    group_score = lax.top_k(sel.reshape(-1, N_GROUPS, EXPERTS_PER_GROUP), TOP_K)[0].sum(-1)
    best_group = jnp.argmax(group_score, axis=-1)
    in_group = (jnp.arange(N_EXPERTS) // EXPERTS_PER_GROUP)[None, :] == best_group[:, None]
    _, idx = lax.top_k(jnp.where(in_group, sel, -jnp.inf), TOP_K)
    w = jnp.take_along_axis(scores, idx, axis=-1)
    w = w / jnp.sum(w, axis=-1, keepdims=True)
    combine = jnp.sum(jax.nn.one_hot(idx, N_EXPERTS, dtype=jnp.float32) * w[..., None], axis=1)
    combine = combine.astype(h.dtype)
    out = jnp.zeros_like(h)
    for e in range(N_EXPERTS):
        y = (jax.nn.silu(h @ w_gate[e]) * (h @ w_up[e])) @ w_down[e]
        out = out + combine[:, e:e + 1] * y
    return out

def setup_inputs(seed: int = 0) -> dict:
    key = jax.random.key(seed)
    keys = iter(jax.random.split(key, 40))
    D = D_MODEL
    n_even = (DEPTH + 1) // 2
    n_odd = DEPTH // 2

    def nrm(shape, scale):
        return jax.random.normal(next(keys), shape, jnp.float32) * scale

    x = nrm((BATCH, SEQ, D), 1.0)
    c = nrm((BATCH, D), 1.0)
    ctx = nrm((BATCH, CTX_LEN, D), 1.0)
    c_ctx = nrm((D,), 1.0)
    router_w = nrm((D, N_EXPERTS), D ** -0.5)
    router_bias = nrm((N_EXPERTS,), 0.01)
    ada_w = nrm((DEPTH, D, 6 * D), 0.02)
    ada_b = nrm((DEPTH, 6 * D), 0.02)
    norm_mix_g = 1.0 + nrm((DEPTH, D), 0.02)
    norm_ffn_g = 1.0 + nrm((DEPTH, D), 0.02)
    moe_w_gate = nrm((DEPTH, N_EXPERTS, D, D_EXPERT), D ** -0.5)
    moe_w_up = nrm((DEPTH, N_EXPERTS, D, D_EXPERT), D ** -0.5)
    moe_w_down = nrm((DEPTH, N_EXPERTS, D_EXPERT, D), D_EXPERT ** -0.5)
    ev_w_in = nrm((n_even, D, EVEN_IN), D ** -0.5)
    ev_w_out = nrm((n_even, EVEN_MIX, D), EVEN_MIX ** -0.5)
    ev_conv_w = nrm((n_even, CONV_W, LRU_WIDTH), CONV_W ** -0.5)
    ev_conv_b = nrm((n_even, LRU_WIDTH), 0.02)
    ev_rg_w = nrm((n_even, 2, LRU_BLOCKS, LRU_BLOCK, LRU_BLOCK), LRU_BLOCK ** -0.5)
    ev_rg_b = nrm((n_even, 2, LRU_WIDTH), 0.02)
    ev_ig_w = nrm((n_even, 2, LRU_BLOCKS, LRU_BLOCK, LRU_BLOCK), LRU_BLOCK ** -0.5)
    ev_ig_b = nrm((n_even, 2, LRU_WIDTH), 0.02)
    a_pow = jax.random.uniform(next(keys), (n_even, 2, LRU_WIDTH), jnp.float32, 0.9, 0.999)
    a_base = a_pow ** (1.0 / LRU_C)
    ev_lambda = jnp.log(a_base) - jnp.log1p(-a_base)
    ev_q_norm_g = 1.0 + nrm((n_even, HEAD_DIM), 0.02)
    ev_k_norm_g = 1.0 + nrm((n_even, HEAD_DIM), 0.02)
    ev_sink = nrm((n_even, ATT_HEADS), 1.0)
    od_w_in = nrm((n_odd, D, ODD_IN), D ** -0.5)
    od_w_out = nrm((n_odd, ODD_MIX, D), ODD_MIX ** -0.5)
    od_gate_up = nrm((n_odd, 2, GLA_LOWRANK, GLA_K_WIDTH), GLA_LOWRANK ** -0.5)
    od_gate_b = nrm((n_odd, 2, GLA_K_WIDTH), 0.02)
    od_out_norm_g = 1.0 + nrm((n_odd, GLA_DV), 0.02)
    return {'x': x, 'c': c, 'ctx': ctx, 'c_ctx': c_ctx, 'router_w': router_w,
            'router_bias': router_bias, 'ada_w': ada_w, 'ada_b': ada_b,
            'norm_mix_g': norm_mix_g, 'norm_ffn_g': norm_ffn_g, 'moe_w_gate': moe_w_gate,
            'moe_w_up': moe_w_up, 'moe_w_down': moe_w_down, 'ev_w_in': ev_w_in,
            'ev_w_out': ev_w_out, 'ev_conv_w': ev_conv_w, 'ev_conv_b': ev_conv_b,
            'ev_rg_w': ev_rg_w, 'ev_rg_b': ev_rg_b, 'ev_ig_w': ev_ig_w, 'ev_ig_b': ev_ig_b,
            'ev_lambda': ev_lambda, 'ev_q_norm_g': ev_q_norm_g, 'ev_k_norm_g': ev_k_norm_g,
            'ev_sink': ev_sink, 'od_w_in': od_w_in, 'od_w_out': od_w_out,
            'od_gate_up': od_gate_up, 'od_gate_b': od_gate_b, 'od_out_norm_g': od_out_norm_g}

def reference(x, c, ctx, c_ctx, router_w, router_bias, ada_w, ada_b, norm_mix_g, norm_ffn_g,
              moe_w_gate, moe_w_up, moe_w_down, ev_w_in, ev_w_out, ev_conv_w, ev_conv_b,
              ev_rg_w, ev_rg_b, ev_ig_w, ev_ig_b, ev_lambda, ev_q_norm_g, ev_k_norm_g, ev_sink,
              od_w_in, od_w_out, od_gate_up, od_gate_b, od_out_norm_g):
    B, T, D = x.shape
    rope = axial_rope_tables(T)
    h_lat, h_ctx = x, ctx
    cond_lat = jax.nn.silu(c)[:, None, :]
    cond_ctx = jax.nn.silu(c_ctx)[None, None, :]
    for layer in range(DEPTH):
        last = layer == DEPTH - 1
        j = layer // 2
        mod_lat = jnp.split(cond_lat @ ada_w[layer] + ada_b[layer], 6, axis=-1)
        mod_ctx = jnp.split(cond_ctx @ ada_w[layer] + ada_b[layer], 6, axis=-1)
        n_lat = modulate(h_lat, norm_mix_g[layer], mod_lat[0], mod_lat[1])
        n_ctx = modulate(h_ctx, norm_mix_g[layer], mod_ctx[0], mod_ctx[1])
        if layer % 2 == 0:
            y_lat, y_ctx = rglru_swa_layer(n_lat, n_ctx, rope, ev_w_in[j], ev_w_out[j], ev_conv_w[j],
                                           ev_conv_b[j], ev_rg_w[j], ev_rg_b[j], ev_ig_w[j],
                                           ev_ig_b[j], ev_lambda[j], ev_q_norm_g[j],
                                           ev_k_norm_g[j], ev_sink[j], not last)
        else:
            y_lat, y_ctx = gla_layer(n_lat, n_ctx, od_w_in[j], od_w_out[j], od_gate_up[j],
                                     od_gate_b[j], od_out_norm_g[j], not last)
        h_lat = h_lat + mod_lat[2] * y_lat
        rows = modulate(h_lat, norm_ffn_g[layer], mod_lat[3], mod_lat[4]).reshape(-1, D)
        if not last:
            h_ctx = h_ctx + mod_ctx[2] * y_ctx
            f_ctx = modulate(h_ctx, norm_ffn_g[layer], mod_ctx[3], mod_ctx[4])
            rows = jnp.concatenate([rows, f_ctx.reshape(-1, D)], axis=0)
        ffn = grouped_top2_moe(rows, router_w, router_bias, moe_w_gate[layer], moe_w_up[layer],
                               moe_w_down[layer])
        h_lat = h_lat + mod_lat[5] * ffn[:B * T].reshape(B, T, D)
        if not last:
            h_ctx = h_ctx + mod_ctx[5] * ffn[B * T:].reshape(h_ctx.shape)
    return h_lat


_drawn_inputs = setup_inputs


def setup_inputs(seed=0):
    import zlib

    import numpy as np

    out = dict(_drawn_inputs(seed))
    spreads = {}
    factors = {'ev_rg_b': 7.806,
     'ev_q_norm_g': 7.998,
     'ev_k_norm_g': 8.0,
     'ev_sink': 8.0,
     'od_gate_b': 8.0,
     'od_out_norm_g': 12.8,
     'ev_ig_b': 8.0}
    for name, (base, spread) in spreads.items():
        noise = np.random.default_rng([zlib.crc32(name.encode()), seed]).standard_normal(out[name].shape)
        drawn = base * np.exp(spread * noise) if base else spread * noise
        out[name] = jnp.asarray(drawn.astype(out[name].dtype))
    for name, factor in factors.items():
        out[name] = (out[name] * factor).astype(out[name].dtype)
    return out
```

```python
from contextlib import ExitStack

import concourse.bass as bass
from concourse import mybir

F32 = mybir.dt.float32
ALU = mybir.AluOpType
ACT = mybir.ActivationFunctionType
AX_X = mybir.AxisListType.X

P = 128
D = 1024
KD = D // P
EPS = 1e-6
NEG = -1e30
N_EXPERTS = 16
D_EXPERT = 512
FT = D_EXPERT // P
RING = 3
SLOT = 4096
CREDIT = 1
ATT_SCALE = 64 ** -0.5
CHUNK = 64
DK = 128
DV = 256
HEADS = 4

ADA_EARLY = 4
ADA_LATE = 8
L0_SLOTS = ADA_EARLY + 4 + ADA_LATE + 2
MOE_SLOTS = 3 * N_EXPERTS
L1_SLOTS = ADA_EARLY + 7 + ADA_LATE + 2
L1_BASE = L0_SLOTS + MOE_SLOTS
L1_MOE = L1_BASE + L1_SLOTS


class Chain:

    def __init__(self, eng, sem):
        self.eng, self.sem, self.n = eng, sem, 0

    def __call__(self, ins):
        self.add(ins)
        self.wait()

    def add(self, ins):
        ins.then_inc(self.sem, 1)
        self.n += 1

    def wait(self):
        self.eng.wait_ge(self.sem, self.n)


def build(nc, x, c, ctx, c_ctx, router_w, router_bias, ada_w, ada_b, norm_mix_g, norm_ffn_g,
          moe_w_gate, moe_w_up, moe_w_down, ev_w_in, ev_w_out, ev_conv_w, ev_conv_b,
          ev_rg_w, ev_rg_b, ev_ig_w, ev_ig_b, ev_lambda, ev_q_norm_g, ev_k_norm_g, ev_sink,
          od_w_in, od_w_out, od_gate_up, od_gate_b, od_out_norm_g, rope_cos, rope_sin, out):
    with ExitStack() as stack:
        def sb(name, shape):
            return stack.enter_context(nc.sbuf_tensor(name, shape, F32))

        def sem(name):
            return stack.enter_context(nc.semaphore(name))

        ps = stack.enter_context(nc.psum_tensor("ps", [P, 8, 512], F32))

        ring = sb("ring", [P, RING, SLOT])
        h = sb("h", [P, 4, D])
        nT = sb("nT", [P, KD, 512])
        xn = sb("xn", [P, 4, D])
        region_r = sb("region_r", [P, 2048])
        region_u = sb("region_u", [P, 2048])
        region_g = sb("region_g", [P, 2048])
        region_q = sb("region_q", [P, 2560])
        region_t = sb("region_t", [P, 2560])
        region_b = sb("region_b", [P, 2048])
        region_v = sb("region_v", [P, 512])
        tmp = sb("tmp", [P, 2, 512])
        ident = sb("ident", [P, P])
        ones = sb("ones", [P, P])
        wmask = sb("wmask", [P, 2, 512])
        gla_mask = sb("gla_mask", [P, 2, P])
        rope = sb("rope", [P, 2, 2, 32])
        rows_a = sb("rows_a", [P, P])
        rows_b = sb("rows_b", [68, P])
        vec_a = sb("vec_a", [P, P])
        vec_b = sb("vec_b", [P, 68])
        cond = sb("cond", [P, 2, KD])
        mod = sb("mod", [P, 2, 48, 2])
        affine = sb("affine", [P, 4, KD, 2])
        sp = sb("sp", [P, 8, 8])
        small = sb("small", [P, 64])
        ssq = sb("ssq", [P, 4, 8])
        rstd = sb("rstd", [P, 4, 8])
        g_qk = sb("g_qk", [P, 2, 64])
        sink = sb("sink", [P, 2, 8])
        g_out = sb("g_out", [P, DV])
        bias_r = sb("bias_r", [P, N_EXPERTS])
        rw = sb("rw", [P, KD, N_EXPERTS])
        qk_ss = sb("qk_ss", [P, 3, 40])
        soft = sb("soft", [P, 2, 5, 4])
        rt = sb("rt", [P, 10, 64])
        rt4 = sb("rt4", [P, 1, 64])
        comb = sb("comb", [P, 4, N_EXPERTS])
        gla_small = sb("gla_small", [P, 2, 8])
        eps_c = sb("eps_c", [P, 1])

        uc = region_u[:, :].rearrange("p (c t) -> p c t", c=4)
        gg = region_g[:, :].rearrange("p (c t) -> p c t", c=4)
        qk = region_q[:, :].rearrange("p (t n) -> p t n", t=4)
        qkT = region_t[:, :].rearrange("p (j t) -> p j t", j=5)
        v_sb = region_v[:, :].rearrange("p (t n) -> p t n", t=4)
        bd = region_b[:, :].rearrange("p (m n) -> p m n", m=16)
        mixT = xn[:, :, :].rearrange("p a b -> p (a b)").rearrange("p (k t) -> p k t", k=8)
        rg_r = region_r[:, :].rearrange("p (u t) -> p u t", u=4)
        nT_flat = nT[:, :, :].rearrange("p k t -> p (k t)")
        rg_i = nT[:, 0:4, :]
        rg_a = nT[:, 4:8, :]
        prob = nT_flat.rearrange("p (b g t) -> p b g t", b=2, g=4)
        probT = region_r[:, :].rearrange("p (s n) -> p s n", s=4)
        gate_row = region_g[:, :].rearrange("p (s n) -> p s n", s=2)
        diag = region_q[:, 0:2048].rearrange("p (s k n) -> p s k n", s=2, k=8)
        v1 = xn
        kT = region_u[:, :].rearrange("p (h t) -> p h t", h=4)
        r_sb = region_g[:, :].rearrange("p (t n) -> p t n", t=2)
        qT = region_q[:, 0:1024].rearrange("p (h t) -> p h t", h=4)
        aT = region_q[0:16, 1024:2048].rearrange("p (d t) -> p d t", d=2)
        gate_up = region_t[0:16, 0:1024].rearrange("p (d n) -> p d n", d=2)
        absz = region_t[:, 1024:2048].rearrange("p (d t) -> p d t", d=2)
        att = region_t[:, 2048:2560].rearrange("p (d t n) -> p d t n", d=2, t=2)
        lmin = nT[:, 0:2, :]
        bcum = nT[:, 2:4, :]
        ebuf = nT[:, 4:6, :]
        kendT = nT[:, 6:8, :]
        kend = region_r[:, 0:1024].rearrange("p (d t n) -> p d t n", d=2, t=4)
        qdec = region_r[:, 1024:1536].rearrange("p (d t) -> p d t", d=2)
        kinc = region_r[:, 1536:2048].rearrange("p (d t) -> p d t", d=2)
        state = region_b[:, 0:1024].rearrange("p (b d n) -> p b d n", b=2, d=2)
        og = nT_flat[:, 0:2048].rearrange("p (t n) -> p t n", t=2)
        oT = nT_flat[:, 2048:4096].rearrange("p (k t) -> p k t", k=8)
        reset = region_b[:, 1024:1536]
        actT = [region_u[:, :].rearrange("p (f t) -> p f t", f=FT),
                region_g[:, :].rearrange("p (f t) -> p f t", f=FT)]
        acc = xn

        s_rows = sem("rows_loaded")
        s_small = sem("small_loaded")
        s_bdl = sem("blocks_loaded")
        s_gup = sem("gate_up_loaded")
        s_h0 = sem("h_loaded")
        slot_full = [sem(f"slot_full{i}") for i in range(RING)]
        s_const = sem("constants_ready")
        s_bd0 = sem("blocks_zeroed")
        pool_step = sem("pool_step")
        act_step = sem("act_step")
        dve_step = sem("dve_step")
        vec_ps = sem("vectors_transposed")
        vec_rd = sem("vectors_ready")
        cond_rd = sem("cond_ready")
        ada_ps = sem("ada_product")
        mod_rd = sem("mod_ready")
        std_rd = [sem(f"std_ready{n}") for n in range(4)]
        rstd_rd = [sem(f"rstd_ready{n}") for n in range(4)]
        xn_rd = [sem(f"xn_ready{n}") for n in range(4)]
        tp_ps = [sem(f"norm_transposed{n}") for n in range(4)]
        nT_act = [sem(f"nT_act{n}") for n in range(4)]
        nT_dve = [sem(f"nT_dve{n}") for n in range(4)]
        h_rd = sem("h_updated")
        proj_ps = sem("proj_product")
        uc_rd = sem("uc_ready")
        gelu_rd = sem("gelu_ready")
        qkv_rd = sem("qkv_ready")
        qkss = sem("qk_squares")
        qkstd = sem("qk_std")
        qkn_rd = sem("qk_ready")
        qkt_ps = sem("qk_transposed")
        qkt_rd = sem("qkT_ready")
        sp_e = sem("softplus_exp")
        sp_x = sem("softplus_arg")
        sp_l = sem("softplus_ln")
        sp_rd = sem("softplus_ready")
        rg_ps = sem("rg_product")
        sg_rd = sem("sigmoid_ready")
        at_rd = sem("exp_tanh_ready")
        va_rd = sem("variance_ready")
        sq_rd = sem("sqrt_ready")
        half_rd = sem("rglru_half_done")
        sc_ps = sem("scores_product")
        sc_rd = sem("scores_ready")
        nm_rd = sem("negmax_ready")
        ex_rd = sem("probs_ready")
        pn_rd = sem("probs_normed")
        pt_ps = sem("probs_transposed")
        pt_rd = sem("probT_ready")
        pv_ps = sem("pv_product")
        pv_rd = sem("att_out_ready")
        dg_rd = sem("diag_ready")
        gr_ps = sem("gate_rows_product")
        gr_rd = sem("gate_rows_ready")
        y_ps = sem("mixer_product")
        y_rd = sem("mixer_added")
        rt_ps = sem("router_product")
        rt_sg = sem("router_scores")
        rt_rd = sem("routing_ready")
        gu_ps = sem("gate_up_product")
        silu_rd = sem("silu_ready")
        actT_rd = sem("actT_ready")
        dn_ps = sem("down_product")
        dn_rd = sem("down_added")
        p1_ps = sem("proj1_product")
        p1_act = sem("proj1_act")
        p1_dve = sem("proj1_dve")
        z_ps = sem("gate_logits")
        z_rd = sem("gate_abs_ready")
        zl_rd = sem("gate_ln_ready")
        bc_rd = sem("decay_sum_ready")
        ee_rd = sem("decay_exp")
        ee_us = sem("decay_exp_used")
        ke_ps = sem("kend_transposed")
        ke_rd = sem("kend_ready")
        qd_rd = sem("qdec_kinc_ready")
        at_ps = sem("intra_product")
        att_rd = sem("intra_masked")
        ds_ps = sem("state_product")
        st_rd = sem("state_ready")
        o_ps = sem("gla_out_product")
        og_std = sem("og_std")
        og_rd = sem("og_ready")
        og_ps = sem("og_transposed")
        oT_rd = sem("oT_ready")
        res_rd = sem("result_ready")
        s_out = sem("result_stored")

        block = stack.enter_context(nc.Block())

        def slot(n):
            return ring[:, n % RING, :]

        def slot_kn(n, k=8):
            return slot(n).rearrange("p (k n) -> p k n", k=k)

        def last_use(n):
            if n < ADA_EARLY:
                return ada_ps, n + 1
            n -= ADA_EARLY
            if n < 4:
                return proj_ps, 4 * n + 4
            n -= 4
            if n < ADA_LATE:
                return ada_ps, ADA_EARLY + n + 1
            n -= ADA_LATE
            if n < 2:
                return y_ps, 8
            n -= 2
            if n < MOE_SLOTS:
                return (gu_ps, FT * (n // 3 + 1)) if n % 3 < 2 else (dn_ps, 8 * (n // 3 + 1))
            n -= MOE_SLOTS
            ada0 = ADA_EARLY + ADA_LATE
            if n < ADA_EARLY:
                return ada_ps, ada0 + n + 1
            n -= ADA_EARLY
            if n < 7:
                return p1_ps, (4, 8, 12, 16, 20, 20, 22)[n]
            n -= 7
            if n < ADA_LATE:
                return ada_ps, ada0 + ADA_EARLY + n + 1
            return y_ps, 12

        def norm_tiles(n):
            return 2 if n == 3 else 4

        @block.sync
        def _(sp_eng):
            def load(n, dst, src):
                if n >= RING:
                    sp_eng.wait_ge(*last_use(n - RING))
                sp_eng.dma_start(dst, src).then_inc(slot_full[n % RING], 16)

            def ada(layer, first, count, n):
                for j in range(count):
                    src = ada_w[layer, :, (first + j) * 512:(first + j + 1) * 512]
                    load(n + j, slot_kn(n + j), src.rearrange("(k p) n -> p k n", p=P))

            def columns(n, w, a, b):
                width = b - a
                dst = slot(n)[:, 0:KD * width].rearrange("p (k n) -> p k n", k=KD)
                load(n, dst, w[0, :, a:b].rearrange("(k p) n -> p k n", p=P))

            def rows(n, w, half):
                load(n, slot_kn(n, 4), w[0, half * 512:(half + 1) * 512, :].rearrange("(k p) n -> p k n", p=P))

            def expert(layer, e, m):
                w = (moe_w_gate, moe_w_up, moe_w_down)[m]
                src = w[layer, bass.ds(e, 1), :, :].rearrange("o (k p) n -> p (o k) n", p=P)
                return ring[:, m, :].rearrange("p (k n) -> p k n", k=8 if m < 2 else 4), src

            def experts(layer, base):
                for m in range(3):
                    load(base + m, *expert(layer, 0, m))
                with sp_eng.Fori(1, N_EXPERTS) as e:
                    for m in range(3):
                        if m < 2:
                            sp_eng.wait_ge(gu_ps, e * FT + layer * N_EXPERTS * FT)
                        else:
                            sp_eng.wait_ge(dn_ps, e * (8, 4)[layer] + layer * N_EXPERTS * 8)
                        sp_eng.dma_start(*expert(layer, e, m)).then_inc(slot_full[m], 16)

            ada(0, 0, ADA_EARLY, 0)
            n = ADA_EARLY
            for a, b in ((0, 512), (512, 1024), (1024, 1536), (1536, 1792)):
                columns(n, ev_w_in, a, b)
                n += 1
            ada(0, ADA_EARLY, ADA_LATE, n)
            n += ADA_LATE
            rows(n, ev_w_out, 0)
            rows(n + 1, ev_w_out, 1)
            experts(0, L0_SLOTS)
            n = L1_BASE
            ada(1, 0, ADA_EARLY, n)
            n += ADA_EARLY
            for a, b in ((0, 512), (512, 1024), (1024, 1536), (1536, 2048), (2048, 2560), (2560, 3072),
                         (3072, 3104)):
                columns(n, od_w_in, a, b)
                n += 1
            ada(1, ADA_EARLY, ADA_LATE, n)
            n += ADA_LATE
            rows(n, od_w_out, 0)
            rows(n + 1, od_w_out, 1)
            experts(1, L1_MOE)
            for t in range(2):
                sp_eng.wait_ge(res_rd, t + 1)
                sp_eng.dma_start(out[0, t * P:(t + 1) * P, :], h[:, t, :]).then_inc(s_out, 16)
            sp_eng.wait_ge(s_out, 32)

        @block.gpsimd
        def _(pool):
            step = Chain(pool, pool_step)
            pool.memset(region_b[:, :], 0.0).then_inc(s_bd0, 1)
            pool.memset(ident[:, :], 0.0).then_inc(pool_step, 1)
            pool.memset(gla_mask[:, :, :], 1.0).then_inc(pool_step, 1)
            pool.memset(wmask[:, :, :], 0.0).then_inc(pool_step, 1)
            step.n = 3
            step.wait()
            pool.memset(ones[:, :], 1.0).then_inc(s_const, 1)
            pool.memset(eps_c[:, :], EPS).then_inc(s_const, 1)
            pool.affine_select(out=ident[:, :], in_=ident[:, :], compare_op=ALU.not_equal, fill=1.0,
                               base=0, pattern=[[-1, P]], channel_multiplier=1).then_inc(s_const, 1)
            pool.affine_select(out=wmask[:, 0, P:2 * P], in_=wmask[:, 0, P:2 * P], compare_op=ALU.is_ge,
                               fill=NEG, base=0, pattern=[[-1, P]], channel_multiplier=1).then_inc(s_const, 1)
            pool.affine_select(out=wmask[:, 1, 0:P], in_=wmask[:, 1, 0:P], compare_op=ALU.is_ge,
                               fill=NEG, base=0, pattern=[[1, P]], channel_multiplier=-1).then_inc(s_const, 1)
            step(pool.affine_select(out=gla_mask[:, 0, :], in_=gla_mask[:, 0, :], compare_op=ALU.is_ge,
                                    fill=0.0, base=0, pattern=[[1, P]], channel_multiplier=-1))
            step(pool.affine_select(out=gla_mask[:, 1, :], in_=gla_mask[:, 1, :], compare_op=ALU.is_ge,
                                    fill=0.0, base=0, pattern=[[-1, P]], channel_multiplier=1))
            pool.memset(gla_mask[0:CHUNK, 0, CHUNK:P], 0.0).then_inc(s_const, 1)
            pool.memset(gla_mask[CHUNK:P, 1, 0:CHUNK], 0.0).then_inc(s_const, 1)
            pool.wait_ge(s_bd0, 1)
            for b2 in range(2):
                for gate, w in enumerate((ev_rg_w, ev_ig_w)):
                    for d in range(2):
                        dst = bd[b2 * 64:(b2 + 1) * 64, gate * 8 + d * 4:gate * 8 + d * 4 + 4, b2 * 64:(b2 + 1) * 64]
                        src = w[0, d].rearrange("(ct b) c e -> b c ct e", b=2)[b2]
                        pool.dma_start(dst, src).then_inc(s_bdl, 16)

        @block.scalar
        def _(act):
            step = Chain(act, act_step)
            ra = [(0, ada_b[0].rearrange("(k p) -> k p", p=P)), (48, ada_b[1].rearrange("(k p) -> k p", p=P)),
                  (96, norm_mix_g.rearrange("l (k p) -> (l k) p", p=P)),
                  (112, norm_ffn_g.rearrange("l (k p) -> (l k) p", p=P))]
            rb = [(0, c[0].rearrange("(k p) -> k p", p=P)), (8, c_ctx.rearrange("(k p) -> k p", p=P)),
                  (16, ev_conv_w[0].rearrange("j (k p) -> (j k) p", p=P)),
                  (32, ev_conv_b[0].rearrange("(k p) -> k p", p=P)),
                  (36, ev_rg_b[0].rearrange("d (k p) -> (d k) p", p=P)),
                  (44, ev_ig_b[0].rearrange("d (k p) -> (d k) p", p=P)),
                  (52, ev_lambda[0].rearrange("d (k p) -> (d k) p", p=P)),
                  (60, od_gate_b[0].rearrange("d (k p) -> (d k) p", p=P))]
            for tile, parts in ((rows_b, rb), (rows_a, ra)):
                for at, src in parts:
                    act.dma_start(tile[at:at + src.shape[0], :], src).then_inc(s_rows, 16)
            for t in range(4):
                src = (x, ctx)[t // 2][0, (t % 2) * P:(t % 2 + 1) * P, :]
                act.dma_start(h[:, t, :], src).then_inc(s_h0, 16)
            for cs, table in enumerate((rope_cos, rope_sin)):
                act.dma_start(rope[:, cs, :, :], table.rearrange("(t p) n -> p t n", p=P)).then_inc(s_small, 16)
            act.dma_start(g_qk[:, 0, :], ev_q_norm_g[0].partition_broadcast(P)).then_inc(s_small, 16)
            act.dma_start(g_qk[:, 1, :], ev_k_norm_g[0].partition_broadcast(P)).then_inc(s_small, 16)
            act.dma_start(sink[:, 0, :], ev_sink[0].partition_broadcast(P)).then_inc(s_small, 16)
            act.dma_start(g_out[:, :], od_out_norm_g[0].partition_broadcast(P)).then_inc(s_small, 16)
            act.dma_start(bias_r[:, :], router_bias.partition_broadcast(P)).then_inc(s_small, 16)
            act.dma_start(rw[:, :, :], router_w.rearrange("(k p) e -> p k e", p=P)).then_inc(s_small, 16)

            act.wait_ge(vec_rd, 1)
            act.activation(cond[:, :, :].rearrange("p s k -> p (s k)"), vec_b[:, 0:16], ACT.Silu).then_inc(cond_rd, 1)

            def norm(n):
                tiles = norm_tiles(n)
                if n == 0:
                    act.wait_ge(s_h0, 64)
                    act.wait_ge(s_const, 7)
                else:
                    act.wait_ge(h_rd, (0, 4, 8, 10)[n])
                for t in range(tiles):
                    step(act.activation(xn[:, t, :], h[:, t, :], ACT.Square, accum_out=ssq[:, n, t:t + 1]))
                act.activation(ssq[:, n, 4:4 + tiles], ssq[:, n, 0:tiles], ACT.Sqrt,
                               scale=1.0 / D, bias=eps_c[:, 0:1]).then_inc(std_rd[n], 1)
                act.wait_ge(rstd_rd[n], 1)
                for t in range(0, tiles, 2):
                    act.activation(xn[:, t, :], h[:, t, :], ACT.Copy, scale=rstd[:, n, t:t + 1]).then_inc(xn_rd[n], 1)
                for k in range(0, KD, 2):
                    act.wait_ge(tp_ps[n], k + 1)
                    if k == 0:
                        act.wait_ge(mod_rd, (1, 2, 3, 4)[n])
                    for s in range(tiles // 2):
                        act.activation(nT[:, k, s * 256:(s + 1) * 256], ps[:, k % 4, s * 256:(s + 1) * 256],
                                       ACT.Identity, scale=affine[:, n, k, s:s + 1],
                                       bias=mod[:, n // 2, (0 if n % 2 == 0 else 24) + k, s:s + 1]).then_inc(nT_act[n], 1)

            norm(0)

            act.wait_ge(sp_x, 1)
            act.activation(sp[:, 1, :], sp[:, 0, :], ACT.Exp, scale=-1.0).then_inc(sp_e, 1)
            act.wait_ge(sp_x, 2)
            act.activation(sp[:, 3, :], sp[:, 2, :], ACT.Ln).then_inc(sp_l, 1)

            for t in range(4):
                act.wait_ge(proj_ps, 5 + t)
                act.activation(gg[:, t, :], ps[:, 4 + t, :], ACT.Gelu_apprx_tanh).then_inc(gelu_rd, 1)
            for t in range(4):
                act.wait_ge(proj_ps, 9 + t)
                act.activation(qk[:, t, 0:512].rearrange("p (g kv d) -> p g kv d", g=4, kv=2),
                               ps[:, t, :].rearrange("p (kv g d) -> p g kv d", kv=2, g=4), ACT.Copy).then_inc(qkv_rd, 1)
            for t in range(4):
                act.wait_ge(proj_ps, 13 + t)
                act.activation(qk[:, t, 512:640], ps[:, 4 + t, 0:128], ACT.Copy).then_inc(qkv_rd, 1)
                act.activation(v_sb[:, t, :], ps[:, 4 + t, 128:256], ACT.Copy).then_inc(qkv_rd, 1)
            act.wait_ge(qkss, 1)
            act.activation(qk_ss[:, 1, :], qk_ss[:, 0, :], ACT.Sqrt, scale=1.0 / 64, bias=eps_c[:, 0:1]).then_inc(qkstd, 1)

            for half in range(2):
                if half == 1:
                    act.wait_ge(half_rd, 1)
                for u in range(4):
                    ct, d = 2 * half + u // 2, u % 2
                    for gate in range(2):
                        act.wait_ge(rg_ps, half * 8 + 2 * u + gate + 1)
                        dst = (rg_r, rg_i)[gate][:, u, :]
                        act.activation(dst, ps[:, 2 * u + gate, :], ACT.Sigmoid,
                                       bias=vec_b[:, 36 + gate * 8 + d * 4 + ct:37 + gate * 8 + d * 4 + ct]).then_inc(sg_rd, 1)
                act.wait_ge(sg_rd, half * 8 + 8)
                act.wait_ge(sp_rd, 2)
                for u in range(4):
                    ct, d = 2 * half + u // 2, u % 2
                    col = d * 4 + ct
                    act.activation(rg_a[:, u, :], rg_r[:, u, :], ACT.Exp, scale=sp[:, 6, col:col + 1]).then_inc(at_rd, 1)
                    act.activation(rg_r[:, u, :], rg_r[:, u, :], ACT.Tanh, scale=sp[:, 7, col:col + 1]).then_inc(at_rd, 1)
                act.wait_ge(va_rd, 4 * half + 4)
                act.activation(region_r[:, :], region_r[:, :], ACT.Sqrt).then_inc(sq_rd, 1)

            for j in range(5):
                act.wait_ge(qkt_ps, j + 1)
                act.activation(qkT[:, j, :], ps[:, j, :], ACT.Copy).then_inc(qkt_rd, 1)

            for u in range(8):
                keys = 512 if u < 4 else 256
                b = u % 2
                act.wait_ge(nm_rd, u + 1)
                for g in range(4):
                    act.activation(prob[:, b, g, 0:keys], prob[:, b, g, 0:keys], ACT.Exp,
                                   bias=soft[:, b, 1, g:g + 1], accum_out=soft[:, b, 3, g:g + 1]).then_inc(ex_rd, 1)
                act.activation(soft[:, b, 2, :], soft[:, b, 2, :], ACT.Exp).then_inc(ex_rd, 1)
                if u > 0:
                    act.wait_ge(pv_ps, u)
                for s in range(keys // P):
                    n = (4 * u if u < 4 else 16 + 2 * (u - 4)) + s
                    act.wait_ge(pt_ps, n + 1)
                    act.activation(probT[:, s, :], ps[:, 4 + n % 3, :], ACT.Copy).then_inc(pt_rd, 1)

            def gate_rows(n, streams):
                for s in range(streams):
                    for half in range(2):
                        act.wait_ge(gr_ps, n + 2 * s + half + 1)
                        act.activation(gate_row[:, s, half * 512:(half + 1) * 512], ps[:, 2 * s + half, :],
                                       ACT.Copy).then_inc(gr_rd, 1)

            gate_rows(0, 2)
            norm(1)

            def router(layer):
                tiles = (4, 2)[layer]
                act.wait_ge(rt_ps, layer + 1)
                act.activation(rt[:, 0, 0:16 * tiles], ps[:, 4, 0:16 * tiles], ACT.Sigmoid).then_inc(rt_sg, 1)

            def experts(layer):
                T = (512, 256)[layer]
                base = layer * N_EXPERTS * FT
                with act.Fori(0, N_EXPERTS // 2) as i:
                    for j in range(2):
                        for f in range(FT):
                            q = j * FT + f
                            n = i * (2 * FT) + (base + q)
                            act.wait_ge(gu_ps, n + 1)
                            if base + q >= 2:
                                act.wait_ge(actT_rd, n - 1 + CREDIT)
                            else:
                                act.wait_ge(actT_rd, i * (2 * FT) + CREDIT)
                            act.activation(tmp[:, f % 2, 0:T], ps[:, f % 2, 0:T], ACT.Silu).then_inc(silu_rd, 1)

            router(0)
            experts(0)
            gate_rows(4, 2)
            norm(2)

            act.dma_start(gate_up, od_gate_up[0].rearrange("d r n -> r d n")).then_inc(s_gup, 16)
            for hd in range(4):
                act.wait_ge(p1_ps, hd + 1)
                act.activation(qT[:, hd, :], ps[:, hd, 0:256], ACT.Copy, scale=DK ** -0.5).then_inc(p1_act, 1)
            for t in range(2):
                for half in range(2):
                    n = 16 + 2 * t + half
                    act.wait_ge(p1_ps, n + 1)
                    act.activation(r_sb[:, t, half * 512:(half + 1) * 512], ps[:, 4 + 2 * t + half, :],
                                   ACT.Silu).then_inc(p1_act, 1)
            for d in range(2):
                act.wait_ge(p1_ps, 21 + d)
                act.activation(aT[:, d, :], ps[0:16, d, :], ACT.Copy).then_inc(p1_act, 1)

            for hd in range(HEADS):
                act.wait_ge(z_rd, 2 * hd + 2)
                step(act.activation(absz[:, :, :], lmin[:, :, :], ACT.Abs))
                step(act.activation(absz[:, :, :], absz[:, :, :], ACT.Exp, scale=-1.0))
                act.activation(absz[:, :, :], absz[:, :, :], ACT.Ln, bias=1.0).then_inc(zl_rd, 1)
                act.wait_ge(bc_rd, 2 * hd + 1)
                act.activation(ebuf[:, :, 0:256], bcum[:, :, 0:256], ACT.Exp, scale=1 / 16.0).then_inc(ee_rd, 1)
                act.activation(ebuf[:, :, 256:512], bcum[:, :, 0:256], ACT.Exp, scale=-1 / 16.0).then_inc(ee_rd, 1)
                act.wait_ge(bc_rd, 2 * hd + 2)
                act.activation(gla_small[:, :, :], gla_small[:, :, :], ACT.Exp, scale=1 / 16.0).then_inc(ee_rd, 1)
                act.activation(absz[:, :, :], lmin[:, :, :], ACT.Exp, scale=1 / 16.0).then_inc(ee_rd, 1)
                for d in range(2):
                    act.wait_ge(ke_ps, 2 * hd + d + 1)
                    act.activation(kend[:, d, :, :].rearrange("p t n -> p (t n)"), ps[:, d, :],
                                   ACT.Copy).then_inc(ke_rd, 1)

            act.wait_ge(o_ps, HEADS)
            for t in range(2):
                for hd in range(4):
                    src = ps[:, 4 + 2 * t + hd // 2, (hd % 2) * DV:(hd % 2 + 1) * DV]
                    step(act.activation(ebuf[:, 0, 0:DV], src, ACT.Square, accum_out=small[:, t * 4 + hd:t * 4 + hd + 1]))
            act.activation(small[:, 8:16], small[:, 0:8], ACT.Sqrt, scale=1.0 / DV, bias=eps_c[:, 0:1]).then_inc(og_std, 1)
            for k in range(4):
                act.wait_ge(og_ps, k + 1)
                act.activation(oT[:, 2 * k:2 * k + 2, :], ps[:, k, :].rearrange("p (a t) -> p a t", a=2),
                               ACT.Copy).then_inc(oT_rd, 1)
            gate_rows(8, 1)
            norm(3)
            router(1)
            experts(1)
            gate_rows(10, 1)

        @block.tensor
        def _(pe):
            def wait_slot(n):
                pe.wait_ge(slot_full[n % RING], 16 * (n // RING + 1))

            pe.wait_ge(s_const, 7)
            pe.wait_ge(s_rows, 16 * 12)
            pe.transpose(ps[:, 0, 0:68], rows_b[:, :], ident[0:68, 0:68])
            pe.transpose(ps[:, 0, 128:256], rows_a[:, :], ident[:, :]).then_inc(vec_ps, 1)

            def ada(layer, part, n, bank):
                first, count = ((0, ADA_EARLY), (ADA_EARLY, ADA_LATE))[part]
                pe.wait_ge(cond_rd, 1)
                for q in range(count):
                    wait_slot(n + q)
                    w = slot_kn(n + q)
                    for j in range(4):
                        at = (q * 4 + j) * 2
                        for k in range(KD):
                            mm = pe.matmul(ps[:, bank, at:at + 2], w[:, k, j * P:(j + 1) * P], cond[:, :, k],
                                           start=(k == 0), stop=(k == KD - 1))
                    mm.then_inc(ada_ps, 1)

            def norm(n):
                tiles = norm_tiles(n)
                pe.wait_ge(xn_rd[n], tiles)
                for k in range(KD):
                    if k >= 4:
                        s2 = tiles // 2
                        if k % 2 == 0:
                            pe.wait_ge(nT_act[n], ((k - 4) // 2 + 1) * s2)
                        else:
                            pe.wait_ge(nT_dve[n], ((k - 4) // 2 + 1) * s2)
                    for t in range(tiles):
                        tp = pe.transpose(ps[:, k % 4, t * P:(t + 1) * P], xn[:, t, k * P:(k + 1) * P], ident[:, :])
                    tp.then_inc(tp_ps[n], 1)
                pe.wait_ge(nT_act[n], 4 * (tiles // 2))
                pe.wait_ge(nT_dve[n], 4 * (tiles // 2))

            ada(0, 0, 0, 7)
            norm(0)

            n = ADA_EARLY
            for grp in range(2):
                wait_slot(n)
                w = slot_kn(n)
                for ct in range(4):
                    for k in range(KD):
                        mm = pe.matmul(ps[:, 4 * grp + ct, :], w[:, k, ct * P:(ct + 1) * P], nT[:, k, :],
                                       start=(k == 0), stop=(k == KD - 1))
                    mm.then_inc(proj_ps, 1)
                n += 1
            wait_slot(n)
            w = slot_kn(n)
            for t in range(4):
                pe.wait_ge(uc_rd, t + 1)
                for k in range(KD):
                    mm = pe.matmul(ps[:, t, :], nT[:, k, t * P:(t + 1) * P], w[:, k, :],
                                   start=(k == 0), stop=(k == KD - 1))
                mm.then_inc(proj_ps, 1)
            n += 1
            wait_slot(n)
            w = slot(n)[:, 0:KD * 256].rearrange("p (k n) -> p k n", k=KD)
            for t in range(4):
                pe.wait_ge(gelu_rd, t + 1)
                for k in range(KD):
                    mm = pe.matmul(ps[:, 4 + t, 0:256], nT[:, k, t * P:(t + 1) * P], w[:, k, :],
                                   start=(k == 0), stop=(k == KD - 1))
                mm.then_inc(proj_ps, 1)
            n += 1

            pe.wait_ge(s_bdl, 16 * 8)
            pe.wait_ge(qkv_rd, 12)
            for half in range(2):
                for u in range(4):
                    ct, d = 2 * half + u // 2, u % 2
                    for gate in range(2):
                        if half:
                            pe.wait_ge(sg_rd, 2 * u + gate + 1)
                        mm = pe.matmul(ps[:, 2 * u + gate, :], bd[:, gate * 8 + d * 4 + ct, :], uc[:, ct, :],
                                       start=True, stop=True)
                        mm.then_inc(rg_ps, 1)
            pe.wait_ge(sg_rd, 16)
            for j in range(5):
                if j == 0:
                    pe.wait_ge(qkn_rd, 1)
                for t in range(4):
                    tp = pe.transpose(ps[:, j, t * P:(t + 1) * P], qk[:, t, j * P:(j + 1) * P], ident[:, :])
                tp.then_inc(qkt_ps, 1)
            ada(0, 1, n, 7)
            n += ADA_LATE

            pe.wait_ge(qkt_rd, 5)
            pe.wait_ge(mod_rd, 2)

            def scores(u):
                i, kv = u // 2, u % 2
                a, b = (0, 512) if u < 4 else (256, 512)
                if u > 0:
                    pe.wait_ge(sc_rd, u)
                rows = slice(kv * 64, kv * 64 + 64)
                for g in range(4):
                    mm = pe.matmul(ps[:, g, 0:b - a], qkT[rows, g, i * P:(i + 1) * P], qkT[rows, 4, a:b],
                                   start=True, stop=True)
                mm.then_inc(sc_ps, 1)

            scores(0)
            for u in range(8):
                if u < 7:
                    scores(u + 1)
                kv = u % 2
                tiles = 4 if u < 4 else 2
                pe.wait_ge(pn_rd, u + 1)
                for s in range(tiles):
                    m = (4 * u if u < 4 else 16 + 2 * (u - 4)) + s
                    if m >= 3:
                        pe.wait_ge(pt_rd, m - 2)
                    for g in range(4):
                        tp = pe.transpose(ps[:, 4 + m % 3, g * P:(g + 1) * P], prob[:, u % 2, g, s * P:(s + 1) * P],
                                          ident[:, :])
                    tp.then_inc(pt_ps, 1)
                if u > 0:
                    pe.wait_ge(pv_rd, 2 * u)
                for s in range(tiles):
                    m = (4 * u if u < 4 else 16 + 2 * (u - 4)) + s
                    pe.wait_ge(pt_rd, m + 1)
                    vt = s if u < 4 else 2 + s
                    mm = pe.matmul(ps[0:64, 7, :], v_sb[:, vt, kv * 64:kv * 64 + 64], probT[:, s, :],
                                   start=(s == 0), stop=(s == tiles - 1))
                mm.then_inc(pv_ps, 1)

            def gate_rows(count, streams):
                pe.wait_ge(dg_rd, count)
                for s in range(streams):
                    for half in range(2):
                        pe.matmul(ps[:, 2 * s + half, :], ones[:, :], diag[:, s, 4 * half:4 * half + 4, :],
                                  start=True, stop=True).then_inc(gr_ps, 1)

            pe.wait_ge(pv_rd, 16)
            pe.wait_ge(pt_rd, 24)
            gate_rows(1, 2)
            wait_slot(n)
            wait_slot(n + 1)
            for t in range(4):
                for half in range(2):
                    m = 2 * t + half
                    if m >= 4:
                        pe.wait_ge(y_rd, m - 3)
                    for k in range(KD):
                        w = slot_kn(n + k // 4, 4)
                        mm = pe.matmul(ps[:, 4 + m % 4, :], mixT[:, k, t * P:(t + 1) * P],
                                       w[:, k % 4, half * 512:(half + 1) * 512],
                                       start=(k == 0), stop=(k == KD - 1))
                    mm.then_inc(y_ps, 1)
            n += 2

            def router(layer):
                tiles = (4, 2)[layer]
                for t in range(tiles):
                    for k in range(KD):
                        mm = pe.matmul(ps[:, 4, t * 16:(t + 1) * 16], nT[:, k, t * P:(t + 1) * P], rw[:, k, :],
                                       start=(k == 0), stop=(k == KD - 1))
                mm.then_inc(rt_ps, 1)
                pe.wait_ge(rt_sg, layer + 1)

            def experts(layer, base):
                T = (512, 256)[layer]
                tiles = T // P
                gu0 = layer * N_EXPERTS * FT
                dn0 = (0, N_EXPERTS * 8)[layer]
                use0 = base // RING
                with pe.Fori(0, N_EXPERTS // 2) as i:
                    for j in range(2):
                        pe.wait_ge(slot_full[0], i * 32 + 16 * (use0 + j + 1))
                        pe.wait_ge(slot_full[1], i * 32 + 16 * (use0 + j + 1))
                        for f in range(FT):
                            q = j * FT + f
                            n = i * (2 * FT) + (gu0 + q)
                            if gu0 + q >= 2:
                                pe.wait_ge(actT_rd, n - 1 + CREDIT)
                            else:
                                pe.wait_ge(actT_rd, i * (2 * FT) + CREDIT)
                            for m in range(2):
                                w = ring[:, m, :].rearrange("p (k n) -> p k n", k=8)
                                for k in range(KD):
                                    mm = pe.matmul(ps[:, 2 * m + f % 2, 0:T], w[:, k, f * P:(f + 1) * P], nT[:, k, 0:T],
                                                   start=(k == 0), stop=(k == KD - 1))
                            mm.then_inc(gu_ps, 1)
                        pe.wait_ge(slot_full[2], i * 32 + 16 * (use0 + j + 1))
                        w = ring[:, 2, :].rearrange("p (k n) -> p k n", k=4)
                        pe.wait_ge(actT_rd, i * (2 * FT) + (gu0 + (j + 1) * FT + CREDIT))
                        for t in range(tiles):
                            for half in range(2):
                                q = j * 2 * tiles + 2 * t + half
                                n = i * (4 * tiles) + (dn0 + q)
                                if dn0 + q >= 4:
                                    pe.wait_ge(dn_rd, n - 3 + CREDIT)
                                else:
                                    pe.wait_ge(dn_rd, i * (4 * tiles) + CREDIT)
                                for f in range(FT):
                                    mm = pe.matmul(ps[:, 4 + q % 4, :], actT[j][:, f, t * P:(t + 1) * P],
                                                   w[:, f, half * 512:(half + 1) * 512],
                                                   start=(f == 0), stop=(f == FT - 1))
                                mm.then_inc(dn_ps, 1)

            pe.wait_ge(gr_rd, 4)
            norm(1)
            router(0)
            experts(0, L0_SLOTS)
            pe.wait_ge(dn_rd, N_EXPERTS * 8 + CREDIT)
            gate_rows(2, 2)
            n = L1_BASE
            ada(1, 0, n, 7)
            n += ADA_EARLY
            pe.wait_ge(gr_rd, 8)
            norm(2)

            wait_slot(n)
            w = slot_kn(n)
            for hd in range(4):
                for k in range(KD):
                    mm = pe.matmul(ps[:, hd, 0:256], w[:, k, hd * P:(hd + 1) * P], nT[:, k, 0:256],
                                   start=(k == 0), stop=(k == KD - 1))
                mm.then_inc(p1_ps, 1)
            n += 1
            wait_slot(n)
            w = slot_kn(n)
            pe.wait_ge(mod_rd, 3)
            for hd in range(4):
                for k in range(KD):
                    mm = pe.matmul(ps[:, 4 + hd, :], w[:, k, hd * P:(hd + 1) * P], nT[:, k, :],
                                   start=(k == 0), stop=(k == KD - 1))
                mm.then_inc(p1_ps, 1)
            n += 1
            for half in range(2):
                wait_slot(n)
                w = slot_kn(n)
                for t in range(4):
                    m = half * 4 + t
                    if half == 0:
                        pe.wait_ge(p1_act, t + 1)
                    else:
                        pe.wait_ge(p1_dve, t + 1)
                    for k in range(KD):
                        mm = pe.matmul(ps[:, m, :], nT[:, k, t * P:(t + 1) * P], w[:, k, :],
                                       start=(k == 0), stop=(k == KD - 1))
                    mm.then_inc(p1_ps, 1)
                n += 1
            wait_slot(n)
            wait_slot(n + 1)
            pe.wait_ge(p1_dve, 12)
            for t in range(2):
                for half in range(2):
                    w = slot_kn(n + half)
                    for k in range(KD):
                        mm = pe.matmul(ps[:, 4 + 2 * t + half, :], nT[:, k, t * P:(t + 1) * P], w[:, k, :],
                                       start=(k == 0), stop=(k == KD - 1))
                    mm.then_inc(p1_ps, 1)
            n += 2
            wait_slot(n)
            w = slot(n)[:, 0:KD * 32].rearrange("p (k n) -> p k n", k=KD)
            for d in range(2):
                for k in range(KD):
                    mm = pe.matmul(ps[0:16, d, :], w[:, k, d * 16:(d + 1) * 16], nT[:, k, :],
                                   start=(k == 0), stop=(k == KD - 1))
                mm.then_inc(p1_ps, 1)
            n += 1
            pe.wait_ge(p1_act, 10)
            ada(1, 1, n, 3)
            n += ADA_LATE

            pe.wait_ge(s_gup, 16)
            for hd in range(HEADS):
                if hd:
                    pe.wait_ge(st_rd, 14 * hd)
                for d in range(2):
                    mm = pe.matmul(ps[:, d, :], gate_up[:, d, hd * P:(hd + 1) * P], aT[:, d, :], start=True, stop=True)
                mm.then_inc(z_ps, 1)
                pe.wait_ge(qd_rd, 2 * hd + 2)
                if hd:
                    pe.wait_ge(att_rd, hd)
                for d in range(2):
                    for t in range(2):
                        mm = pe.matmul(ps[:, 2, (2 * d + t) * P:(2 * d + t + 1) * P], kinc[:, d, t * P:(t + 1) * P],
                                       qdec[:, d, t * P:(t + 1) * P], start=True, stop=True)
                mm.then_inc(at_ps, 1)
                pe.wait_ge(ee_us, hd + 1)
                for d in range(2):
                    for t in range(4):
                        tp = pe.transpose(ps[:, d, t * P:(t + 1) * P], kendT[:, d, t * P:(t + 1) * P], ident[:, :])
                    tp.then_inc(ke_ps, 1)

                def head_out(t):
                    return ps[:, 4 + 2 * t + hd // 2, (hd % 2) * DV:(hd % 2 + 1) * DV]

                pe.wait_ge(att_rd, hd + 1)
                for t in range(2):
                    for d in range(2):
                        pe.matmul(head_out(t), att[:, d, t, :], v1[:, t, hd * DV:(hd + 1) * DV],
                                  start=(d == 0), stop=False, skip_group_check=True)
                pe.wait_ge(ke_rd, 2 * hd + 2)
                for q in range(8):
                    for d in range(2):
                        ch = (4 + q if q < 4 else q - 4) if d == 0 else 7 - q + (0 if q >= 4 else 0)
                        t, lo = ch // 2, (ch % 2) * CHUNK
                        if q:
                            pe.wait_ge(st_rd, 14 * hd + 2 * (q - 1) + d + 1)
                        if q >= 4:
                            mm = pe.matmul(head_out(t)[lo:lo + CHUNK, :], qdec[:, d, ch * CHUNK:(ch + 1) * CHUNK],
                                           state[:, (q - 1) % 2, d, :], start=False, stop=(q >= 6),
                                           skip_group_check=True)
                        if q < 7:
                            pe.matmul(ps[:, d, 0:DV], kend[lo:lo + CHUNK, d, t, :],
                                      v1[lo:lo + CHUNK, t, hd * DV:(hd + 1) * DV],
                                      start=True, stop=True).then_inc(ds_ps, 1)
                mm.then_inc(o_ps, 1)

            pe.wait_ge(og_rd, 2)
            pe.wait_ge(mod_rd, 4)
            for k in range(4):
                for a in range(2):
                    for t in range(2):
                        tp = pe.transpose(ps[:, k, a * 256 + t * P:a * 256 + (t + 1) * P],
                                          og[:, t, (2 * k + a) * P:(2 * k + a + 1) * P], ident[:, :])
                tp.then_inc(og_ps, 1)
            pe.wait_ge(oT_rd, 4)
            gate_rows(3, 1)
            wait_slot(n)
            wait_slot(n + 1)
            for t in range(2):
                for half in range(2):
                    for k in range(KD):
                        w = slot_kn(n + k // 4, 4)
                        mm = pe.matmul(ps[:, 4 + 2 * t + half, :], oT[:, k, t * P:(t + 1) * P],
                                       w[:, k % 4, half * 512:(half + 1) * 512],
                                       start=(k == 0), stop=(k == KD - 1))
                    mm.then_inc(y_ps, 1)
            pe.wait_ge(gr_rd, 10)
            norm(3)
            router(1)
            experts(1, L1_MOE)
            pe.wait_ge(dn_rd, N_EXPERTS * 12 + CREDIT)
            gate_rows(4, 1)

        @block.vector
        def _(dve):
            step = Chain(dve, dve_step)

            dve.wait_ge(vec_ps, 1)
            dve.tensor_copy(vec_b[:, :], ps[:, 0, 0:68]).then_inc(vec_rd, 1)
            dve.tensor_copy(vec_a[:, :], ps[:, 0, 128:256]).then_inc(vec_rd, 1)
            dve.wait_ge(vec_rd, 2)
            def ada(layer, part, bank):
                a, b = ((0, 16), (16, 48))[part]
                dve.wait_ge(ada_ps, (ADA_EARLY + ADA_LATE) * layer + ADA_EARLY + ADA_LATE * part)
                bias = vec_a[:, 48 * layer + a:48 * layer + b].unsqueeze(2).to_broadcast([P, b - a, 2])
                step(dve.tensor_tensor(mod[:, layer, a:b, :], ps[:, bank, 0:2 * (b - a)].rearrange("p (j s) -> p j s", s=2),
                                       bias, ALU.add))
                first = 8 + 24 * part
                gain_at = 96 + 16 * part + 8 * layer
                gain = vec_a[:, gain_at:gain_at + 8].unsqueeze(2).to_broadcast([P, 8, 2])
                dve.scalar_tensor_tensor(affine[:, 2 * layer + part, :, :], mod[:, layer, first:first + 8, :], 1.0,
                                         gain, ALU.add, ALU.mult).then_inc(mod_rd, 1)

            def norm(n):
                tiles = norm_tiles(n)
                dve.wait_ge(std_rd[n], 1)
                dve.reciprocal(rstd[:, n, 0:tiles], ssq[:, n, 4:4 + tiles]).then_inc(rstd_rd[n], 1)
                dve.wait_ge(rstd_rd[n], 1)
                for t in range(1, tiles, 2):
                    dve.tensor_scalar(xn[:, t, :], h[:, t, :], rstd[:, n, t:t + 1], None, ALU.mult).then_inc(xn_rd[n], 1)
                dve.wait_ge(mod_rd, (1, 2, 3, 4)[n])
                for k in range(1, KD, 2):
                    dve.wait_ge(tp_ps[n], k + 1)
                    for s in range(tiles // 2):
                        dve.tensor_scalar(nT[:, k, s * 256:(s + 1) * 256], ps[:, k % 4, s * 256:(s + 1) * 256],
                                          affine[:, n, k, s:s + 1],
                                          mod[:, n // 2, (0 if n % 2 == 0 else 24) + k, s:s + 1],
                                          ALU.mult, ALU.add).then_inc(nT_dve[n], 1)

            ada(0, 0, 7)
            norm(0)

            lam = vec_b[:, 52:60]
            dve.scalar_tensor_tensor(sp[:, 0, :], lam, -1.0, lam, ALU.mult, ALU.max).then_inc(sp_x, 1)
            dve.wait_ge(sp_e, 1)
            dve.tensor_scalar(sp[:, 2, :], sp[:, 1, :], 1.0, None, ALU.add).then_inc(sp_x, 1)
            dve.wait_ge(sp_x, 2)
            step(dve.tensor_scalar(sp[:, 4, :], sp[:, 2, :], 1.0, None, ALU.subtract))
            step(dve.tensor_scalar(sp[:, 5, :], sp[:, 4, :], 0.0, None, ALU.is_equal))
            step(dve.tensor_tensor(sp[:, 4, :], sp[:, 4, :], sp[:, 5, :], ALU.add))
            dve.wait_ge(sp_l, 1)
            step(dve.tensor_tensor(sp[:, 3, :], sp[:, 3, :], sp[:, 5, :], ALU.add))
            step(dve.reciprocal(sp[:, 5, :], sp[:, 4, :]))
            step(dve.tensor_tensor(sp[:, 3, :], sp[:, 3, :], sp[:, 5, :], ALU.mult))
            step(dve.tensor_tensor(sp[:, 3, :], sp[:, 3, :], sp[:, 1, :], ALU.mult))
            step(dve.tensor_scalar(sp[:, 4, :], lam, -1.0, 0.0, ALU.mult, ALU.max))
            step(dve.tensor_tensor(sp[:, 3, :], sp[:, 3, :], sp[:, 4, :], ALU.add))
            dve.tensor_scalar(sp[:, 6, :], sp[:, 3, :], -8.0, None, ALU.mult).then_inc(sp_rd, 1)
            dve.tensor_scalar(sp[:, 7, :], sp[:, 3, :], 8.0, None, ALU.mult).then_inc(sp_rd, 1)

            for ct in range(4):
                dve.wait_ge(proj_ps, ct + 1)
                u2 = ps[:, ct, :].rearrange("p (s t) -> p s t", s=2)
                y2 = uc[:, ct, :].rearrange("p (s t) -> p s t", s=2)

                def tap(j):
                    return vec_b[:, 16 + 4 * j + ct:17 + 4 * j + ct]

                step(dve.tensor_scalar(y2, u2, tap(1), vec_b[:, 32 + ct:33 + ct], ALU.mult, ALU.add))
                step(dve.scalar_tensor_tensor(y2[:, :, 1:256], u2[:, :, 0:255], tap(0), y2[:, :, 1:256], ALU.mult, ALU.add))
                step(dve.scalar_tensor_tensor(y2[:, :, 0:255], u2[:, :, 1:256], tap(2), y2[:, :, 0:255], ALU.mult, ALU.add))
                dve.scalar_tensor_tensor(y2[:, :, 0:254], u2[:, :, 2:256], tap(3), y2[:, :, 0:254],
                                         ALU.mult, ALU.add).then_inc(uc_rd, 1)

            dve.wait_ge(qkv_rd, 12)
            dve.wait_ge(s_small, 16 * 8)
            flat = region_q[:, :]
            qsq = region_t[:, :]
            heads = flat.rearrange("p (n d) -> p n d", d=64)
            step(dve.tensor_tensor(qsq, flat, flat, ALU.mult))
            dve.tensor_reduce(qk_ss[:, 0, :], qsq.rearrange("p (n d) -> p n d", d=64), AX_X, ALU.add).then_inc(qkss, 1)
            dve.wait_ge(qkstd, 1)
            step(dve.reciprocal(qk_ss[:, 2, :], qk_ss[:, 1, :]))
            step(dve.tensor_tensor(heads, heads, qk_ss[:, 2, :].unsqueeze(2).to_broadcast([P, 40, 64]), ALU.mult))
            for w, (a, b) in enumerate(((0, 512), (512, 640))):
                part = qk[:, :, a:b].rearrange("p t (n d) -> p t n d", d=64)
                gain = g_qk[:, w, :].unsqueeze(1).unsqueeze(1).to_broadcast([P, 4, (b - a) // 64, 64])
                step.add(dve.tensor_tensor(part, part, gain, ALU.mult))
            step.wait()
            for t in range(2):
                hv = qk[:, t, :].rearrange("p (n a x f) -> p n a x f", n=10, a=2, x=2)
                x1, x2 = hv[:, :, :, 0, :], hv[:, :, :, 1, :]
                shape = [P, 10, 2, 16]
                cos = rope[:, 0, t, :].rearrange("p (a f) -> p a f", a=2).unsqueeze(1).to_broadcast(shape)
                sin = rope[:, 1, t, :].rearrange("p (a f) -> p a f", a=2).unsqueeze(1).to_broadcast(shape)
                scratch = region_t[:, 0:1280].rearrange("p (w n a f) -> p w n a f", w=4, n=10, a=2)
                step.add(dve.tensor_tensor(scratch[:, 0], x1, cos, ALU.mult))
                step.add(dve.tensor_tensor(scratch[:, 1], x2, sin, ALU.mult))
                step.add(dve.tensor_tensor(scratch[:, 2], x2, cos, ALU.mult))
                step(dve.tensor_tensor(scratch[:, 3], x1, sin, ALU.mult))
                step.add(dve.tensor_tensor(x1, scratch[:, 0], scratch[:, 1], ALU.subtract))
                step(dve.tensor_tensor(x2, scratch[:, 2], scratch[:, 3], ALU.add))
            dve.tensor_scalar(sink[:, 1, :], sink[:, 0, :], -1.0, None, ALU.mult).then_inc(qkn_rd, 1)
            dve.wait_ge(qkn_rd, 1)

            for half in range(2):
                for u in range(4):
                    ct = 2 * half + u // 2
                    dve.wait_ge(at_rd, 8 * half + 2 * u + 2)
                    step.add(dve.tensor_tensor(tmp[:, u % 2, :], rg_a[:, u, :], rg_a[:, u, :], ALU.mult))
                    step(dve.tensor_tensor(rg_i[:, u, :], rg_i[:, u, :], uc[:, ct, :], ALU.mult))
                    dve.scalar_tensor_tensor(rg_r[:, u, :], tmp[:, u % 2, :], 1.0, rg_r[:, u, :],
                                             ALU.add, ALU.mult).then_inc(va_rd, 1)
                dve.wait_ge(sq_rd, half + 1)
                step(dve.tensor_tensor(nT[:, 0:4, :], nT[:, 0:4, :], rg_r[:, :, :], ALU.mult))
                for u in range(4):
                    if u % 2 == 0:
                        a, b = rg_a[:, u, :], rg_i[:, u, :]
                        o = rg_r[:, u, :]
                        step(dve.tensor_tensor_scan(o[:, 256:512], a[:, 256:512], b[:, 256:512], 0.0, ALU.mult, ALU.add))
                        step(dve.tensor_tensor_scan(o[:, 0:256], a[:, 0:256], b[:, 0:256], o[:, 511:512], ALU.mult, ALU.add))
                    else:
                        step(dve.tensor_tensor_scan(rg_r[:, u, ::-1], rg_a[:, u, ::-1], rg_i[:, u, ::-1], 0.0,
                                                    ALU.mult, ALU.add))
                for c2 in range(2):
                    ct = 2 * half + c2
                    dve.wait_ge(gelu_rd, ct + 1)
                    step(dve.tensor_tensor(tmp[:, 0, :], rg_r[:, 2 * c2, :], rg_r[:, 2 * c2 + 1, :], ALU.add))
                    ins = dve.tensor_tensor(mixT[:, ct, :], tmp[:, 0, :], gg[:, ct, :], ALU.mult)
                    if c2 == 0:
                        step(ins)
                    else:
                        ins.then_inc(half_rd, 1)
                        dve.wait_ge(half_rd, half + 1)

            ada(0, 1, 7)

            for u in range(8):
                i, kv = u // 2, u % 2
                keys = 512 if u < 4 else 256
                b = u % 2
                dve.wait_ge(sc_ps, u + 1)
                if u >= 2:
                    dve.wait_ge(pv_ps, u - 1)
                if u < 4:
                    ins = dve.scalar_tensor_tensor(prob[:, b, :, :], ps[:, 0:4, :], ATT_SCALE,
                                                   wmask[:, i, :].unsqueeze(1).to_broadcast([P, 4, 512]), ALU.mult, ALU.add)
                else:
                    ins = dve.tensor_scalar(prob[:, b, :, 0:256], ps[:, 0:4, 0:256], ATT_SCALE, None, ALU.mult)
                ins.then_inc(sc_rd, 1)
                dve.wait_ge(sc_rd, u + 1)
                step(dve.tensor_reduce(soft[:, b, 0, :], prob[:, b, :, 0:keys], AX_X, ALU.max))
                step(dve.scalar_tensor_tensor(soft[:, b, 1, :], soft[:, b, 0, :], -1.0, sink[:, 1, kv * 4:kv * 4 + 4],
                                              ALU.mult, ALU.min))
                dve.tensor_tensor(soft[:, b, 2, :], soft[:, b, 1, :], sink[:, 0, kv * 4:kv * 4 + 4],
                                  ALU.add).then_inc(nm_rd, 1)
                dve.wait_ge(ex_rd, 5 * u + 5)
                step(dve.tensor_tensor(soft[:, b, 3, :], soft[:, b, 3, :], soft[:, b, 2, :], ALU.add))
                step(dve.reciprocal(soft[:, b, 4, :], soft[:, b, 3, :]))
                dve.tensor_tensor(prob[:, b, :, 0:keys], prob[:, b, :, 0:keys],
                                  soft[:, b, 4, :].unsqueeze(2).to_broadcast([P, 4, keys]), ALU.mult).then_inc(pn_rd, 1)
                dve.wait_ge(pv_ps, u + 1)
                for odd in range(2):
                    src = ps[0:64, 7, :].rearrange("p (a o t) -> p a o t", a=2, o=2)[:, :, odd, :]
                    dve.tensor_copy(mixT[64 * odd:64 * odd + 64, 4 + 2 * kv:6 + 2 * kv, i * P:(i + 1) * P],
                                    src).then_inc(pv_rd, 1)

            def diagonals(layer, m, streams):
                for s in range(streams):
                    ins = dve.tensor_tensor(diag[:, s, :, :], ident[:, :].unsqueeze(1).to_broadcast([P, 8, P]),
                                            mod[:, layer, 8 * m:8 * m + 8, s:s + 1].to_broadcast([P, 8, P]), ALU.mult)
                    if s == streams - 1:
                        step(ins)
                    else:
                        step.add(ins)
                dve.tensor_copy(small[0:1, 32:33], ident[0:1, 0:1]).then_inc(dg_rd, 1)

            def residual(layer, products, rows, added):
                tiles = (4, 2)[layer]
                dve.wait_ge(gr_rd, rows)
                for t in range(tiles):
                    for half in range(2):
                        m = 2 * t + half
                        dve.wait_ge(y_ps, products + m + 1)
                        bank = 4 + m % 4
                        cols = slice(half * 512, half * 512 + 512)
                        if m >= 1:
                            step.wait()
                        dve.tensor_tensor(tmp[:, m % 2, :], ps[:, bank, :], gate_row[:, t // 2, cols],
                                          ALU.mult).then_inc(y_rd, 1)
                        dve.wait_ge(y_rd, products + m + 1)
                        ins = dve.tensor_tensor(h[:, t, cols], h[:, t, cols], tmp[:, m % 2, :], ALU.add)
                        if half == 0:
                            step.add(ins)
                        else:
                            ins.then_inc(h_rd, 1)

            diagonals(0, 2, 2)
            residual(0, 0, 4, 0)
            norm(1)

            def router(layer):
                tiles = (4, 2)[layer]
                G = 4 * tiles
                dve.wait_ge(rt_sg, layer + 1)
                score = rt[:, 0, 0:4 * G]
                sel = rt[:, 1, 0:4 * G]
                s3 = score.rearrange("p (t e) -> p t e", t=tiles)
                step(dve.tensor_tensor(sel.rearrange("p (t e) -> p t e", t=tiles), s3,
                                       bias_r[:, :].unsqueeze(1).to_broadcast([P, tiles, 16]), ALU.add))

                def rank(values, n, res):
                    v = values.rearrange("p (n e) -> p n e", e=4)
                    res3 = res.rearrange("p (n e) -> p n e", e=4)
                    step(dve.memset(res, 0.0))
                    a = rt4[:, 0, 0:4 * n].rearrange("p (n e) -> p n e", e=4)
                    for e in range(4):
                        me = v[:, :, e:e + 1].to_broadcast([P, n, 4])
                        if e > 0:
                            step.add(dve.tensor_tensor(a[:, :, 0:e], v[:, :, 0:e], me[:, :, 0:e], ALU.is_ge))
                        if e < 3:
                            step.add(dve.tensor_tensor(a[:, :, e + 1:4], v[:, :, e + 1:4], me[:, :, e + 1:4], ALU.is_gt))
                        step.wait()
                        for o in range(4):
                            if o != e:
                                step(dve.tensor_tensor(res3[:, :, e:e + 1], res3[:, :, e:e + 1], a[:, :, o:o + 1], ALU.add))

                r4 = rt[:, 2, 0:4 * G]
                rank(sel, G, r4)
                top2 = rt[:, 3, 0:4 * G]
                step(dve.tensor_scalar(top2, r4, 2.0, None, ALU.is_lt))
                both = rt[:, 4, 0:4 * G]
                step(dve.tensor_tensor(both, top2, sel, ALU.mult))
                gs = rt[:, 5, 0:G]
                step(dve.tensor_reduce(gs, both.rearrange("p (n e) -> p n e", e=4), AX_X, ALU.add))
                gr = rt[:, 6, 0:G]
                rank(gs, tiles, gr)
                best = rt[:, 7, 0:G]
                step(dve.tensor_scalar(best, gr, 0.0, None, ALU.is_equal))
                step(dve.tensor_tensor(both.rearrange("p (n e) -> p n e", e=4), top2.rearrange("p (n e) -> p n e", e=4),
                                       best.unsqueeze(2).to_broadcast([P, G, 4]), ALU.mult))
                step(dve.tensor_tensor(both, both, score, ALU.mult))
                tot = rt[:, 8, 0:tiles]
                step(dve.tensor_reduce(tot, both.rearrange("p (t e) -> p t e", t=tiles), AX_X, ALU.add))
                step(dve.reciprocal(rt[:, 8, 8:8 + tiles], tot))
                dve.tensor_tensor(comb[:, 0:tiles, :], both.rearrange("p (t e) -> p t e", t=tiles),
                                  rt[:, 8, 8:8 + tiles].unsqueeze(2).to_broadcast([P, tiles, 16]), ALU.mult).then_inc(rt_rd, 1)
                dve.wait_ge(rt_rd, layer + 1)
                step(dve.memset(acc[:, 0:tiles, :], 0.0))
                if layer == 0:
                    dve.memset(small[:, 40:41], 0.0).then_inc(actT_rd, CREDIT)
                    dve.memset(small[:, 41:42], 0.0).then_inc(dn_rd, CREDIT)

            def experts(layer):
                T = (512, 256)[layer]
                tiles = T // P
                gu0 = layer * N_EXPERTS * FT
                dn0 = (0, N_EXPERTS * 8)[layer]
                with dve.Fori(0, N_EXPERTS // 2) as i:
                    for j in range(2):
                        for f in range(FT):
                            q = j * FT + f
                            n = i * (2 * FT) + (gu0 + q)
                            dve.wait_ge(silu_rd, n + 1)
                            dve.tensor_tensor(actT[j][:, f, 0:T], tmp[:, f % 2, 0:T], ps[:, 2 + f % 2, 0:T],
                                              ALU.mult).then_inc(actT_rd, 1)
                        for t in range(tiles):
                            for half in range(2):
                                q = j * 2 * tiles + 2 * t + half
                                n = i * (4 * tiles) + (dn0 + q)
                                dve.wait_ge(dn_ps, n + 1)
                                if dn0 + q >= 2 * tiles:
                                    dve.wait_ge(dn_rd, n - (2 * tiles - 1) + CREDIT)
                                else:
                                    dve.wait_ge(dn_rd, i * (4 * tiles) + CREDIT)
                                dst = acc[:, t, half * 512:(half + 1) * 512]
                                dve.scalar_tensor_tensor(dst, ps[:, 4 + q % 4, :], comb[:, t, bass.ds(i * 2 + j, 1)],
                                                         dst, ALU.mult, ALU.add).then_inc(dn_rd, 1)

            def add_experts(layer, rows):
                tiles = (4, 2)[layer]
                dve.wait_ge(gr_rd, rows)
                dve.wait_ge(dn_rd, N_EXPERTS * (8, 12)[layer] + CREDIT)
                for t in range(tiles):
                    step(dve.tensor_tensor(acc[:, t, :], acc[:, t, :], gate_row[:, t // 2, :], ALU.mult))
                    dve.tensor_tensor(h[:, t, :], h[:, t, :], acc[:, t, :], ALU.add).then_inc((h_rd, res_rd)[layer], 1)

            router(0)
            experts(0)
            diagonals(0, 5, 2)
            add_experts(0, 8)
            ada(1, 0, 7)
            norm(2)

            for hd in range(4):
                dve.wait_ge(p1_ps, 5 + hd)
                dve.tensor_copy(kT[:, hd, :], ps[:, 4 + hd, :]).then_inc(p1_dve, 1)
            for half in range(2):
                for t in range(4):
                    m = half * 4 + t
                    dve.wait_ge(p1_ps, 9 + m)
                    dve.tensor_copy(v1[:, t, half * 512:(half + 1) * 512], ps[:, m, :]).then_inc(p1_dve, 1)
            step(dve.memset(reset, 1.0))
            step(dve.memset(reset.rearrange("p (n t) -> p n t", t=CHUNK)[:, :, 0:1], 0.0))
            ada(1, 1, 3)

            for hd in range(HEADS):
                dve.wait_ge(z_ps, hd + 1)
                for d in range(2):
                    gb = vec_b[:, 60 + 4 * d + hd:61 + 4 * d + hd]
                    dve.tensor_scalar(lmin[:, d, :], ps[:, d, :], gb, None, ALU.add).then_inc(z_rd, 1)
                dve.wait_ge(zl_rd, hd + 1)
                step(dve.scalar_tensor_tensor(lmin[:, :, :], lmin[:, :, :], 0.0, absz[:, :, :], ALU.min, ALU.subtract))
                step.add(dve.tensor_tensor_scan(bcum[:, 0, :], reset, lmin[:, 0, :], 0.0, ALU.mult, ALU.add))
                step(dve.tensor_tensor_scan(bcum[:, 1, ::-1], reset, lmin[:, 1, ::-1], 0.0, ALU.mult, ALU.add))
                b3 = [bcum[:, d, :].rearrange("p (n t) -> p n t", t=CHUNK) for d in range(2)]
                ends = [b3[0][:, :, CHUNK - 1:CHUNK], b3[1][:, :, 0:1]]
                l3 = [lmin[:, d, :].rearrange("p (n t) -> p n t", t=CHUNK) for d in range(2)]
                dve.tensor_copy(gla_small[:, 0, :].unsqueeze(2), ends[0]).then_inc(bc_rd, 1)
                step.add(dve.tensor_copy(gla_small[:, 1, :].unsqueeze(2), ends[1]))
                for d in range(2):
                    ins = dve.tensor_tensor(l3[d], ends[d].to_broadcast([P, 8, CHUNK]), b3[d], ALU.subtract)
                    if d:
                        step.wait()
                        ins.then_inc(bc_rd, 1)
                    else:
                        step.add(ins)
                dve.wait_ge(ee_rd, 4 * hd + 2)
                q2 = qT[:, hd, :].unsqueeze(1).to_broadcast([P, 2, 256])
                k2 = kT[:, hd, 0:256].unsqueeze(1).to_broadcast([P, 2, 256])
                dve.tensor_tensor(qdec[:, :, :], ebuf[:, :, 0:256], q2, ALU.mult).then_inc(qd_rd, 1)
                dve.tensor_tensor(kinc[:, :, :], ebuf[:, :, 256:512], k2, ALU.mult).then_inc(qd_rd, 1)
                dve.wait_ge(ee_rd, 4 * hd + 4)
                dve.tensor_tensor(kendT[:, :, :], absz[:, :, :], kT[:, hd, :].unsqueeze(1).to_broadcast([P, 2, 512]),
                                  ALU.mult).then_inc(ee_us, 1)
                dve.wait_ge(at_ps, hd + 1)
                dve.tensor_tensor(att[:, :, :, :], ps[:, 2, :].rearrange("p (d t n) -> p d t n", d=2, t=2),
                                  gla_mask[:, :, :].unsqueeze(2).to_broadcast([P, 2, 2, P]), ALU.mult).then_inc(att_rd, 1)
                for q in range(7):
                    for d in range(2):
                        ch = (4 + q if q < 4 else q - 4) if d == 0 else 7 - q
                        dve.wait_ge(ds_ps, 14 * hd + 2 * q + d + 1)
                        if q == 0:
                            dve.tensor_copy(state[:, 0, d, :], ps[:, d, 0:DV]).then_inc(st_rd, 1)
                        else:
                            dve.wait_ge(st_rd, 14 * hd + 2 * (q - 1) + d + 1)
                            dve.scalar_tensor_tensor(state[:, q % 2, d, :], state[:, (q - 1) % 2, d, :],
                                                     gla_small[:, d, ch:ch + 1], ps[:, d, 0:DV],
                                                     ALU.mult, ALU.add).then_inc(st_rd, 1)
                dve.wait_ge(o_ps, hd + 1)

            dve.wait_ge(og_std, 1)
            step(dve.reciprocal(small[:, 16:24], small[:, 8:16]))
            for t in range(2):
                for hd in range(4):
                    src = ps[:, 4 + 2 * t + hd // 2, (hd % 2) * DV:(hd % 2 + 1) * DV]
                    step.add(dve.scalar_tensor_tensor(og[:, t, hd * DV:(hd + 1) * DV], src,
                                                      small[:, 16 + t * 4 + hd:17 + t * 4 + hd], g_out[:, :],
                                                      ALU.mult, ALU.mult))
                step.wait()
                dve.tensor_tensor(og[:, t, :], og[:, t, :], r_sb[:, t, :], ALU.mult).then_inc(og_rd, 1)
            dve.wait_ge(og_rd, 2)
            diagonals(1, 2, 1)
            residual(1, 8, 10, 8)
            norm(3)
            router(1)
            experts(1)
            diagonals(1, 5, 1)
            add_experts(1, 12)


_INS = ['x', 'c', 'ctx', 'c_ctx', 'router_w', 'router_bias', 'ada_w', 'ada_b', 'norm_mix_g', 'norm_ffn_g',
        'moe_w_gate', 'moe_w_up', 'moe_w_down', 'ev_w_in', 'ev_w_out', 'ev_conv_w', 'ev_conv_b',
        'ev_rg_w', 'ev_rg_b', 'ev_ig_w', 'ev_ig_b', 'ev_lambda', 'ev_q_norm_g', 'ev_k_norm_g', 'ev_sink',
        'od_w_in', 'od_w_out', 'od_gate_up', 'od_gate_b', 'od_out_norm_g']


def rope_tables(tokens, grid, head_dim):
    import numpy as np
    freqs = head_dim // 4
    inv = np.float32(10000.0) ** (-np.arange(freqs, dtype=np.float32) / np.float32(freqs))
    pos = np.arange(tokens)
    row = (pos // grid).astype(np.float32)[:, None] * inv
    col = (pos % grid).astype(np.float32)[:, None] * inv
    angle = np.concatenate([row, col], axis=1)
    return np.cos(angle).astype(np.float32), np.sin(angle).astype(np.float32)


def kernel(**inputs):
    import numpy as _np
    import concourse.bacc as _bacc
    from concourse import mybir as _mybir
    from concourse.bass_utils import run_bass_kernel_spmd as _run

    nc = _bacc.Bacc("TRN2", target_bir_lowering=False, num_devices=1)
    arrays, args = {}, []
    for name in _INS:
        a = _np.ascontiguousarray(inputs[name])
        arrays[f"in_{name}_dram"] = a
        args.append(nc.dram_tensor(f"in_{name}_dram", a.shape, _mybir.dt.from_np(a.dtype), kind="ExternalInput").ap())
    for name, a in zip(("rope_cos", "rope_sin"), rope_tables(256, 64, 64)):
        arrays[f"in_{name}_dram"] = a
        args.append(nc.dram_tensor(f"in_{name}_dram", a.shape, _mybir.dt.float32, kind="ExternalInput").ap())
    args.append(nc.dram_tensor("out_0_dram", (1, 256, 1024), _mybir.dt.float32, kind="ExternalOutput").ap())
    build(nc, *args)
    r = _run(nc, [arrays], core_ids=[0])
    return r.results[0]["out_0_dram"]
```

```python
from contextlib import ExitStack

import concourse.bass as bass
from concourse import mybir

F32 = mybir.dt.float32
F32R = mybir.dt.float32r
I32 = mybir.dt.int32
U32 = mybir.dt.uint32
ALU = mybir.AluOpType
ACT = mybir.ActivationFunctionType
AX_X = mybir.AxisListType.X

P = 128
D = 1024
MEM0 = 16896
MEM_END = 229344
KD = D // P
EPS = 1e-6
NEG = -1e30
N_EXPERTS = 16
D_EXPERT = 512
FT = D_EXPERT // P
RING = 3
SLOT = 4096
HALF = SLOT // 2
HALVES = 6
SPLITS = 4
CAPACITY = 512
FAR = 16384.0
ATT_SCALE = 64 ** -0.5
CHUNK = 64
DK = 128
DV = 256
HEADS = 4

ADA_EARLY = 4
ADA_LATE = 8
L0_SLOTS = ADA_EARLY + 4 + ADA_LATE + 2
MOE_SLOTS = 3 * N_EXPERTS
L1_SLOTS = ADA_EARLY + 7 + ADA_LATE + 2
L1_BASE = L0_SLOTS + MOE_SLOTS
L1_MOE = L1_BASE + L1_SLOTS


class Chain:

    def __init__(self, eng, sem):
        self.eng, self.sem, self.n = eng, sem, 0

    def __call__(self, ins):
        self.add(ins)
        self.wait()

    def add(self, ins):
        ins.then_inc(self.sem, 1)
        self.n += 1

    def wait(self):
        self.eng.wait_ge(self.sem, self.n)


def build(nc, x, c, ctx, c_ctx, router_w, router_bias, ada_w, ada_b, norm_mix_g, norm_ffn_g,
          moe_w_gate, moe_w_up, moe_w_down, ev_w_in, ev_w_out, ev_conv_w, ev_conv_b,
          ev_rg_w, ev_rg_b, ev_ig_w, ev_ig_b, ev_lambda, ev_q_norm_g, ev_k_norm_g, ev_sink,
          od_w_in, od_w_out, od_gate_up, od_gate_b, od_out_norm_g, rope_cos, rope_sin, out):
    with ExitStack() as stack:
        def sem(name):
            return stack.enter_context(nc.semaphore(name))

        ps = stack.enter_context(nc.psum_tensor("ps", [P, 8, 512], F32))

        def at(name, shape, kib, dtype=F32):
            return nc.alloc_sbuf_tensor_at(name, shape, dtype, offset=MEM0 + int(kib * 1024))

        h = at("h", [P, 4, D], 0)
        nT = at("nT", [P, KD, 512], 16)
        xn = at("xn", [P, 4, D], 32)
        ring = at("ring", [P, RING, SLOT], 64)
        region_r = at("region_r", [P, 2048], 112)
        region_u = at("region_u", [P, 2048], 120)
        region_g = at("region_g", [P, 2048], 128)
        region_q = at("region_q", [P, 2560], 136)
        region_t = at("region_t", [P, 2560], 146)
        region_b = at("region_b", [P, 2048], 156)
        region_v = at("region_v", [P, 512], 164)
        tmp = at("tmp", [P, 2, 512], 166)
        x_hi = at("x_hi", [P, 4, D], 32, F32R)
        x_lo = at("x_lo", [P, 4, D], 48, F32R)
        xg_hi = at("xg_hi", [P, KD, P], 16, F32R)
        xg_lo = at("xg_lo", [P, KD, P], 20, F32R)
        pick = at("pick", [P, 4, P], 24, F32R)
        glu = at("glu", [P, D_EXPERT], 26)
        glu_hi = at("glu_hi", [P, FT, P], 28, F32R)
        glu_lo = at("glu_lo", [P, FT, P], 30, F32R)
        w_hi = at("w_hi", [P, SPLITS, HALF], 112, F32R)
        w_lo = at("w_lo", [P, SPLITS, HALF], 144, F32R)
        y_sb = at("y_sb", [P, D], 176)
        xg_f = at("xg_f", [P, KD, P], 16)
        glu_t = at("glu_t", [P, FT, P], 28)
        y_two = at("y_two", [P, 4, 2, D], 32)

        small_at = [MEM0 + 180 * 1024]

        def sb(name, shape, dtype=F32):
            size = 4
            for n in shape[1:]:
                size *= n
            t = nc.alloc_sbuf_tensor_at(name, shape, dtype, offset=small_at[0])
            small_at[0] += -(-size // 32) * 32
            assert small_at[0] <= MEM_END
            return t

        ident = sb("ident", [P, P])
        ones = sb("ones", [P, P])
        wmask = sb("wmask", [P, 2, P])
        gla_mask = sb("gla_mask", [P, 2, P])
        rope = sb("rope", [P, 2, 2, 32])
        rows_a = sb("rows_a", [P, P])
        rows_b = sb("rows_b", [68, P])
        vec_a = sb("vec_a", [P, P])
        vec_b = sb("vec_b", [P, 68])
        cond = sb("cond", [P, 2, KD])
        mod = sb("mod", [P, 2, 48, 2])
        affine = sb("affine", [P, 4, KD, 2])
        sp = sb("sp", [P, 8, 8])
        small = sb("small", [P, 64])
        ssq = sb("ssq", [P, 4, 8])
        rstd = sb("rstd", [P, 4, 8])
        g_qk = sb("g_qk", [P, 2, 64])
        sink = sb("sink", [P, 2, 8])
        g_out = sb("g_out", [P, DV])
        bias_r = sb("bias_r", [P, N_EXPERTS])
        rw = sb("rw", [P, KD, N_EXPERTS])
        qk_ss = sb("qk_ss", [P, 3, 40])
        soft = sb("soft", [P, 2, 5, 4])
        rt = sb("rt", [P, 10, 64])
        rt4 = sb("rt4", [P, 1, 64])
        comb = sb("comb", [P, 4, N_EXPERTS])
        routed = sb("routed", [P, 4, N_EXPERTS])
        rank_e = sb("rank_e", [P, 4, N_EXPERTS])
        two_w = sb("two_w", [P, 2, 4])
        two_at = sb("two_at", [P, 2, 4])
        two_idx = sb("two_idx", [P, 2, 4], U32)
        count_i = sb("count_i", [P, 1], I32)
        before = sb("before", [P, P])
        slots_i = sb("slots_i", [P, P], I32)
        slots = sb("slots", [P, P])
        ekey_i = sb("ekey_i", [P, N_EXPERTS], I32)
        ekey = sb("ekey", [P, N_EXPERTS])
        gla_small = sb("gla_small", [P, 2, 8])
        eps_c = sb("eps_c", [P, 1])

        uc = region_u[:, :].rearrange("p (c t) -> p c t", c=4)
        gg = region_g[:, :].rearrange("p (c t) -> p c t", c=4)
        qk = region_q[:, :].rearrange("p (t n) -> p t n", t=4)
        qkT = region_t[:, :].rearrange("p (j t) -> p j t", j=5)
        v_sb = region_v[:, :].rearrange("p (t n) -> p t n", t=4)
        bd = region_b[:, :].rearrange("p (m n) -> p m n", m=16)
        mixT = xn[:, :, :].rearrange("p a b -> p (a b)").rearrange("p (k t) -> p k t", k=8)
        rg_r = region_r[:, :].rearrange("p (u t) -> p u t", u=4)
        nT_flat = nT[:, :, :].rearrange("p k t -> p (k t)")
        rg_i = nT[:, 0:4, :]
        rg_a = nT[:, 4:8, :]
        prob = nT_flat.rearrange("p (b g t) -> p b g t", b=2, g=4)
        probT = region_r[:, :].rearrange("p (s n) -> p s n", s=4)
        gate_row = region_g[:, :].rearrange("p (s n) -> p s n", s=2)
        diag = region_q[:, 0:2048].rearrange("p (s k n) -> p s k n", s=2, k=8)
        v1 = xn
        kT = region_u[:, :].rearrange("p (h t) -> p h t", h=4)
        r_sb = region_g[:, :].rearrange("p (t n) -> p t n", t=2)
        qT = region_q[:, 0:1024].rearrange("p (h t) -> p h t", h=4)
        aT = region_q[0:16, 1024:2048].rearrange("p (d t) -> p d t", d=2)
        gate_up = region_t[0:16, 0:1024].rearrange("p (d n) -> p d n", d=2)
        absz = region_t[:, 1024:2048].rearrange("p (d t) -> p d t", d=2)
        att = region_t[:, 2048:2560].rearrange("p (d t n) -> p d t n", d=2, t=2)
        lmin = nT[:, 0:2, :]
        bcum = nT[:, 2:4, :]
        ebuf = nT[:, 4:6, :]
        kendT = nT[:, 6:8, :]
        kend = region_r[:, 0:1024].rearrange("p (d t n) -> p d t n", d=2, t=4)
        qdec = region_r[:, 1024:1536].rearrange("p (d t) -> p d t", d=2)
        kinc = region_r[:, 1536:2048].rearrange("p (d t) -> p d t", d=2)
        state = region_b[:, 0:1024].rearrange("p (b d n) -> p b d n", b=2, d=2)
        og = nT_flat[:, 0:2048].rearrange("p (t n) -> p t n", t=2)
        oT = nT_flat[:, 2048:4096].rearrange("p (k t) -> p k t", k=8)
        reset = region_b[:, 1024:1536]
        y_dram = nc.dram_tensor("expert_rows", (N_EXPERTS * CAPACITY, D), F32, kind="Internal").ap()

        s_rows = sem("rows_loaded")
        s_small = sem("small_loaded")
        s_bdl = sem("blocks_loaded")
        s_gup = sem("gate_up_loaded")
        s_h0 = sem("h_loaded")
        slot_full = [sem(f"slot_full{i}") for i in range(RING)]
        s_const = sem("constants_ready")
        s_bd0 = sem("blocks_zeroed")
        pool_step = sem("pool_step")
        act_step = sem("act_step")
        dve_step = sem("dve_step")
        vec_ps = sem("vectors_transposed")
        vec_rd = sem("vectors_ready")
        cond_rd = sem("cond_ready")
        ada_ps = sem("ada_product")
        mod_rd = sem("mod_ready")
        std_rd = sem("std_ready")
        rstd_rd = sem("rstd_ready")
        xn_rd = sem("xn_ready")
        tp_ps = sem("norm_transposed")
        nT_act = sem("nT_act")
        nT_dve = sem("nT_dve")
        h_rd = sem("h_updated")
        proj_ps = sem("proj_product")
        uc_rd = sem("uc_ready")
        gelu_rd = sem("gelu_ready")
        qkv_rd = sem("qkv_ready")
        qkss = sem("qk_squares")
        qkstd = sem("qk_std")
        qkn_rd = sem("qk_ready")
        qkt_ps = sem("qk_transposed")
        qkt_rd = sem("qkT_ready")
        sp_e = sem("softplus_exp")
        sp_x = sem("softplus_arg")
        sp_l = sem("softplus_ln")
        sp_rd = sem("softplus_ready")
        rg_ps = sem("rg_product")
        sg_rd = sem("sigmoid_ready")
        at_rd = sem("exp_tanh_ready")
        va_rd = sem("variance_ready")
        sq_rd = sem("sqrt_ready")
        half_rd = sem("rglru_half_done")
        sc_ps = sem("scores_product")
        sc_rd = sem("scores_ready")
        nm_rd = sem("negmax_ready")
        ex_rd = sem("probs_ready")
        pn_rd = sem("probs_normed")
        pt_ps = sem("probs_transposed")
        pt_rd = sem("probT_ready")
        pv_ps = sem("pv_product")
        pv_rd = sem("att_out_ready")
        dg_rd = sem("diag_ready")
        gr_ps = sem("gate_rows_product")
        gr_rd = sem("gate_rows_ready")
        y_ps = sem("mixer_product")
        y_rd = sem("mixer_added")
        rt_ps = sem("router_product")
        rt_sg = sem("router_scores")
        rt_rd = sem("routing_ready")
        rank_ps = sem("ranks_product")
        back_ps = sem("rows_transposed_back")
        xhi_rd = sem("x_hi_ready")
        xlo_rd = sem("x_lo_ready")
        whi_rd = sem("w_hi_ready")
        wlo_rd = sem("w_lo_ready")
        w_ps = sem("split_weights_used")
        pick_rd = sem("pick_ready")
        pick_ps = sem("gather_product")
        xg_rd = sem("gathered_ready")
        silu_rd = sem("silu_ready")
        glu_rd = sem("glu_ready")
        gt_ps = sem("glu_transposed")
        ghi_rd = sem("glu_hi_ready")
        glo_rd = sem("glu_lo_ready")
        y_sbrd = sem("expert_rows_ready")
        y_st = sem("expert_rows_stored")
        all_done = sem("experts_done")
        two_ld = sem("expert_rows_loaded")
        two_rd = sem("first_rows_weighted")
        more_rank = [sem(f"more_rank{n}") for n in range(2)]
        more_st = [sem(f"more_stored{n}") for n in range(2)]
        more_ld = [sem(f"more_loaded{n}") for n in range(2)]
        more_dve = [sem(f"more_dve{n}") for n in range(2)]
        more_act = [sem(f"more_act{n}") for n in range(2)]
        more_pe = [sem(f"more_pe{n}") for n in range(2)]
        p1_ps = sem("proj1_product")
        p1_act = sem("proj1_act")
        p1_dve = sem("proj1_dve")
        z_ps = sem("gate_logits")
        z_rd = sem("gate_abs_ready")
        zl_rd = sem("gate_ln_ready")
        bc_rd = sem("decay_sum_ready")
        ee_rd = sem("decay_exp")
        ee_us = sem("decay_exp_used")
        ke_ps = sem("kend_transposed")
        ke_rd = sem("kend_ready")
        qd_rd = sem("qdec_kinc_ready")
        at_ps = sem("intra_product")
        att_rd = sem("intra_masked")
        ds_ps = sem("state_product")
        st_rd = sem("state_ready")
        o_ps = sem("gla_out_product")
        og_std = sem("og_std")
        og_rd = sem("og_ready")
        og_ps = sem("og_transposed")
        oT_rd = sem("oT_ready")
        res_rd = sem("result_ready")
        s_out = sem("result_stored")

        block = stack.enter_context(nc.Block())

        def slot(n):
            return ring[:, n % RING, :]

        def slot_kn(n, k=8):
            return slot(n).rearrange("p (k n) -> p k n", k=k)

        def last_use(n):
            if n < ADA_EARLY:
                return ada_ps, n + 1
            n -= ADA_EARLY
            if n < 4:
                return proj_ps, 4 * n + 4
            n -= 4
            if n < ADA_LATE:
                return ada_ps, ADA_EARLY + n + 1
            n -= ADA_LATE
            if n < 2:
                return y_ps, 8
            n -= 2
            if n < MOE_SLOTS:
                return wlo_rd, 2 * n + 2
            n -= MOE_SLOTS
            ada0 = ADA_EARLY + ADA_LATE
            if n < ADA_EARLY:
                return ada_ps, ada0 + n + 1
            n -= ADA_EARLY
            if n < 7:
                return p1_ps, (4, 8, 12, 16, 20, 20, 22)[n]
            n -= 7
            if n < ADA_LATE:
                return ada_ps, ada0 + ADA_EARLY + n + 1
            return y_ps, 12

        fills = [L0_SLOTS // RING, L1_MOE // RING]

        def norm_tiles(n):
            return 2 if n == 3 else 4

        @block.sync
        def _(sp_eng):
            def load(n, dst, src):
                if n >= RING:
                    sp_eng.wait_ge(*last_use(n - RING))
                sp_eng.dma_start(dst, src).then_inc(slot_full[n % RING], 16)

            def ada(layer, first, count, n):
                for j in range(count):
                    src = ada_w[layer, :, (first + j) * 512:(first + j + 1) * 512]
                    load(n + j, slot_kn(n + j), src.rearrange("(k p) n -> p k n", p=P))

            def columns(n, w, a, b):
                width = b - a
                dst = slot(n)[:, 0:KD * width].rearrange("p (k n) -> p k n", k=KD)
                load(n, dst, w[0, :, a:b].rearrange("(k p) n -> p k n", p=P))

            def rows(n, w, half):
                load(n, slot_kn(n, 4), w[0, half * 512:(half + 1) * 512, :].rearrange("(k p) n -> p k n", p=P))

            def expert(layer, e, m):
                w = (moe_w_gate, moe_w_up, moe_w_down)[m]
                src = w[layer, bass.ds(e, 1), :, :].rearrange("o (k p) n -> p (o k) n", p=P)
                return ring[:, m, :].rearrange("p (k n) -> p k n", k=8 if m < 2 else 4), src

            def experts(layer, base):
                for m in range(3):
                    load(base + m, *expert(layer, 0, m))
                with sp_eng.Fori(1, N_EXPERTS) as e:
                    for m in range(3):
                        sp_eng.wait_ge(wlo_rd, e * HALVES + (2 * m + 2 - HALVES + layer * N_EXPERTS * HALVES))
                        sp_eng.dma_start(*expert(layer, e, m)).then_inc(slot_full[m], 16)
                sp_eng.wait_ge(wlo_rd, (layer + 1) * N_EXPERTS * HALVES)
                sp_eng.wait_ge(rt_rd, 2 * layer + 2)
                most = sp_eng.value_load(count_i[0:1, 0:1], min_val=0, max_val=CAPACITY)
                with sp_eng.If(most > P):
                    sp_eng.sem_inc(more_st[layer], 1)
                    with sp_eng.Fori(1, (4, 2)[layer]) as p:
                        with sp_eng.Fori(0, N_EXPERTS) as e:
                            g = p * N_EXPERTS + e
                            rows_at = y_dram[bass.ds(e * P + p * (N_EXPERTS * P), P), :]
                            sp_eng.wait_ge(more_pe[layer], g * 4 + (1 - 4 * N_EXPERTS))
                            sp_eng.wait_ge(more_st[layer], g * 16 + (1 - 16 * N_EXPERTS))
                            for m in range(3):
                                sp_eng.dma_start(*expert(layer, e, m)).then_inc(more_ld[layer], 16)
                            sp_eng.wait_ge(more_dve[layer], g * 5 + (5 - 5 * N_EXPERTS))
                            sp_eng.dma_start(rows_at, y_sb[:, :]).then_inc(more_st[layer], 16)
                    sp_eng.wait_ge(more_st[layer], 16 * N_EXPERTS * ((4, 2)[layer] - 1) + 1)
                sp_eng.sem_inc(all_done, 1)

            ada(0, 0, ADA_EARLY, 0)
            n = ADA_EARLY
            for a, b in ((0, 512), (512, 1024), (1024, 1536), (1536, 1792)):
                columns(n, ev_w_in, a, b)
                n += 1
            ada(0, ADA_EARLY, ADA_LATE, n)
            n += ADA_LATE
            rows(n, ev_w_out, 0)
            rows(n + 1, ev_w_out, 1)
            experts(0, L0_SLOTS)
            n = L1_BASE
            ada(1, 0, ADA_EARLY, n)
            n += ADA_EARLY
            for a, b in ((0, 512), (512, 1024), (1024, 1536), (1536, 2048), (2048, 2560), (2560, 3072),
                         (3072, 3104)):
                columns(n, od_w_in, a, b)
                n += 1
            ada(1, ADA_EARLY, ADA_LATE, n)
            n += ADA_LATE
            rows(n, od_w_out, 0)
            rows(n + 1, od_w_out, 1)
            experts(1, L1_MOE)
            for t in range(2):
                sp_eng.wait_ge(res_rd, t + 1)
                sp_eng.dma_start(out[0, t * P:(t + 1) * P, :], h[:, t, :]).then_inc(s_out, 16)
            sp_eng.wait_ge(s_out, 32)

        @block.gpsimd
        def _(pool):
            step = Chain(pool, pool_step)
            pool.memset(region_b[:, :], 0.0).then_inc(s_bd0, 1)
            pool.memset(ident[:, :], 0.0).then_inc(pool_step, 1)
            pool.iota(slots_i[:, :], [[1, P]], base=0, channel_multiplier=0).then_inc(pool_step, 1)
            pool.iota(ekey_i[:, :], [[P, N_EXPERTS]], base=0, channel_multiplier=0).then_inc(pool_step, 1)
            pool.memset(before[:, :], 1.0).then_inc(pool_step, 1)
            pool.memset(gla_mask[:, :, :], 1.0).then_inc(pool_step, 1)
            pool.memset(wmask[:, :, :], 0.0).then_inc(pool_step, 1)
            step.n = 6
            step.wait()
            pool.memset(ones[:, :], 1.0).then_inc(s_const, 1)
            pool.memset(eps_c[:, :], EPS).then_inc(s_const, 1)
            pool.tensor_copy(slots[:, :], slots_i[:, :]).then_inc(s_const, 1)
            pool.tensor_copy(ekey[:, :], ekey_i[:, :]).then_inc(s_const, 1)
            pool.affine_select(out=before[:, :], in_=before[:, :], compare_op=ALU.is_gt, fill=0.0,
                               base=0, pattern=[[1, P]], channel_multiplier=-1).then_inc(s_const, 1)
            pool.affine_select(out=ident[:, :], in_=ident[:, :], compare_op=ALU.not_equal, fill=1.0,
                               base=0, pattern=[[-1, P]], channel_multiplier=1).then_inc(s_const, 1)
            pool.affine_select(out=wmask[:, 0, :], in_=wmask[:, 0, :], compare_op=ALU.is_ge,
                               fill=NEG, base=0, pattern=[[-1, P]], channel_multiplier=1).then_inc(s_const, 1)
            pool.affine_select(out=wmask[:, 1, :], in_=wmask[:, 1, :], compare_op=ALU.is_ge,
                               fill=NEG, base=0, pattern=[[1, P]], channel_multiplier=-1).then_inc(s_const, 1)
            step(pool.affine_select(out=gla_mask[:, 0, :], in_=gla_mask[:, 0, :], compare_op=ALU.is_ge,
                                    fill=0.0, base=0, pattern=[[1, P]], channel_multiplier=-1))
            step(pool.affine_select(out=gla_mask[:, 1, :], in_=gla_mask[:, 1, :], compare_op=ALU.is_ge,
                                    fill=0.0, base=0, pattern=[[-1, P]], channel_multiplier=1))
            pool.memset(gla_mask[0:CHUNK, 0, CHUNK:P], 0.0).then_inc(s_const, 1)
            pool.memset(gla_mask[CHUNK:P, 1, 0:CHUNK], 0.0).then_inc(s_const, 1)
            pool.wait_ge(s_bd0, 1)
            for b2 in range(2):
                for gate, w in enumerate((ev_rg_w, ev_ig_w)):
                    for d in range(2):
                        dst = bd[b2 * 64:(b2 + 1) * 64, gate * 8 + d * 4:gate * 8 + d * 4 + 4, b2 * 64:(b2 + 1) * 64]
                        src = w[0, d].rearrange("(ct b) c e -> b c ct e", b=2)[b2]
                        pool.dma_start(dst, src).then_inc(s_bdl, 16)
            for layer in range(2):
                pool.wait_ge(rt_rd, 2 * layer + 2)
                pool.wait_ge(y_st, 16 * N_EXPERTS * (layer + 1))
                pool.wait_ge(all_done, layer + 1)

                def two_rows(written):
                    for t in range((4, 2)[layer]):
                        for two in range(2):
                            pool.indirect_dma_start(y_two[:, t, two, :], None, y_dram[0:written, :],
                                                    bass.IndirectOffsetOnAxis(ap=two_idx[:, two, t:t + 1], axis=0)
                                                    ).then_inc(two_ld, 16)

                most = pool.value_load(count_i[0:1, 0:1], min_val=0, max_val=CAPACITY)
                with pool.If(most > P):
                    two_rows((4, 2)[layer] * N_EXPERTS * P)
                with pool.Else():
                    two_rows(N_EXPERTS * P)

        @block.scalar
        def _(act):
            step = Chain(act, act_step)
            ra = [(0, ada_b[0].rearrange("(k p) -> k p", p=P)), (48, ada_b[1].rearrange("(k p) -> k p", p=P)),
                  (96, norm_mix_g.rearrange("l (k p) -> (l k) p", p=P)),
                  (112, norm_ffn_g.rearrange("l (k p) -> (l k) p", p=P))]
            rb = [(0, c[0].rearrange("(k p) -> k p", p=P)), (8, c_ctx.rearrange("(k p) -> k p", p=P)),
                  (16, ev_conv_w[0].rearrange("j (k p) -> (j k) p", p=P)),
                  (32, ev_conv_b[0].rearrange("(k p) -> k p", p=P)),
                  (36, ev_rg_b[0].rearrange("d (k p) -> (d k) p", p=P)),
                  (44, ev_ig_b[0].rearrange("d (k p) -> (d k) p", p=P)),
                  (52, ev_lambda[0].rearrange("d (k p) -> (d k) p", p=P)),
                  (60, od_gate_b[0].rearrange("d (k p) -> (d k) p", p=P))]
            for tile, parts in ((rows_b, rb), (rows_a, ra)):
                for at, src in parts:
                    act.dma_start(tile[at:at + src.shape[0], :], src).then_inc(s_rows, 16)
            for t in range(4):
                src = (x, ctx)[t // 2][0, (t % 2) * P:(t % 2 + 1) * P, :]
                act.dma_start(h[:, t, :], src).then_inc(s_h0, 16)
            for cs, table in enumerate((rope_cos, rope_sin)):
                act.dma_start(rope[:, cs, :, :], table.rearrange("(t p) n -> p t n", p=P)).then_inc(s_small, 16)
            act.dma_start(g_qk[:, 0, :], ev_q_norm_g[0].partition_broadcast(P)).then_inc(s_small, 16)
            act.dma_start(g_qk[:, 1, :], ev_k_norm_g[0].partition_broadcast(P)).then_inc(s_small, 16)
            act.dma_start(sink[:, 0, :], ev_sink[0].partition_broadcast(P)).then_inc(s_small, 16)
            act.dma_start(g_out[:, :], od_out_norm_g[0].partition_broadcast(P)).then_inc(s_small, 16)
            act.dma_start(bias_r[:, :], router_bias.partition_broadcast(P)).then_inc(s_small, 16)
            act.dma_start(rw[:, :, :], router_w.rearrange("(k p) e -> p k e", p=P)).then_inc(s_small, 16)

            act.wait_ge(vec_rd, 1)
            act.activation(cond[:, :, :].rearrange("p s k -> p (s k)"), vec_b[:, 0:16], ACT.Silu).then_inc(cond_rd, 1)

            def norm(n):
                tiles = norm_tiles(n)
                if n == 0:
                    act.wait_ge(s_h0, 64)
                    act.wait_ge(s_const, 10)
                else:
                    act.wait_ge(h_rd, (0, 4, 8, 10)[n])
                for t in range(tiles):
                    step(act.activation(xn[:, t, :], h[:, t, :], ACT.Square, accum_out=ssq[:, n, t:t + 1]))
                act.activation(ssq[:, n, 4:4 + tiles], ssq[:, n, 0:tiles], ACT.Sqrt,
                               scale=1.0 / D, bias=eps_c[:, 0:1]).then_inc(std_rd, 1)
                act.wait_ge(rstd_rd, n + 1)
                for t in range(0, tiles, 2):
                    act.activation(xn[:, t, :], h[:, t, :], ACT.Copy, scale=rstd[:, n, t:t + 1]).then_inc(xn_rd, 1)
                for k in range(0, KD, 2):
                    act.wait_ge(tp_ps, KD * n + k + 1)
                    if k == 0:
                        act.wait_ge(mod_rd, (1, 2, 3, 4)[n])
                    for s in range(tiles // 2):
                        act.activation(nT[:, k, s * 256:(s + 1) * 256], ps[:, k % 4, s * 256:(s + 1) * 256],
                                       ACT.Identity, scale=affine[:, n, k, s:s + 1],
                                       bias=mod[:, n // 2, (0 if n % 2 == 0 else 24) + k, s:s + 1]).then_inc(nT_act, 1)

            norm(0)

            act.wait_ge(sp_x, 1)
            act.activation(sp[:, 1, :], sp[:, 0, :], ACT.Exp, scale=-1.0).then_inc(sp_e, 1)
            act.wait_ge(sp_x, 2)
            act.activation(sp[:, 3, :], sp[:, 2, :], ACT.Ln).then_inc(sp_l, 1)

            for t in range(4):
                act.wait_ge(proj_ps, 5 + t)
                act.activation(gg[:, t, :], ps[:, 4 + t, :], ACT.Gelu_apprx_tanh).then_inc(gelu_rd, 1)
            for t in range(4):
                act.wait_ge(proj_ps, 9 + t)
                act.activation(qk[:, t, 0:512].rearrange("p (g kv d) -> p g kv d", g=4, kv=2),
                               ps[:, t, :].rearrange("p (kv g d) -> p g kv d", kv=2, g=4), ACT.Copy).then_inc(qkv_rd, 1)
            for t in range(4):
                act.wait_ge(proj_ps, 13 + t)
                act.activation(qk[:, t, 512:640], ps[:, 4 + t, 0:128], ACT.Copy).then_inc(qkv_rd, 1)
                act.activation(v_sb[:, t, :], ps[:, 4 + t, 128:256], ACT.Copy).then_inc(qkv_rd, 1)
            act.wait_ge(qkss, 1)
            act.activation(qk_ss[:, 1, :], qk_ss[:, 0, :], ACT.Sqrt, scale=1.0 / 64, bias=eps_c[:, 0:1]).then_inc(qkstd, 1)

            for half in range(2):
                if half == 1:
                    act.wait_ge(half_rd, 1)
                for u in range(4):
                    ct, d = 2 * half + u // 2, u % 2
                    for gate in range(2):
                        act.wait_ge(rg_ps, half * 8 + 2 * u + gate + 1)
                        dst = (rg_r, rg_i)[gate][:, u, :]
                        act.activation(dst, ps[:, 2 * u + gate, :], ACT.Sigmoid,
                                       bias=vec_b[:, 36 + gate * 8 + d * 4 + ct:37 + gate * 8 + d * 4 + ct]).then_inc(sg_rd, 1)
                act.wait_ge(sg_rd, half * 8 + 8)
                act.wait_ge(sp_rd, 2)
                for u in range(4):
                    ct, d = 2 * half + u // 2, u % 2
                    col = d * 4 + ct
                    act.activation(rg_a[:, u, :], rg_r[:, u, :], ACT.Exp, scale=sp[:, 6, col:col + 1]).then_inc(at_rd, 1)
                    act.activation(rg_r[:, u, :], rg_r[:, u, :], ACT.Tanh, scale=sp[:, 7, col:col + 1]).then_inc(at_rd, 1)
                act.wait_ge(va_rd, 4 * half + 4)
                act.activation(region_r[:, :], region_r[:, :], ACT.Sqrt).then_inc(sq_rd, 1)

            for j in range(5):
                act.wait_ge(qkt_ps, j + 1)
                act.activation(qkT[:, j, :], ps[:, j, :], ACT.Copy).then_inc(qkt_rd, 1)

            for u in range(8):
                keys = 512 if u < 4 else 256
                b = u % 2
                act.wait_ge(nm_rd, u + 1)
                for g in range(4):
                    act.activation(prob[:, b, g, 0:keys], prob[:, b, g, 0:keys], ACT.Exp,
                                   bias=soft[:, b, 1, g:g + 1], accum_out=soft[:, b, 3, g:g + 1]).then_inc(ex_rd, 1)
                act.activation(soft[:, b, 2, :], soft[:, b, 2, :], ACT.Exp).then_inc(ex_rd, 1)
                if u > 0:
                    act.wait_ge(pv_ps, u)
                for s in range(keys // P):
                    n = (4 * u if u < 4 else 16 + 2 * (u - 4)) + s
                    act.wait_ge(pt_ps, n + 1)
                    act.activation(probT[:, s, :], ps[:, 4 + n % 3, :], ACT.Copy).then_inc(pt_rd, 1)

            def gate_rows(n, streams):
                for s in range(streams):
                    for half in range(2):
                        act.wait_ge(gr_ps, n + 2 * s + half + 1)
                        act.activation(gate_row[:, s, half * 512:(half + 1) * 512], ps[:, 2 * s + half, :],
                                       ACT.Copy).then_inc(gr_rd, 1)

            gate_rows(0, 2)
            norm(1)

            def router(layer):
                tiles = (4, 2)[layer]
                act.wait_ge(rt_ps, layer + 1)
                act.activation(rt[:, 0, 0:16 * tiles], ps[:, 4, 0:16 * tiles], ACT.Sigmoid).then_inc(rt_sg, 1)

            def experts(layer):
                tiles = (4, 2)[layer]
                for k in range(KD):
                    act.wait_ge(back_ps, KD * layer + k + 1)
                    act.activation(x_hi[:, 0:tiles, k * P:(k + 1) * P],
                                   ps[:, k % 4, 0:tiles * P].rearrange("p (t n) -> p t n", t=tiles), ACT.Copy).then_inc(xhi_rd, 1)

                def first(e):
                    return e + layer * N_EXPERTS

                def high(e, j, i):
                    m, half = i // 2, i % 2
                    n = first(e) * HALVES + i
                    act.wait_ge(slot_full[m], e * 16 + 16 * (1 + fills[layer]))
                    if not (isinstance(e, int) and first(e) * HALVES + i < SPLITS):
                        act.wait_ge(w_ps, n - (SPLITS - 1))
                    act.activation(w_hi[:, (j * HALVES + i) % SPLITS, :], ring[:, m, half * HALF:(half + 1) * HALF],
                                   ACT.Copy).then_inc(whi_rd, 1)

                def gathered_hi(e):
                    act.wait_ge(pick_ps, first(e) * 2 + 1)
                    act.activation(xg_hi[:, :, :].rearrange("p (a k) n -> p a (k n)", a=2), ps[:, 0:2, :],
                                   ACT.Copy).then_inc(xg_rd, 1)

                def gathered_lo(e):
                    act.wait_ge(pick_ps, first(e) * 2 + 2)
                    act.activation(xg_lo[:, :, :].rearrange("p (a k) n -> p a (k n)", a=2), ps[:, 3:5, :],
                                   ACT.Copy).then_inc(xg_rd, 1)

                def body(e, j, last):
                    high(e, j, 4)
                    high(e, j, 5)
                    if not last:
                        high(e + 1, 1 - j, 0)
                    act.wait_ge(w_ps, first(e) * HALVES + 4)
                    act.activation(glu[:, :], ps[:, 2, :], ACT.Silu).then_inc(silu_rd, 1)
                    if not last:
                        high(e + 1, 1 - j, 1)
                        gathered_hi(e + 1)
                    act.wait_ge(gt_ps, first(e) + 1)
                    act.activation(glu_hi[:, :, :].rearrange("p f n -> p (f n)"), ps[:, 7, :], ACT.Copy).then_inc(ghi_rd, 1)
                    if not last:
                        gathered_lo(e + 1)
                        high(e + 1, 1 - j, 2)
                    act.wait_ge(w_ps, first(e) * HALVES + 6)
                    if not (isinstance(e, int) and first(e) == 0):
                        act.wait_ge(y_st, first(e) * 16)
                    act.activation(y_sb[:, :].rearrange("p (a n) -> p a n", a=2), ps[:, 5:7, :], ACT.Copy).then_inc(y_sbrd, 1)
                    act.wait_ge(y_sbrd, first(e) + 1)
                    act.dma_start(y_dram[bass.ds(e * P, P), :], y_sb[:, :]).then_inc(y_st, 16)
                    if not last:
                        high(e + 1, 1 - j, 3)

                for i in range(SPLITS):
                    high(0, 0, i)
                gathered_hi(0)
                gathered_lo(0)
                body(0, 0, False)
                with act.Fori(0, N_EXPERTS // 2 - 1) as i:
                    body(i * 2 + 1, 1, False)
                    body(i * 2 + 2, 0, False)
                body(N_EXPERTS - 1, 1, True)
                most = act.value_load(count_i[0:1, 0:1], min_val=0, max_val=CAPACITY)
                with act.If(most > P):
                    with act.Fori(0, ((4, 2)[layer] - 1) * N_EXPERTS) as g:
                        act.wait_ge(more_pe[layer], g * 4 + 3)
                        act.activation(glu[:, :], ps[:, 2, :], ACT.Silu).then_inc(more_act[layer], 1)

            def add_experts(layer):
                for t in range((4, 2)[layer]):
                    act.wait_ge(two_ld, 16 * (8, 12)[layer])
                    act.activation(y_two[:, t, 0, :], y_two[:, t, 0, :], ACT.Copy, scale=two_w[:, 0, t:t + 1]).then_inc(two_rd, 1)

            router(0)
            experts(0)
            gate_rows(4, 2)
            add_experts(0)
            norm(2)

            act.dma_start(gate_up, od_gate_up[0].rearrange("d r n -> r d n")).then_inc(s_gup, 16)
            for hd in range(4):
                act.wait_ge(p1_ps, hd + 1)
                act.activation(qT[:, hd, :], ps[:, hd, 0:256], ACT.Copy, scale=DK ** -0.5).then_inc(p1_act, 1)
            for t in range(2):
                for half in range(2):
                    n = 16 + 2 * t + half
                    act.wait_ge(p1_ps, n + 1)
                    act.activation(r_sb[:, t, half * 512:(half + 1) * 512], ps[:, 4 + 2 * t + half, :],
                                   ACT.Silu).then_inc(p1_act, 1)
            for d in range(2):
                act.wait_ge(p1_ps, 21 + d)
                act.activation(aT[:, d, :], ps[0:16, d, :], ACT.Copy).then_inc(p1_act, 1)

            for hd in range(HEADS):
                act.wait_ge(z_rd, 2 * hd + 2)
                step(act.activation(absz[:, :, :], lmin[:, :, :], ACT.Abs))
                step(act.activation(absz[:, :, :], absz[:, :, :], ACT.Exp, scale=-1.0))
                act.activation(absz[:, :, :], absz[:, :, :], ACT.Ln, bias=1.0).then_inc(zl_rd, 1)
                act.wait_ge(bc_rd, 2 * hd + 1)
                act.activation(ebuf[:, :, 0:256], bcum[:, :, 0:256], ACT.Exp, scale=1 / 16.0).then_inc(ee_rd, 1)
                act.activation(ebuf[:, :, 256:512], bcum[:, :, 0:256], ACT.Exp, scale=-1 / 16.0).then_inc(ee_rd, 1)
                act.wait_ge(bc_rd, 2 * hd + 2)
                act.activation(gla_small[:, :, :], gla_small[:, :, :], ACT.Exp, scale=1 / 16.0).then_inc(ee_rd, 1)
                act.activation(absz[:, :, :], lmin[:, :, :], ACT.Exp, scale=1 / 16.0).then_inc(ee_rd, 1)
                for d in range(2):
                    act.wait_ge(ke_ps, 2 * hd + d + 1)
                    act.activation(kend[:, d, :, :].rearrange("p t n -> p (t n)"), ps[:, d, :],
                                   ACT.Copy).then_inc(ke_rd, 1)

            act.wait_ge(o_ps, HEADS)
            for t in range(2):
                for hd in range(4):
                    src = ps[:, 4 + 2 * t + hd // 2, (hd % 2) * DV:(hd % 2 + 1) * DV]
                    step(act.activation(ebuf[:, 0, 0:DV], src, ACT.Square, accum_out=small[:, t * 4 + hd:t * 4 + hd + 1]))
            act.activation(small[:, 8:16], small[:, 0:8], ACT.Sqrt, scale=1.0 / DV, bias=eps_c[:, 0:1]).then_inc(og_std, 1)
            for k in range(4):
                act.wait_ge(og_ps, k + 1)
                act.activation(oT[:, 2 * k:2 * k + 2, :], ps[:, k, :].rearrange("p (a t) -> p a t", a=2),
                               ACT.Copy).then_inc(oT_rd, 1)
            gate_rows(8, 1)
            norm(3)
            router(1)
            experts(1)
            gate_rows(10, 1)
            add_experts(1)

        @block.tensor
        def _(pe):
            def wait_slot(n):
                pe.wait_ge(slot_full[n % RING], 16 * (n // RING + 1))

            pe.wait_ge(s_const, 10)
            pe.wait_ge(s_rows, 16 * 12)
            pe.transpose(ps[:, 0, 0:68], rows_b[:, :], ident[0:68, 0:68])
            pe.transpose(ps[:, 0, 128:256], rows_a[:, :], ident[:, :]).then_inc(vec_ps, 1)

            def ada(layer, part, n, bank):
                first, count = ((0, ADA_EARLY), (ADA_EARLY, ADA_LATE))[part]
                pe.wait_ge(cond_rd, 1)
                for q in range(count):
                    wait_slot(n + q)
                    w = slot_kn(n + q)
                    for j in range(4):
                        at = (q * 4 + j) * 2
                        for k in range(KD):
                            mm = pe.matmul(ps[:, bank, at:at + 2], w[:, k, j * P:(j + 1) * P], cond[:, :, k],
                                           start=(k == 0), stop=(k == KD - 1))
                    mm.then_inc(ada_ps, 1)

            def norm(n):
                tiles = norm_tiles(n)
                pe.wait_ge(xn_rd, 4 * n + tiles)
                for k in range(KD):
                    if k >= 4:
                        s2 = tiles // 2
                        if k % 2 == 0:
                            pe.wait_ge(nT_act, 8 * n + ((k - 4) // 2 + 1) * s2)
                        else:
                            pe.wait_ge(nT_dve, 8 * n + ((k - 4) // 2 + 1) * s2)
                    for t in range(tiles):
                        tp = pe.transpose(ps[:, k % 4, t * P:(t + 1) * P], xn[:, t, k * P:(k + 1) * P], ident[:, :])
                    tp.then_inc(tp_ps, 1)
                pe.wait_ge(nT_act, 8 * n + 4 * (tiles // 2))
                pe.wait_ge(nT_dve, 8 * n + 4 * (tiles // 2))

            ada(0, 0, 0, 7)
            norm(0)

            n = ADA_EARLY
            for grp in range(2):
                wait_slot(n)
                w = slot_kn(n)
                for ct in range(4):
                    for k in range(KD):
                        mm = pe.matmul(ps[:, 4 * grp + ct, :], w[:, k, ct * P:(ct + 1) * P], nT[:, k, :],
                                       start=(k == 0), stop=(k == KD - 1))
                    mm.then_inc(proj_ps, 1)
                n += 1
            wait_slot(n)
            w = slot_kn(n)
            for t in range(4):
                pe.wait_ge(uc_rd, t + 1)
                for k in range(KD):
                    mm = pe.matmul(ps[:, t, :], nT[:, k, t * P:(t + 1) * P], w[:, k, :],
                                   start=(k == 0), stop=(k == KD - 1))
                mm.then_inc(proj_ps, 1)
            n += 1
            wait_slot(n)
            w = slot(n)[:, 0:KD * 256].rearrange("p (k n) -> p k n", k=KD)
            for t in range(4):
                pe.wait_ge(gelu_rd, t + 1)
                for k in range(KD):
                    mm = pe.matmul(ps[:, 4 + t, 0:256], nT[:, k, t * P:(t + 1) * P], w[:, k, :],
                                   start=(k == 0), stop=(k == KD - 1))
                mm.then_inc(proj_ps, 1)
            n += 1

            pe.wait_ge(s_bdl, 16 * 8)
            pe.wait_ge(qkv_rd, 12)
            for half in range(2):
                for u in range(4):
                    ct, d = 2 * half + u // 2, u % 2
                    for gate in range(2):
                        if half:
                            pe.wait_ge(sg_rd, 2 * u + gate + 1)
                        mm = pe.matmul(ps[:, 2 * u + gate, :], bd[:, gate * 8 + d * 4 + ct, :], uc[:, ct, :],
                                       start=True, stop=True)
                        mm.then_inc(rg_ps, 1)
            pe.wait_ge(sg_rd, 16)
            for j in range(5):
                if j == 0:
                    pe.wait_ge(qkn_rd, 1)
                for t in range(4):
                    tp = pe.transpose(ps[:, j, t * P:(t + 1) * P], qk[:, t, j * P:(j + 1) * P], ident[:, :])
                tp.then_inc(qkt_ps, 1)
            ada(0, 1, n, 7)
            n += ADA_LATE

            pe.wait_ge(qkt_rd, 5)
            pe.wait_ge(mod_rd, 2)

            def scores(u):
                i, kv = u // 2, u % 2
                a, b = (0, 512) if u < 4 else (256, 512)
                if u > 0:
                    pe.wait_ge(sc_rd, u)
                rows = slice(kv * 64, kv * 64 + 64)
                for g in range(4):
                    mm = pe.matmul(ps[:, g, 0:b - a], qkT[rows, g, i * P:(i + 1) * P], qkT[rows, 4, a:b],
                                   start=True, stop=True)
                mm.then_inc(sc_ps, 1)

            scores(0)
            for u in range(8):
                if u < 7:
                    scores(u + 1)
                kv = u % 2
                tiles = 4 if u < 4 else 2
                pe.wait_ge(pn_rd, u + 1)
                for s in range(tiles):
                    m = (4 * u if u < 4 else 16 + 2 * (u - 4)) + s
                    if m >= 3:
                        pe.wait_ge(pt_rd, m - 2)
                    for g in range(4):
                        tp = pe.transpose(ps[:, 4 + m % 3, g * P:(g + 1) * P], prob[:, u % 2, g, s * P:(s + 1) * P],
                                          ident[:, :])
                    tp.then_inc(pt_ps, 1)
                if u > 0:
                    pe.wait_ge(pv_rd, 2 * u)
                for s in range(tiles):
                    m = (4 * u if u < 4 else 16 + 2 * (u - 4)) + s
                    pe.wait_ge(pt_rd, m + 1)
                    vt = s if u < 4 else 2 + s
                    mm = pe.matmul(ps[0:64, 7, :], v_sb[:, vt, kv * 64:kv * 64 + 64], probT[:, s, :],
                                   start=(s == 0), stop=(s == tiles - 1))
                mm.then_inc(pv_ps, 1)

            def gate_rows(count, streams):
                pe.wait_ge(dg_rd, count)
                for s in range(streams):
                    for half in range(2):
                        pe.matmul(ps[:, 2 * s + half, :], ones[:, :], diag[:, s, 4 * half:4 * half + 4, :],
                                  start=True, stop=True).then_inc(gr_ps, 1)

            pe.wait_ge(pv_rd, 16)
            pe.wait_ge(pt_rd, 24)
            gate_rows(1, 2)
            wait_slot(n)
            wait_slot(n + 1)
            for t in range(4):
                for half in range(2):
                    m = 2 * t + half
                    if m >= 4:
                        pe.wait_ge(y_rd, m - 3)
                    for k in range(KD):
                        w = slot_kn(n + k // 4, 4)
                        mm = pe.matmul(ps[:, 4 + m % 4, :], mixT[:, k, t * P:(t + 1) * P],
                                       w[:, k % 4, half * 512:(half + 1) * 512],
                                       start=(k == 0), stop=(k == KD - 1))
                    mm.then_inc(y_ps, 1)
            n += 2

            def router(layer):
                tiles = (4, 2)[layer]
                for t in range(tiles):
                    for k in range(KD):
                        mm = pe.matmul(ps[:, 4, t * 16:(t + 1) * 16], nT[:, k, t * P:(t + 1) * P], rw[:, k, :],
                                       start=(k == 0), stop=(k == KD - 1))
                mm.then_inc(rt_ps, 1)
                pe.wait_ge(rt_sg, layer + 1)

            def experts(layer):
                tiles = (4, 2)[layer]
                for k in range(KD):
                    if k >= 4:
                        pe.wait_ge(xlo_rd, KD * layer + k - 3)
                    for t in range(tiles):
                        tp = pe.transpose(ps[:, k % 4, t * P:(t + 1) * P], nT[:, k, t * P:(t + 1) * P], ident[:, :])
                    tp.then_inc(back_ps, 1)
                pe.wait_ge(rt_rd, 2 * layer + 1)
                for t in range(tiles):
                    for b in range(t + 1):
                        pe.matmul(ps[:, 5, t * 16:(t + 1) * 16], ones[:, :] if b < t else before[:, :], routed[:, b, :],
                                  start=(b == 0), stop=(b == t))
                for b in range(tiles):
                    mm = pe.matmul(ps[:, 5, 64:80], ones[:, :], routed[:, b, :], start=(b == 0), stop=(b == tiles - 1))
                mm.then_inc(rank_ps, 1)
                pe.wait_ge(xlo_rd, KD * layer + KD)

                def first(e):
                    return e + layer * N_EXPERTS

                def gather(e, part):
                    src = (x_hi, x_lo)[part]
                    if part == 0:
                        pe.wait_ge(pick_rd, first(e) + 1)
                    for k in range(KD):
                        bank = ((0, 1), (3, 4))[part][k // 4]
                        for t in range(tiles):
                            mm = pe.matmul(ps[:, bank, (k % 4) * P:(k % 4 + 1) * P], src[:, t, k * P:(k + 1) * P],
                                           pick[:, t, :], start=(t == 0), stop=(t == tiles - 1))
                    mm.then_inc(pick_ps, 1)

                def body(e, j, last):
                    n0 = first(e) * HALVES
                    for m in range(2):
                        if m == 0:
                            pe.wait_ge(xg_rd, first(e) * 2 + 2)
                        for half in range(2):
                            i = 2 * m + half
                            pe.wait_ge(wlo_rd, n0 + i + 1)
                            b = (j * HALVES + i) % SPLITS
                            whi = w_hi[:, b, :].rearrange("p (k n) -> p k n", k=4)
                            wlo = w_lo[:, b, :].rearrange("p (k n) -> p k n", k=4)
                            for q in range(4):
                                k = 4 * half + q
                                out_ap = ps[:, 2 + m, :]
                                pe.matmul(out_ap, xg_hi[:, k, :], whi[:, q, :], start=(k == 0), stop=False)
                                pe.matmul(out_ap, xg_hi[:, k, :], wlo[:, q, :], start=False, stop=False)
                                mm = pe.matmul(out_ap, xg_lo[:, k, :], whi[:, q, :], start=False, stop=(k == KD - 1))
                            mm.then_inc(w_ps, 1)
                    if not last:
                        gather(e + 1, 0)
                    pe.wait_ge(glu_rd, first(e) + 1)
                    for f in range(FT):
                        tp = pe.transpose(ps[:, 7, f * P:(f + 1) * P], glu[:, f * P:(f + 1) * P], ident[:, :])
                    tp.then_inc(gt_ps, 1)
                    if not last:
                        gather(e + 1, 1)
                    pe.wait_ge(glo_rd, first(e) + 1)
                    if not (isinstance(e, int) and first(e) == 0):
                        pe.wait_ge(y_sbrd, first(e))
                    for half in range(2):
                        i = 4 + half
                        pe.wait_ge(wlo_rd, n0 + i + 1)
                        b = (j * HALVES + i) % SPLITS
                        whi = w_hi[:, b, :].rearrange("p (k n) -> p k n", k=2)
                        wlo = w_lo[:, b, :].rearrange("p (k n) -> p k n", k=2)
                        for q in range(2):
                            f = 2 * half + q
                            for c in range(2):
                                cols = slice(c * 512, (c + 1) * 512)
                                out_ap = ps[:, 5 + c, :]
                                pe.matmul(out_ap, glu_hi[:, f, :], whi[:, q, cols], start=(f == 0), stop=False)
                                pe.matmul(out_ap, glu_hi[:, f, :], wlo[:, q, cols], start=False, stop=False)
                                mm = pe.matmul(out_ap, glu_lo[:, f, :], whi[:, q, cols], start=False, stop=(f == FT - 1))
                        mm.then_inc(w_ps, 1)

                gather(0, 0)
                gather(0, 1)
                body(0, 0, False)
                with pe.Fori(0, N_EXPERTS // 2 - 1) as i:
                    body(i * 2 + 1, 1, False)
                    body(i * 2 + 2, 0, False)
                body(N_EXPERTS - 1, 1, True)

                most = pe.value_load(count_i[0:1, 0:1], min_val=0, max_val=CAPACITY)
                with pe.If(most > P):
                    pe.wait_ge(y_sbrd, (layer + 1) * N_EXPERTS)
                    pe.sem_inc(more_pe[layer], 1)
                    with pe.Fori(0, ((4, 2)[layer] - 1) * N_EXPERTS) as g:
                        pe.wait_ge(more_dve[layer], g * 5 + 1)
                        for k in range(KD):
                            for part, src in enumerate((x_hi, x_lo)):
                                for t in range(tiles):
                                    mm = pe.matmul(ps[:, k // 4, (k % 4) * P:(k % 4 + 1) * P], src[:, t, k * P:(k + 1) * P],
                                                   pick[:, t, :], start=(part == 0 and t == 0),
                                                   stop=(part == 1 and t == tiles - 1))
                        mm.then_inc(more_pe[layer], 1)
                        pe.wait_ge(more_dve[layer], g * 5 + 2)
                        pe.wait_ge(more_ld[layer], g * 48 + 48)
                        for m in range(2):
                            w = ring[:, m, :].rearrange("p (k n) -> p k n", k=8)
                            for k in range(KD):
                                mm = pe.matmul(ps[:, 2 + m, :], xg_f[:, k, :], w[:, k, :], start=(k == 0), stop=(k == KD - 1))
                        mm.then_inc(more_pe[layer], 1)
                        pe.wait_ge(more_dve[layer], g * 5 + 3)
                        for f in range(FT):
                            tp = pe.transpose(ps[:, 7, f * P:(f + 1) * P], glu[:, f * P:(f + 1) * P], ident[:, :])
                        tp.then_inc(more_pe[layer], 1)
                        pe.wait_ge(more_dve[layer], g * 5 + 4)
                        w = ring[:, 2, :].rearrange("p (k n) -> p k n", k=4)
                        for c in range(2):
                            for f in range(FT):
                                mm = pe.matmul(ps[:, 5 + c, :], glu_t[:, f, :], w[:, f, c * 512:(c + 1) * 512],
                                               start=(f == 0), stop=(f == FT - 1))
                        mm.then_inc(more_pe[layer], 1)

            pe.wait_ge(gr_rd, 4)
            norm(1)
            router(0)
            experts(0)
            pe.wait_ge(xlo_rd, KD)
            gate_rows(2, 2)
            n = L1_BASE
            ada(1, 0, n, 7)
            n += ADA_EARLY
            pe.wait_ge(gr_rd, 8)
            norm(2)

            wait_slot(n)
            w = slot_kn(n)
            for hd in range(4):
                for k in range(KD):
                    mm = pe.matmul(ps[:, hd, 0:256], w[:, k, hd * P:(hd + 1) * P], nT[:, k, 0:256],
                                   start=(k == 0), stop=(k == KD - 1))
                mm.then_inc(p1_ps, 1)
            n += 1
            wait_slot(n)
            w = slot_kn(n)
            pe.wait_ge(mod_rd, 3)
            for hd in range(4):
                for k in range(KD):
                    mm = pe.matmul(ps[:, 4 + hd, :], w[:, k, hd * P:(hd + 1) * P], nT[:, k, :],
                                   start=(k == 0), stop=(k == KD - 1))
                mm.then_inc(p1_ps, 1)
            n += 1
            for half in range(2):
                wait_slot(n)
                w = slot_kn(n)
                for t in range(4):
                    m = half * 4 + t
                    if half == 0:
                        pe.wait_ge(p1_act, t + 1)
                    else:
                        pe.wait_ge(p1_dve, t + 1)
                    for k in range(KD):
                        mm = pe.matmul(ps[:, m, :], nT[:, k, t * P:(t + 1) * P], w[:, k, :],
                                       start=(k == 0), stop=(k == KD - 1))
                    mm.then_inc(p1_ps, 1)
                n += 1
            wait_slot(n)
            wait_slot(n + 1)
            pe.wait_ge(p1_dve, 12)
            for t in range(2):
                for half in range(2):
                    w = slot_kn(n + half)
                    for k in range(KD):
                        mm = pe.matmul(ps[:, 4 + 2 * t + half, :], nT[:, k, t * P:(t + 1) * P], w[:, k, :],
                                       start=(k == 0), stop=(k == KD - 1))
                    mm.then_inc(p1_ps, 1)
            n += 2
            wait_slot(n)
            w = slot(n)[:, 0:KD * 32].rearrange("p (k n) -> p k n", k=KD)
            for d in range(2):
                for k in range(KD):
                    mm = pe.matmul(ps[0:16, d, :], w[:, k, d * 16:(d + 1) * 16], nT[:, k, :],
                                   start=(k == 0), stop=(k == KD - 1))
                mm.then_inc(p1_ps, 1)
            n += 1
            pe.wait_ge(p1_act, 10)
            ada(1, 1, n, 3)
            n += ADA_LATE

            pe.wait_ge(s_gup, 16)
            for hd in range(HEADS):
                if hd:
                    pe.wait_ge(st_rd, 14 * hd)
                for d in range(2):
                    mm = pe.matmul(ps[:, d, :], gate_up[:, d, hd * P:(hd + 1) * P], aT[:, d, :], start=True, stop=True)
                mm.then_inc(z_ps, 1)
                pe.wait_ge(qd_rd, 2 * hd + 2)
                if hd:
                    pe.wait_ge(att_rd, hd)
                for d in range(2):
                    for t in range(2):
                        mm = pe.matmul(ps[:, 2, (2 * d + t) * P:(2 * d + t + 1) * P], kinc[:, d, t * P:(t + 1) * P],
                                       qdec[:, d, t * P:(t + 1) * P], start=True, stop=True)
                mm.then_inc(at_ps, 1)
                pe.wait_ge(ee_us, hd + 1)
                for d in range(2):
                    for t in range(4):
                        tp = pe.transpose(ps[:, d, t * P:(t + 1) * P], kendT[:, d, t * P:(t + 1) * P], ident[:, :])
                    tp.then_inc(ke_ps, 1)

                def head_out(t):
                    return ps[:, 4 + 2 * t + hd // 2, (hd % 2) * DV:(hd % 2 + 1) * DV]

                pe.wait_ge(att_rd, hd + 1)
                for t in range(2):
                    for d in range(2):
                        pe.matmul(head_out(t), att[:, d, t, :], v1[:, t, hd * DV:(hd + 1) * DV],
                                  start=(d == 0), stop=False, skip_group_check=True)
                pe.wait_ge(ke_rd, 2 * hd + 2)
                for q in range(8):
                    for d in range(2):
                        ch = (4 + q if q < 4 else q - 4) if d == 0 else 7 - q + (0 if q >= 4 else 0)
                        t, lo = ch // 2, (ch % 2) * CHUNK
                        if q:
                            pe.wait_ge(st_rd, 14 * hd + 2 * (q - 1) + d + 1)
                        if q >= 4:
                            mm = pe.matmul(head_out(t)[lo:lo + CHUNK, :], qdec[:, d, ch * CHUNK:(ch + 1) * CHUNK],
                                           state[:, (q - 1) % 2, d, :], start=False, stop=(q >= 6),
                                           skip_group_check=True)
                        if q < 7:
                            pe.matmul(ps[:, d, 0:DV], kend[lo:lo + CHUNK, d, t, :],
                                      v1[lo:lo + CHUNK, t, hd * DV:(hd + 1) * DV],
                                      start=True, stop=True).then_inc(ds_ps, 1)
                mm.then_inc(o_ps, 1)

            pe.wait_ge(og_rd, 2)
            pe.wait_ge(mod_rd, 4)
            for k in range(4):
                for a in range(2):
                    for t in range(2):
                        tp = pe.transpose(ps[:, k, a * 256 + t * P:a * 256 + (t + 1) * P],
                                          og[:, t, (2 * k + a) * P:(2 * k + a + 1) * P], ident[:, :])
                tp.then_inc(og_ps, 1)
            pe.wait_ge(oT_rd, 4)
            gate_rows(3, 1)
            wait_slot(n)
            wait_slot(n + 1)
            for t in range(2):
                for half in range(2):
                    for k in range(KD):
                        w = slot_kn(n + k // 4, 4)
                        mm = pe.matmul(ps[:, 4 + 2 * t + half, :], oT[:, k, t * P:(t + 1) * P],
                                       w[:, k % 4, half * 512:(half + 1) * 512],
                                       start=(k == 0), stop=(k == KD - 1))
                    mm.then_inc(y_ps, 1)
            pe.wait_ge(gr_rd, 10)
            norm(3)
            router(1)
            experts(1)
            gate_rows(4, 1)

        @block.vector
        def _(dve):
            step = Chain(dve, dve_step)

            dve.wait_ge(vec_ps, 1)
            dve.tensor_copy(vec_b[:, :], ps[:, 0, 0:68]).then_inc(vec_rd, 1)
            dve.tensor_copy(vec_a[:, :], ps[:, 0, 128:256]).then_inc(vec_rd, 1)
            dve.wait_ge(vec_rd, 2)
            def ada(layer, part, bank):
                a, b = ((0, 16), (16, 48))[part]
                dve.wait_ge(ada_ps, (ADA_EARLY + ADA_LATE) * layer + ADA_EARLY + ADA_LATE * part)
                bias = vec_a[:, 48 * layer + a:48 * layer + b].unsqueeze(2).to_broadcast([P, b - a, 2])
                step(dve.tensor_tensor(mod[:, layer, a:b, :], ps[:, bank, 0:2 * (b - a)].rearrange("p (j s) -> p j s", s=2),
                                       bias, ALU.add))
                first = 8 + 24 * part
                gain_at = 96 + 16 * part + 8 * layer
                gain = vec_a[:, gain_at:gain_at + 8].unsqueeze(2).to_broadcast([P, 8, 2])
                dve.scalar_tensor_tensor(affine[:, 2 * layer + part, :, :], mod[:, layer, first:first + 8, :], 1.0,
                                         gain, ALU.add, ALU.mult).then_inc(mod_rd, 1)

            def norm(n):
                tiles = norm_tiles(n)
                dve.wait_ge(std_rd, n + 1)
                dve.reciprocal(rstd[:, n, 0:tiles], ssq[:, n, 4:4 + tiles]).then_inc(rstd_rd, 1)
                dve.wait_ge(rstd_rd, n + 1)
                for t in range(1, tiles, 2):
                    dve.tensor_scalar(xn[:, t, :], h[:, t, :], rstd[:, n, t:t + 1], None, ALU.mult).then_inc(xn_rd, 1)
                dve.wait_ge(mod_rd, (1, 2, 3, 4)[n])
                for k in range(1, KD, 2):
                    dve.wait_ge(tp_ps, KD * n + k + 1)
                    for s in range(tiles // 2):
                        dve.tensor_scalar(nT[:, k, s * 256:(s + 1) * 256], ps[:, k % 4, s * 256:(s + 1) * 256],
                                          affine[:, n, k, s:s + 1],
                                          mod[:, n // 2, (0 if n % 2 == 0 else 24) + k, s:s + 1],
                                          ALU.mult, ALU.add).then_inc(nT_dve, 1)

            ada(0, 0, 7)
            norm(0)

            lam = vec_b[:, 52:60]
            dve.scalar_tensor_tensor(sp[:, 0, :], lam, -1.0, lam, ALU.mult, ALU.max).then_inc(sp_x, 1)
            dve.wait_ge(sp_e, 1)
            dve.tensor_scalar(sp[:, 2, :], sp[:, 1, :], 1.0, None, ALU.add).then_inc(sp_x, 1)
            dve.wait_ge(sp_x, 2)
            step(dve.tensor_scalar(sp[:, 4, :], sp[:, 2, :], 1.0, None, ALU.subtract))
            step(dve.tensor_scalar(sp[:, 5, :], sp[:, 4, :], 0.0, None, ALU.is_equal))
            step(dve.tensor_tensor(sp[:, 4, :], sp[:, 4, :], sp[:, 5, :], ALU.add))
            dve.wait_ge(sp_l, 1)
            step(dve.tensor_tensor(sp[:, 3, :], sp[:, 3, :], sp[:, 5, :], ALU.add))
            step(dve.reciprocal(sp[:, 5, :], sp[:, 4, :]))
            step(dve.tensor_tensor(sp[:, 3, :], sp[:, 3, :], sp[:, 5, :], ALU.mult))
            step(dve.tensor_tensor(sp[:, 3, :], sp[:, 3, :], sp[:, 1, :], ALU.mult))
            step(dve.tensor_scalar(sp[:, 4, :], lam, -1.0, 0.0, ALU.mult, ALU.max))
            step(dve.tensor_tensor(sp[:, 3, :], sp[:, 3, :], sp[:, 4, :], ALU.add))
            dve.tensor_scalar(sp[:, 6, :], sp[:, 3, :], -8.0, None, ALU.mult).then_inc(sp_rd, 1)
            dve.tensor_scalar(sp[:, 7, :], sp[:, 3, :], 8.0, None, ALU.mult).then_inc(sp_rd, 1)

            for ct in range(4):
                dve.wait_ge(proj_ps, ct + 1)
                u2 = ps[:, ct, :].rearrange("p (s t) -> p s t", s=2)
                y2 = uc[:, ct, :].rearrange("p (s t) -> p s t", s=2)

                def tap(j):
                    return vec_b[:, 16 + 4 * j + ct:17 + 4 * j + ct]

                step(dve.tensor_scalar(y2, u2, tap(1), vec_b[:, 32 + ct:33 + ct], ALU.mult, ALU.add))
                step(dve.scalar_tensor_tensor(y2[:, :, 1:256], u2[:, :, 0:255], tap(0), y2[:, :, 1:256], ALU.mult, ALU.add))
                step(dve.scalar_tensor_tensor(y2[:, :, 0:255], u2[:, :, 1:256], tap(2), y2[:, :, 0:255], ALU.mult, ALU.add))
                dve.scalar_tensor_tensor(y2[:, :, 0:254], u2[:, :, 2:256], tap(3), y2[:, :, 0:254],
                                         ALU.mult, ALU.add).then_inc(uc_rd, 1)

            dve.wait_ge(qkv_rd, 12)
            dve.wait_ge(s_small, 16 * 8)
            flat = region_q[:, :]
            qsq = region_t[:, :]
            heads = flat.rearrange("p (n d) -> p n d", d=64)
            step(dve.tensor_tensor(qsq, flat, flat, ALU.mult))
            dve.tensor_reduce(qk_ss[:, 0, :], qsq.rearrange("p (n d) -> p n d", d=64), AX_X, ALU.add).then_inc(qkss, 1)
            dve.wait_ge(qkstd, 1)
            step(dve.reciprocal(qk_ss[:, 2, :], qk_ss[:, 1, :]))
            step(dve.tensor_tensor(heads, heads, qk_ss[:, 2, :].unsqueeze(2).to_broadcast([P, 40, 64]), ALU.mult))
            for w, (a, b) in enumerate(((0, 512), (512, 640))):
                part = qk[:, :, a:b].rearrange("p t (n d) -> p t n d", d=64)
                gain = g_qk[:, w, :].unsqueeze(1).unsqueeze(1).to_broadcast([P, 4, (b - a) // 64, 64])
                step.add(dve.tensor_tensor(part, part, gain, ALU.mult))
            step.wait()
            for t in range(2):
                hv = qk[:, t, :].rearrange("p (n a x f) -> p n a x f", n=10, a=2, x=2)
                x1, x2 = hv[:, :, :, 0, :], hv[:, :, :, 1, :]
                shape = [P, 10, 2, 16]
                cos = rope[:, 0, t, :].rearrange("p (a f) -> p a f", a=2).unsqueeze(1).to_broadcast(shape)
                sin = rope[:, 1, t, :].rearrange("p (a f) -> p a f", a=2).unsqueeze(1).to_broadcast(shape)
                scratch = region_t[:, 0:1280].rearrange("p (w n a f) -> p w n a f", w=4, n=10, a=2)
                step.add(dve.tensor_tensor(scratch[:, 0], x1, cos, ALU.mult))
                step.add(dve.tensor_tensor(scratch[:, 1], x2, sin, ALU.mult))
                step.add(dve.tensor_tensor(scratch[:, 2], x2, cos, ALU.mult))
                step(dve.tensor_tensor(scratch[:, 3], x1, sin, ALU.mult))
                step.add(dve.tensor_tensor(x1, scratch[:, 0], scratch[:, 1], ALU.subtract))
                step(dve.tensor_tensor(x2, scratch[:, 2], scratch[:, 3], ALU.add))
            dve.tensor_scalar(sink[:, 1, :], sink[:, 0, :], -1.0, None, ALU.mult).then_inc(qkn_rd, 1)
            dve.wait_ge(qkn_rd, 1)

            for half in range(2):
                for u in range(4):
                    ct = 2 * half + u // 2
                    dve.wait_ge(at_rd, 8 * half + 2 * u + 2)
                    step.add(dve.tensor_tensor(tmp[:, u % 2, :], rg_a[:, u, :], rg_a[:, u, :], ALU.mult))
                    step(dve.tensor_tensor(rg_i[:, u, :], rg_i[:, u, :], uc[:, ct, :], ALU.mult))
                    dve.scalar_tensor_tensor(rg_r[:, u, :], tmp[:, u % 2, :], 1.0, rg_r[:, u, :],
                                             ALU.add, ALU.mult).then_inc(va_rd, 1)
                dve.wait_ge(sq_rd, half + 1)
                step(dve.tensor_tensor(nT[:, 0:4, :], nT[:, 0:4, :], rg_r[:, :, :], ALU.mult))
                for u in range(4):
                    if u % 2 == 0:
                        a, b = rg_a[:, u, :], rg_i[:, u, :]
                        o = rg_r[:, u, :]
                        step(dve.tensor_tensor_scan(o[:, 256:512], a[:, 256:512], b[:, 256:512], 0.0, ALU.mult, ALU.add))
                        step(dve.tensor_tensor_scan(o[:, 0:256], a[:, 0:256], b[:, 0:256], o[:, 511:512], ALU.mult, ALU.add))
                    else:
                        step(dve.tensor_tensor_scan(rg_r[:, u, ::-1], rg_a[:, u, ::-1], rg_i[:, u, ::-1], 0.0,
                                                    ALU.mult, ALU.add))
                for c2 in range(2):
                    ct = 2 * half + c2
                    dve.wait_ge(gelu_rd, ct + 1)
                    step(dve.tensor_tensor(tmp[:, 0, :], rg_r[:, 2 * c2, :], rg_r[:, 2 * c2 + 1, :], ALU.add))
                    ins = dve.tensor_tensor(mixT[:, ct, :], tmp[:, 0, :], gg[:, ct, :], ALU.mult)
                    if c2 == 0:
                        step(ins)
                    else:
                        ins.then_inc(half_rd, 1)
                        dve.wait_ge(half_rd, half + 1)

            ada(0, 1, 7)

            for u in range(8):
                i, kv = u // 2, u % 2
                keys = 512 if u < 4 else 256
                b = u % 2
                dve.wait_ge(sc_ps, u + 1)
                if u >= 2:
                    dve.wait_ge(pv_ps, u - 1)
                if u < 4:
                    step(dve.tensor_scalar(prob[:, b, :, :], ps[:, 0:4, :], ATT_SCALE, None, ALU.mult))
                    far = prob[:, b, :, (1 - i) * P:(2 - i) * P]
                    ins = dve.tensor_tensor(far, far, wmask[:, i, :].unsqueeze(1).to_broadcast([P, 4, P]), ALU.add)
                else:
                    ins = dve.tensor_scalar(prob[:, b, :, 0:256], ps[:, 0:4, 0:256], ATT_SCALE, None, ALU.mult)
                ins.then_inc(sc_rd, 1)
                dve.wait_ge(sc_rd, u + 1)
                step(dve.tensor_reduce(soft[:, b, 0, :], prob[:, b, :, 0:keys], AX_X, ALU.max))
                step(dve.scalar_tensor_tensor(soft[:, b, 1, :], soft[:, b, 0, :], -1.0, sink[:, 1, kv * 4:kv * 4 + 4],
                                              ALU.mult, ALU.min))
                dve.tensor_tensor(soft[:, b, 2, :], soft[:, b, 1, :], sink[:, 0, kv * 4:kv * 4 + 4],
                                  ALU.add).then_inc(nm_rd, 1)
                dve.wait_ge(ex_rd, 5 * u + 5)
                step(dve.tensor_tensor(soft[:, b, 3, :], soft[:, b, 3, :], soft[:, b, 2, :], ALU.add))
                step(dve.reciprocal(soft[:, b, 4, :], soft[:, b, 3, :]))
                dve.tensor_tensor(prob[:, b, :, 0:keys], prob[:, b, :, 0:keys],
                                  soft[:, b, 4, :].unsqueeze(2).to_broadcast([P, 4, keys]), ALU.mult).then_inc(pn_rd, 1)
                dve.wait_ge(pv_ps, u + 1)
                for odd in range(2):
                    src = ps[0:64, 7, :].rearrange("p (a o t) -> p a o t", a=2, o=2)[:, :, odd, :]
                    dve.tensor_copy(mixT[64 * odd:64 * odd + 64, 4 + 2 * kv:6 + 2 * kv, i * P:(i + 1) * P],
                                    src).then_inc(pv_rd, 1)

            def diagonals(layer, m, streams):
                for s in range(streams):
                    ins = dve.tensor_tensor(diag[:, s, :, :], ident[:, :].unsqueeze(1).to_broadcast([P, 8, P]),
                                            mod[:, layer, 8 * m:8 * m + 8, s:s + 1].to_broadcast([P, 8, P]), ALU.mult)
                    if s == streams - 1:
                        step(ins)
                    else:
                        step.add(ins)
                dve.tensor_copy(small[0:1, 32:33], ident[0:1, 0:1]).then_inc(dg_rd, 1)

            def residual(layer, products, rows, added):
                tiles = (4, 2)[layer]
                dve.wait_ge(gr_rd, rows)
                for t in range(tiles):
                    for half in range(2):
                        m = 2 * t + half
                        dve.wait_ge(y_ps, products + m + 1)
                        bank = 4 + m % 4
                        cols = slice(half * 512, half * 512 + 512)
                        if m >= 1:
                            step.wait()
                        dve.tensor_tensor(tmp[:, m % 2, :], ps[:, bank, :], gate_row[:, t // 2, cols],
                                          ALU.mult).then_inc(y_rd, 1)
                        dve.wait_ge(y_rd, products + m + 1)
                        ins = dve.tensor_tensor(h[:, t, cols], h[:, t, cols], tmp[:, m % 2, :], ALU.add)
                        if half == 0:
                            step.add(ins)
                        else:
                            ins.then_inc(h_rd, 1)

            diagonals(0, 2, 2)
            residual(0, 0, 4, 0)
            norm(1)

            def router(layer):
                tiles = (4, 2)[layer]
                G = 4 * tiles
                dve.wait_ge(rt_sg, layer + 1)
                score = rt[:, 0, 0:4 * G]
                sel = rt[:, 1, 0:4 * G]
                s3 = score.rearrange("p (t e) -> p t e", t=tiles)
                step(dve.tensor_tensor(sel.rearrange("p (t e) -> p t e", t=tiles), s3,
                                       bias_r[:, :].unsqueeze(1).to_broadcast([P, tiles, 16]), ALU.add))

                def rank(values, n, res):
                    v = values.rearrange("p (n e) -> p n e", e=4)
                    res3 = res.rearrange("p (n e) -> p n e", e=4)
                    step(dve.memset(res, 0.0))
                    a = rt4[:, 0, 0:4 * n].rearrange("p (n e) -> p n e", e=4)
                    for e in range(4):
                        me = v[:, :, e:e + 1].to_broadcast([P, n, 4])
                        if e > 0:
                            step.add(dve.tensor_tensor(a[:, :, 0:e], v[:, :, 0:e], me[:, :, 0:e], ALU.is_ge))
                        if e < 3:
                            step.add(dve.tensor_tensor(a[:, :, e + 1:4], v[:, :, e + 1:4], me[:, :, e + 1:4], ALU.is_gt))
                        step.wait()
                        for o in range(4):
                            if o != e:
                                step(dve.tensor_tensor(res3[:, :, e:e + 1], res3[:, :, e:e + 1], a[:, :, o:o + 1], ALU.add))

                r4 = rt[:, 2, 0:4 * G]
                rank(sel, G, r4)
                top2 = rt[:, 3, 0:4 * G]
                step(dve.tensor_scalar(top2, r4, 2.0, None, ALU.is_lt))
                both = rt[:, 4, 0:4 * G]
                step(dve.tensor_tensor(both, top2, sel, ALU.mult))
                gs = rt[:, 5, 0:G]
                step(dve.tensor_reduce(gs, both.rearrange("p (n e) -> p n e", e=4), AX_X, ALU.add))
                gr = rt[:, 6, 0:G]
                rank(gs, tiles, gr)
                best = rt[:, 7, 0:G]
                step(dve.tensor_scalar(best, gr, 0.0, None, ALU.is_equal))
                mine = routed[:, 0:tiles, :].rearrange("p t e -> p (t e)")
                dve.tensor_tensor(mine.rearrange("p (n e) -> p n e", e=4), top2.rearrange("p (n e) -> p n e", e=4),
                                  best.unsqueeze(2).to_broadcast([P, G, 4]), ALU.mult).then_inc(rt_rd, 1)
                dve.wait_ge(rt_rd, 2 * layer + 1)
                step(dve.tensor_tensor(both, mine, score, ALU.mult))
                tot = rt[:, 8, 0:tiles]
                step(dve.tensor_reduce(tot, both.rearrange("p (t e) -> p t e", t=tiles), AX_X, ALU.add))
                step(dve.reciprocal(rt[:, 8, 8:8 + tiles], tot))
                step(dve.tensor_tensor(comb[:, 0:tiles, :], both.rearrange("p (t e) -> p t e", t=tiles),
                                       rt[:, 8, 8:8 + tiles].unsqueeze(2).to_broadcast([P, tiles, 16]), ALU.mult))

                for k in range(KD):
                    dve.wait_ge(xhi_rd, KD * layer + k + 1)
                    cols = slice(k * P, (k + 1) * P)
                    dve.tensor_tensor(x_lo[:, 0:tiles, cols], ps[:, k % 4, 0:tiles * P].rearrange("p (t n) -> p t n", t=tiles),
                                      x_hi[:, 0:tiles, cols].bitcast(F32), ALU.subtract).then_inc(xlo_rd, 1)

                dve.wait_ge(rank_ps, layer + 1)
                rank = ps[:, 5, 0:4 * G].rearrange("p (t e) -> p t e", t=tiles)
                mine = routed[:, 0:tiles, :]
                step(dve.scalar_tensor_tensor(rank_e[:, 0:tiles, :], rank, 1.0, mine, ALU.add, ALU.mult))
                step(dve.tensor_scalar(rank_e[:, 0:tiles, :], rank_e[:, 0:tiles, :], 1.0, None, ALU.subtract))
                step.add(dve.tensor_reduce(small[:, 48:49], ps[:, 5, 64:80], AX_X, ALU.max))
                key = [rt[:, 2 + n, 0:4 * G].rearrange("p (t e) -> p t e", t=tiles) for n in range(2)]
                place = rt[:, 4, 0:4 * G].rearrange("p (t e) -> p t e", t=tiles)
                step(dve.tensor_tensor(place, rank_e[:, 0:tiles, :], ekey[:, :].unsqueeze(1).to_broadcast([P, tiles, 16]),
                                       ALU.add))
                step(dve.tensor_copy(count_i[:, :], small[:, 48:49]))
                for p in range(1, tiles):
                    step(dve.tensor_scalar(key[0], rank_e[:, 0:tiles, :], float(P * p), float((N_EXPERTS - 1) * P),
                                           ALU.is_ge, ALU.mult))
                    step(dve.tensor_tensor(place, place, key[0], ALU.add))
                for two, far in enumerate((FAR, -1.0)):
                    step(dve.scalar_tensor_tensor(key[two], place, far, mine, ALU.subtract, ALU.mult))
                    step(dve.tensor_scalar(key[two], key[two], far, None, ALU.add))
                    step(dve.tensor_reduce(two_at[:, two, 0:tiles], key[two], AX_X, (ALU.min, ALU.max)[two]))
                    step.add(dve.tensor_copy(two_idx[:, two, 0:tiles], two_at[:, two, 0:tiles]))
                    step(dve.tensor_tensor(key[two], key[two], two_at[:, two, 0:tiles].unsqueeze(2).to_broadcast([P, tiles, 16]),
                                           ALU.is_equal))
                    step(dve.tensor_tensor(key[two], key[two], comb[:, 0:tiles, :], ALU.mult))
                    ins = dve.tensor_reduce(two_w[:, two, 0:tiles], key[two], AX_X, ALU.add)
                    if two == 0:
                        step(ins)
                    else:
                        ins.then_inc(rt_rd, 1)

            def experts(layer):
                tiles = (4, 2)[layer]

                def first(e):
                    return e + layer * N_EXPERTS

                def choose(e, where):
                    for t in range(tiles):
                        ins = dve.tensor_scalar(pick[:, t, :], slots[:, :], rank_e[:, t, bass.ds(e, 1)], None, ALU.is_equal)
                    ins.then_inc(where, 1)

                def pick_rows(e):
                    if not (isinstance(e, int) and first(e) == 0):
                        dve.wait_ge(pick_ps, first(e) * 2)
                    choose(e, pick_rd)

                def low(e, j, i):
                    m, half = i // 2, i % 2
                    dve.wait_ge(whi_rd, first(e) * HALVES + (i + 1))
                    b = (j * HALVES + i) % SPLITS
                    dve.tensor_tensor(w_lo[:, b, :], ring[:, m, half * HALF:(half + 1) * HALF],
                                      w_hi[:, b, :].bitcast(F32), ALU.subtract).then_inc(wlo_rd, 1)

                def body(e, j, last):
                    low(e, j, 4)
                    if not last:
                        pick_rows(e + 1)
                    low(e, j, 5)
                    if not last:
                        low(e + 1, 1 - j, 0)
                    dve.wait_ge(silu_rd, first(e) + 1)
                    dve.tensor_tensor(glu[:, :], glu[:, :], ps[:, 3, :], ALU.mult).then_inc(glu_rd, 1)
                    if not last:
                        low(e + 1, 1 - j, 1)
                    dve.wait_ge(ghi_rd, first(e) + 1)
                    dve.tensor_tensor(glu_lo[:, :, :].rearrange("p f n -> p (f n)"), ps[:, 7, :],
                                      glu_hi[:, :, :].bitcast(F32).rearrange("p f n -> p (f n)"), ALU.subtract).then_inc(glo_rd, 1)
                    if not last:
                        low(e + 1, 1 - j, 2)
                        low(e + 1, 1 - j, 3)

                pick_rows(0)
                for i in range(SPLITS):
                    low(0, 0, i)
                body(0, 0, False)
                with dve.Fori(0, N_EXPERTS // 2 - 1) as i:
                    body(i * 2 + 1, 1, False)
                    body(i * 2 + 2, 0, False)
                body(N_EXPERTS - 1, 1, True)
                dve.wait_ge(w_ps, (layer + 1) * N_EXPERTS * HALVES)
                dve.wait_ge(y_st, (layer + 1) * N_EXPERTS * 16)

                most = dve.value_load(count_i[0:1, 0:1], min_val=0, max_val=CAPACITY)
                with dve.If(most > P):
                    with dve.Fori(0, (4, 2)[layer] - 1) as p:
                        dve.tensor_scalar(rank_e[:, 0:tiles, :], rank_e[:, 0:tiles, :], float(P), None,
                                          ALU.subtract).then_inc(more_rank[layer], 1)
                        with dve.Fori(0, N_EXPERTS) as e:
                            g = p * N_EXPERTS + e
                            dve.wait_ge(more_rank[layer], p + 1)
                            choose(e, more_dve[layer])
                            dve.wait_ge(more_pe[layer], g * 4 + 2)
                            dve.tensor_copy(xg_f[:, :, :].rearrange("p (a k) n -> p a (k n)", a=2), ps[:, 0:2, :]
                                            ).then_inc(more_dve[layer], 1)
                            dve.wait_ge(more_act[layer], g + 1)
                            dve.tensor_tensor(glu[:, :], glu[:, :], ps[:, 3, :], ALU.mult).then_inc(more_dve[layer], 1)
                            dve.wait_ge(more_pe[layer], g * 4 + 4)
                            dve.tensor_copy(glu_t[:, :, :].rearrange("p f n -> p (f n)"), ps[:, 7, :]
                                            ).then_inc(more_dve[layer], 1)
                            dve.wait_ge(more_pe[layer], g * 4 + 5)
                            dve.tensor_copy(y_sb[:, :].rearrange("p (a n) -> p a n", a=2), ps[:, 5:7, :]
                                            ).then_inc(more_dve[layer], 1)

            def add_experts(layer, rows):
                dve.wait_ge(gr_rd, rows)
                for t in range((4, 2)[layer]):
                    one, other = y_two[:, t, 0, :], y_two[:, t, 1, :]
                    dve.wait_ge(two_rd, (0, 4)[layer] + t + 1)
                    step(dve.scalar_tensor_tensor(one, other, two_w[:, 1, t:t + 1], one, ALU.mult, ALU.add))
                    step(dve.tensor_tensor(one, one, gate_row[:, t // 2, :], ALU.mult))
                    dve.tensor_tensor(h[:, t, :], h[:, t, :], one, ALU.add).then_inc((h_rd, res_rd)[layer], 1)

            router(0)
            experts(0)
            diagonals(0, 5, 2)
            add_experts(0, 8)
            ada(1, 0, 7)
            norm(2)

            for hd in range(4):
                dve.wait_ge(p1_ps, 5 + hd)
                dve.tensor_copy(kT[:, hd, :], ps[:, 4 + hd, :]).then_inc(p1_dve, 1)
            for half in range(2):
                for t in range(4):
                    m = half * 4 + t
                    dve.wait_ge(p1_ps, 9 + m)
                    dve.tensor_copy(v1[:, t, half * 512:(half + 1) * 512], ps[:, m, :]).then_inc(p1_dve, 1)
            step(dve.memset(reset, 1.0))
            step(dve.memset(reset.rearrange("p (n t) -> p n t", t=CHUNK)[:, :, 0:1], 0.0))
            ada(1, 1, 3)

            for hd in range(HEADS):
                dve.wait_ge(z_ps, hd + 1)
                for d in range(2):
                    gb = vec_b[:, 60 + 4 * d + hd:61 + 4 * d + hd]
                    dve.tensor_scalar(lmin[:, d, :], ps[:, d, :], gb, None, ALU.add).then_inc(z_rd, 1)
                dve.wait_ge(zl_rd, hd + 1)
                step(dve.scalar_tensor_tensor(lmin[:, :, :], lmin[:, :, :], 0.0, absz[:, :, :], ALU.min, ALU.subtract))
                step.add(dve.tensor_tensor_scan(bcum[:, 0, :], reset, lmin[:, 0, :], 0.0, ALU.mult, ALU.add))
                step(dve.tensor_tensor_scan(bcum[:, 1, ::-1], reset, lmin[:, 1, ::-1], 0.0, ALU.mult, ALU.add))
                b3 = [bcum[:, d, :].rearrange("p (n t) -> p n t", t=CHUNK) for d in range(2)]
                ends = [b3[0][:, :, CHUNK - 1:CHUNK], b3[1][:, :, 0:1]]
                l3 = [lmin[:, d, :].rearrange("p (n t) -> p n t", t=CHUNK) for d in range(2)]
                dve.tensor_copy(gla_small[:, 0, :].unsqueeze(2), ends[0]).then_inc(bc_rd, 1)
                step.add(dve.tensor_copy(gla_small[:, 1, :].unsqueeze(2), ends[1]))
                for d in range(2):
                    ins = dve.tensor_tensor(l3[d], ends[d].to_broadcast([P, 8, CHUNK]), b3[d], ALU.subtract)
                    if d:
                        step.wait()
                        ins.then_inc(bc_rd, 1)
                    else:
                        step.add(ins)
                dve.wait_ge(ee_rd, 4 * hd + 2)
                q2 = qT[:, hd, :].unsqueeze(1).to_broadcast([P, 2, 256])
                k2 = kT[:, hd, 0:256].unsqueeze(1).to_broadcast([P, 2, 256])
                dve.tensor_tensor(qdec[:, :, :], ebuf[:, :, 0:256], q2, ALU.mult).then_inc(qd_rd, 1)
                dve.tensor_tensor(kinc[:, :, :], ebuf[:, :, 256:512], k2, ALU.mult).then_inc(qd_rd, 1)
                dve.wait_ge(ee_rd, 4 * hd + 4)
                dve.tensor_tensor(kendT[:, :, :], absz[:, :, :], kT[:, hd, :].unsqueeze(1).to_broadcast([P, 2, 512]),
                                  ALU.mult).then_inc(ee_us, 1)
                dve.wait_ge(at_ps, hd + 1)
                dve.tensor_tensor(att[:, :, :, :], ps[:, 2, :].rearrange("p (d t n) -> p d t n", d=2, t=2),
                                  gla_mask[:, :, :].unsqueeze(2).to_broadcast([P, 2, 2, P]), ALU.mult).then_inc(att_rd, 1)
                for q in range(7):
                    for d in range(2):
                        ch = (4 + q if q < 4 else q - 4) if d == 0 else 7 - q
                        dve.wait_ge(ds_ps, 14 * hd + 2 * q + d + 1)
                        if q == 0:
                            dve.tensor_copy(state[:, 0, d, :], ps[:, d, 0:DV]).then_inc(st_rd, 1)
                        else:
                            dve.wait_ge(st_rd, 14 * hd + 2 * (q - 1) + d + 1)
                            dve.scalar_tensor_tensor(state[:, q % 2, d, :], state[:, (q - 1) % 2, d, :],
                                                     gla_small[:, d, ch:ch + 1], ps[:, d, 0:DV],
                                                     ALU.mult, ALU.add).then_inc(st_rd, 1)
                dve.wait_ge(o_ps, hd + 1)

            dve.wait_ge(og_std, 1)
            step(dve.reciprocal(small[:, 16:24], small[:, 8:16]))
            for t in range(2):
                for hd in range(4):
                    src = ps[:, 4 + 2 * t + hd // 2, (hd % 2) * DV:(hd % 2 + 1) * DV]
                    step.add(dve.scalar_tensor_tensor(og[:, t, hd * DV:(hd + 1) * DV], src,
                                                      small[:, 16 + t * 4 + hd:17 + t * 4 + hd], g_out[:, :],
                                                      ALU.mult, ALU.mult))
                step.wait()
                dve.tensor_tensor(og[:, t, :], og[:, t, :], r_sb[:, t, :], ALU.mult).then_inc(og_rd, 1)
            dve.wait_ge(og_rd, 2)
            diagonals(1, 2, 1)
            residual(1, 8, 10, 8)
            norm(3)
            router(1)
            experts(1)
            diagonals(1, 5, 1)
            add_experts(1, 12)


_INS = ['x', 'c', 'ctx', 'c_ctx', 'router_w', 'router_bias', 'ada_w', 'ada_b', 'norm_mix_g', 'norm_ffn_g',
        'moe_w_gate', 'moe_w_up', 'moe_w_down', 'ev_w_in', 'ev_w_out', 'ev_conv_w', 'ev_conv_b',
        'ev_rg_w', 'ev_rg_b', 'ev_ig_w', 'ev_ig_b', 'ev_lambda', 'ev_q_norm_g', 'ev_k_norm_g', 'ev_sink',
        'od_w_in', 'od_w_out', 'od_gate_up', 'od_gate_b', 'od_out_norm_g']


def rope_tables(tokens, grid, head_dim):
    import numpy as np
    freqs = head_dim // 4
    inv = np.float32(10000.0) ** (-np.arange(freqs, dtype=np.float32) / np.float32(freqs))
    pos = np.arange(tokens)
    row = (pos // grid).astype(np.float32)[:, None] * inv
    col = (pos % grid).astype(np.float32)[:, None] * inv
    angle = np.concatenate([row, col], axis=1)
    return np.cos(angle).astype(np.float32), np.sin(angle).astype(np.float32)


def kernel(**inputs):
    import numpy as _np
    import concourse.bacc as _bacc
    from concourse import mybir as _mybir
    from concourse.bass_utils import run_bass_kernel_spmd as _run

    nc = _bacc.Bacc("TRN2", target_bir_lowering=False, num_devices=1)
    arrays, args = {}, []
    for name in _INS:
        a = _np.ascontiguousarray(inputs[name])
        arrays[f"in_{name}_dram"] = a
        args.append(nc.dram_tensor(f"in_{name}_dram", a.shape, _mybir.dt.from_np(a.dtype), kind="ExternalInput").ap())
    for name, a in zip(("rope_cos", "rope_sin"), rope_tables(256, 64, 64)):
        arrays[f"in_{name}_dram"] = a
        args.append(nc.dram_tensor(f"in_{name}_dram", a.shape, _mybir.dt.float32, kind="ExternalInput").ap())
    args.append(nc.dram_tensor("out_0_dram", (1, 256, 1024), _mybir.dt.float32, kind="ExternalOutput").ap())
    build(nc, *args)
    r = _run(nc, [arrays], core_ids=[0])
    return r.results[0]["out_0_dram"]
```

```python
from contextlib import ExitStack

import concourse.bass as bass
from concourse import mybir

F32 = mybir.dt.float32
F32R = mybir.dt.float32r
I32 = mybir.dt.int32
U32 = mybir.dt.uint32
ALU = mybir.AluOpType
ACT = mybir.ActivationFunctionType
AX_X = mybir.AxisListType.X

P = 128
D = 1024
MEM0 = 16896
MEM_END = 229344
KD = D // P
EPS = 1e-6
NEG = -1e30
N_EXPERTS = 16
D_EXPERT = 512
FT = D_EXPERT // P
RING = 3
SLOT = 4096
HALF = SLOT // 2
HALVES = 6
SPLITS = 4
CAPACITY = 512
FAR = 16384.0
ATT_SCALE = 64 ** -0.5
CHUNK = 64
DK = 128
DV = 256
HEADS = 4

ADA_EARLY = 4
ADA_LATE = 8
EV_IN = 4
OD_IN = 7
EV_STEPS = 7
OUT_STEPS = 4
OD_STEPS = 12
L0_SLOTS = ADA_EARLY + EV_IN + ADA_LATE + 2
MOE_SLOTS = 3 * N_EXPERTS
L1_SLOTS = ADA_EARLY + OD_IN + ADA_LATE + 2
L1_BASE = L0_SLOTS + MOE_SLOTS
L1_MOE = L1_BASE + L1_SLOTS


class Chain:

    def __init__(self, eng, sem):
        self.eng, self.sem, self.n = eng, sem, 0

    def __call__(self, ins):
        self.add(ins)
        self.wait()

    def add(self, ins):
        ins.then_inc(self.sem, 1)
        self.n += 1

    def wait(self):
        self.eng.wait_ge(self.sem, self.n)


def build(nc, x, c, ctx, c_ctx, router_w, router_bias, ada_w, ada_b, norm_mix_g, norm_ffn_g,
          moe_w_gate, moe_w_up, moe_w_down, ev_w_in, ev_w_out, ev_conv_w, ev_conv_b,
          ev_rg_w, ev_rg_b, ev_ig_w, ev_ig_b, ev_lambda, ev_q_norm_g, ev_k_norm_g, ev_sink,
          od_w_in, od_w_out, od_gate_up, od_gate_b, od_out_norm_g, rope_cos, rope_sin, out):
    with ExitStack() as stack:
        def sem(name):
            return stack.enter_context(nc.semaphore(name))

        ps = stack.enter_context(nc.psum_tensor("ps", [P, 8, 512], F32))

        def at(name, shape, kib, dtype=F32):
            return nc.alloc_sbuf_tensor_at(name, shape, dtype, offset=MEM0 + int(kib * 1024))

        h = at("h", [P, 4, D], 0)
        nT = at("nT", [P, KD, 512], 16)
        xn = at("xn", [P, 4, D], 32)
        ring = at("ring", [P, RING, SLOT], 64)
        region_r = at("region_r", [P, 2048], 112)
        region_u = at("region_u", [P, 2048], 120)
        region_g = at("region_g", [P, 2048], 128)
        region_q = at("region_q", [P, 2560], 136)
        region_t = at("region_t", [P, 2560], 146)
        region_b = at("region_b", [P, 2048], 156)
        region_v = at("region_v", [P, 512], 164)
        region_w = at("region_w", [P, KD, 512], 48)
        tmp = at("tmp", [P, 2, 512], 166)
        x_hi = at("x_hi", [P, 4, D], 32, F32R)
        x_lo = at("x_lo", [P, 4, D], 48, F32R)
        xg_hi = at("xg_hi", [P, KD, P], 16, F32R)
        xg_lo = at("xg_lo", [P, KD, P], 20, F32R)
        pick = at("pick", [P, 4, P], 24, F32R)
        glu = at("glu", [P, D_EXPERT], 26)
        glu_hi = at("glu_hi", [P, FT, P], 28, F32R)
        glu_lo = at("glu_lo", [P, FT, P], 30, F32R)
        w_hi = at("w_hi", [P, SPLITS, HALF], 112, F32R)
        w_lo = at("w_lo", [P, SPLITS, HALF], 144, F32R)
        y_sb = at("y_sb", [P, D], 176)
        n_hi = at("n_hi", [P, KD, 512], 48, F32R)
        n_lo = [at(f"n_lo{layer}", [P, KD, 512], (32, 156)[layer], F32R) for layer in range(2)]
        in_hi = [[at(f"in_hi{layer}_{b}", [P, HALF], kib, F32R) for b, kib in enumerate(places)]
                 for layer, places in enumerate(((112, 146), (112, 128)))]
        in_lo = [[at(f"in_lo{layer}_{b}", [P, HALF], kib, F32R) for b, kib in enumerate(places)]
                 for layer, places in enumerate(((170, 136), (172, 144)))]
        m_hi = [at(f"m_hi{layer}", [P, KD, (512, 256)[layer]], 48, F32R) for layer in range(2)]
        m_lo = [[at(f"m_lo{layer}_{b}", [P, 4, (512, 256)[layer]], kib, F32R) for b, kib in enumerate(places)]
                for layer, places in enumerate(((120, 156), (56, 60)))]
        out_hi = [[at(f"out_hi{layer}_{b}", [P, HALF], kib, F32R) for b, kib in enumerate(places)]
                  for layer, places in enumerate(((170, 16), (170, 112)))]
        out_lo = [[at(f"out_lo{layer}_{b}", [P, HALF], kib, F32R) for b, kib in enumerate(places)]
                  for layer, places in enumerate(((146, 24), (146, 120)))]
        mod_rows = [at(f"mod_rows{place}", [P, 4, 512], (48, 170)[place]) for place in range(2)]
        xg_f = at("xg_f", [P, KD, P], 16)
        glu_t = at("glu_t", [P, FT, P], 28)
        y_two = at("y_two", [P, 4, 2, D], 32)

        small_at = [MEM0 + 180 * 1024]

        def sb(name, shape, dtype=F32):
            size = 4
            for n in shape[1:]:
                size *= n
            t = nc.alloc_sbuf_tensor_at(name, shape, dtype, offset=small_at[0])
            small_at[0] += -(-size // 32) * 32
            assert small_at[0] <= MEM_END
            return t

        ident = sb("ident", [P, P])
        ones = sb("ones", [P, P])
        wmask = sb("wmask", [P, 2, P])
        gla_mask = sb("gla_mask", [P, 2, P])
        rope = sb("rope", [P, 2, 2, 32])
        rows_a = sb("rows_a", [P, P])
        rows_b = sb("rows_b", [68, P])
        vec_a = sb("vec_a", [P, P])
        vec_b = sb("vec_b", [P, 68])
        cond = sb("cond", [P, 2, KD])
        mod = sb("mod", [P, 2, 48, 2])
        affine = sb("affine", [P, 4, KD, 2])
        sp = sb("sp", [P, 8, 8])
        small = sb("small", [P, 64])
        ssq = sb("ssq", [P, 4, 8])
        rstd = sb("rstd", [P, 4, 8])
        g_qk = sb("g_qk", [P, 2, 64])
        sink = sb("sink", [P, 2, 8])
        g_out = sb("g_out", [P, DV])
        bias_r = sb("bias_r", [P, N_EXPERTS])
        rw = sb("rw", [P, KD, N_EXPERTS])
        qk_ss = sb("qk_ss", [P, 3, 40])
        soft = sb("soft", [P, 2, 5, 4])
        rt = sb("rt", [P, 10, 64])
        cmp = sb("cmp", [P, 2, 256])
        first_of_i = sb("first_of_i", [P, 4, 4], I32)
        first_of = sb("first_of", [P, 4, 4])
        comb = sb("comb", [P, 4, N_EXPERTS])
        routed = sb("routed", [P, 4, N_EXPERTS])
        rank_e = sb("rank_e", [P, 4, N_EXPERTS])
        two_w = sb("two_w", [P, 2, 4])
        two_at = sb("two_at", [P, 2, 4])
        two_idx = sb("two_idx", [P, 2, 4], U32)
        count_i = sb("count_i", [P, 1], I32)
        before = sb("before", [P, P])
        slots_i = sb("slots_i", [P, P], I32)
        slots = sb("slots", [P, P])
        ekey_i = sb("ekey_i", [P, N_EXPERTS], I32)
        ekey = sb("ekey", [P, N_EXPERTS])
        gla_small = sb("gla_small", [P, 2, 2, 8])
        eps_c = sb("eps_c", [P, 1])
        rows_e = sb("rows_e", [P, D])
        gate_up = sb("gate_up", [48, 512])
        gate_in = sb("gate_in", [P, KD, 48])

        uc = region_u[:, :].rearrange("p (c t) -> p c t", c=4)
        gg = region_g[:, :].rearrange("p (c t) -> p c t", c=4)
        qk = region_q[:, :].rearrange("p (t n) -> p t n", t=4)
        qkT = region_t[:, :].rearrange("p (j t) -> p j t", j=5)
        v_sb = region_v[:, :].rearrange("p (t n) -> p t n", t=4)
        bd = region_b[:, :].rearrange("p (m n) -> p m n", m=16)
        mixT = xn[:, :, :].rearrange("p a b -> p (a b)").rearrange("p (k t) -> p k t", k=8)
        rg_r = [region[:, :].rearrange("p (u t) -> p u t", u=4) for region in (region_r, region_b)]
        nT_flat = nT[:, :, :].rearrange("p k t -> p (k t)")
        rg_i = [region[:, 0:4, :] for region in (nT, region_w)]
        rg_a = [region[:, 4:8, :] for region in (nT, region_w)]
        prob = nT_flat.rearrange("p (b g t) -> p b g t", b=2, g=4)
        probT = region_r[:, :].rearrange("p (s n) -> p s n", s=4)
        gate_row = region_g[:, :].rearrange("p (s n) -> p s n", s=2)
        diag = region_q[:, 0:2048].rearrange("p (s k n) -> p s k n", s=2, k=8)
        v1 = xn
        kT = region_u[:, :].rearrange("p (h t) -> p h t", h=4)
        r_sb = region_g[:, :].rearrange("p (t n) -> p t n", t=2)
        qT = region_q[:, 0:1024].rearrange("p (h t) -> p h t", h=4)
        aT = region_q[0:48, 1024:1536]
        absz = region_t[:, 1024:2048].rearrange("p (d t) -> p d t", d=2)
        att = region_t[:, 2048:2560].rearrange("p (d t n) -> p d t n", d=2, t=2)
        gates = region_w[:, :, :].rearrange("p (h d) t -> p h d t", d=2)
        gates_abs = nT[:, :, :].rearrange("p (h d) t -> p h d t", d=2)
        lmin = nT[:, 0:2, :]
        bcum = nT[:, 2:4, :]
        ebuf = nT[:, 4:6, :]
        kendT = nT[:, 6:8, :]
        kend = region_r[:, 0:1024].rearrange("p (d t n) -> p d t n", d=2, t=4)
        qdec = region_r[:, 1024:1536].rearrange("p (d t) -> p d t", d=2)
        kinc = region_r[:, 1536:2048].rearrange("p (d t) -> p d t", d=2)
        state = region_b[:, 0:1024].rearrange("p (b d n) -> p b d n", b=2, d=2)
        og = nT_flat[:, 0:2048].rearrange("p (t n) -> p t n", t=2)
        oT = nT_flat[:, 2048:4096].rearrange("p (k t) -> p k t", k=8)
        reset = region_b[:, 1024:1536]
        y_dram = nc.dram_tensor("expert_rows", (N_EXPERTS * CAPACITY, D), F32, kind="Internal").ap()

        s_rows = sem("rows_loaded")
        s_small = sem("small_loaded")
        s_bdl = sem("blocks_loaded")
        s_gup = sem("gate_up_loaded")
        s_h0 = sem("h_loaded")
        slot_full = [sem(f"slot_full{i}") for i in range(RING)]
        s_const = sem("constants_ready")
        s_bd0 = sem("blocks_zeroed")
        pool_step = sem("pool_step")
        act_step = sem("act_step")
        dve_step = sem("dve_step")
        vec_ps = sem("vectors_transposed")
        vec_rd = sem("vectors_ready")
        cond_rd = sem("cond_ready")
        ada_ps = sem("ada_product")
        ada_row = sem("ada_row_ready")
        ada_tp = sem("ada_transposed")
        mod_add = sem("mod_added")
        mod_rd = sem("mod_ready")
        std_rd = sem("std_ready")
        rstd_rd = sem("rstd_ready")
        xn_rd = sem("xn_ready")
        tp_ps = sem("norm_transposed")
        nT_act = sem("nT_act")
        nT_dve = sem("nT_dve")
        h_rd = sem("h_updated")
        nhi_rd = sem("n_hi_ready")
        nlo_rd = sem("n_lo_ready")
        inhi_rd = sem("in_hi_ready")
        inlo_rd = sem("in_lo_ready")
        even_ps = sem("even_step_product")
        gin_rd = sem("gate_in_ready")
        proj_ps = sem("proj_product")
        uc_rd = sem("uc_ready")
        gelu_rd = sem("gelu_ready")
        qkv_rd = sem("qkv_ready")
        qkss = sem("qk_squares")
        qkstd = sem("qk_std")
        qkn_rd = sem("qk_ready")
        qkt_ps = sem("qk_transposed")
        qkt_rd = sem("qkT_ready")
        sp_e = sem("softplus_exp")
        sp_x = sem("softplus_arg")
        sp_l = sem("softplus_ln")
        sp_rd = sem("softplus_ready")
        rg_ps = sem("rg_product")
        sg_rd = sem("sigmoid_ready")
        at_rd = sem("exp_tanh_ready")
        va_rd = sem("variance_ready")
        sq_rd = sem("sqrt_ready")
        half_rd = sem("rglru_half_done")
        sc_ps = sem("scores_product")
        sc_rd = sem("scores_ready")
        nm_rd = sem("negmax_ready")
        ex_rd = sem("probs_ready")
        pn_rd = sem("probs_normed")
        pt_ps = sem("probs_transposed")
        pt_rd = sem("probT_ready")
        pv_ps = sem("pv_product")
        pv_rd = sem("att_out_ready")
        dg_rd = sem("diag_ready")
        gr_ps = sem("gate_rows_product")
        gr_rd = sem("gate_rows_ready")
        mhi_rd = sem("mixed_hi_ready")
        mlo_rd = sem("mixed_lo_ready")
        outhi_rd = sem("out_hi_ready")
        outlo_rd = sem("out_lo_ready")
        outstep_ps = sem("out_step_product")
        y_ps = sem("mixer_product")
        y_rd = sem("mixer_added")
        rt_ps = sem("router_product")
        rt_sg = sem("router_scores")
        rt_rd = sem("routing_ready")
        rank_ps = sem("ranks_product")
        back_ps = sem("rows_transposed_back")
        xhi_rd = sem("x_hi_ready")
        xlo_rd = sem("x_lo_ready")
        whi_rd = sem("w_hi_ready")
        wlo_rd = sem("w_lo_ready")
        w_ps = sem("split_weights_used")
        pick_rd = sem("pick_ready")
        pick_ps = sem("gather_product")
        row_rd = sem("gathered_rows_ready")
        xt_ps = sem("gathered_transposed")
        xgh_rd = sem("xg_hi_ready")
        xgl_rd = sem("xg_lo_ready")
        silu_rd = sem("silu_ready")
        glu_rd = sem("glu_ready")
        gt_ps = sem("glu_transposed")
        ghi_rd = sem("glu_hi_ready")
        glo_rd = sem("glu_lo_ready")
        y_sbrd = sem("expert_rows_ready")
        y_st = sem("expert_rows_stored")
        all_done = sem("experts_done")
        two_ld = [sem(f"expert_rows_loaded{t}") for t in range(4)]
        two_rd = sem("first_rows_weighted")
        more_rank = [sem(f"more_rank{n}") for n in range(2)]
        more_st = [sem(f"more_stored{n}") for n in range(2)]
        more_ld = [sem(f"more_loaded{n}") for n in range(2)]
        more_dve = [sem(f"more_dve{n}") for n in range(2)]
        more_act = [sem(f"more_act{n}") for n in range(2)]
        more_pe = [sem(f"more_pe{n}") for n in range(2)]
        p1_ps = sem("proj1_product")
        p1_act = sem("proj1_act")
        p1_dve = sem("proj1_dve")
        z_ps = sem("gate_logits")
        z_rd = sem("gate_abs_ready")
        zl_rd = sem("gate_ln_ready")
        bc_rd = sem("decay_sum_ready")
        ee_rd = sem("decay_exp")
        ee_us = sem("decay_exp_used")
        ke_ps = sem("kend_transposed")
        ke_rd = sem("kend_ready")
        qd_rd = sem("qdec_kinc_ready")
        at_ps = sem("intra_product")
        att_rd = sem("intra_masked")
        ds_ps = sem("state_product")
        st_rd = sem("state_ready")
        o_ps = sem("gla_out_product")
        og_std = sem("og_std")
        og_rd = sem("og_ready")
        og_ps = sem("og_transposed")
        oT_rd = sem("oT_ready")
        res_rd = sem("result_ready")
        s_out = sem("result_stored")

        block = stack.enter_context(nc.Block())

        def slot(n):
            return ring[:, n % RING, :]

        def slot_kn(n, k=8):
            return slot(n).rearrange("p (k n) -> p k n", k=k)

        def last_use(n):
            if n < ADA_EARLY:
                return ada_ps, n + 1
            n -= ADA_EARLY
            if n < EV_IN:
                return inlo_rd, min(2 * n + 2, EV_STEPS)
            n -= EV_IN
            if n < ADA_LATE:
                return ada_ps, ADA_EARLY + n + 1
            n -= ADA_LATE
            if n < 2:
                return outlo_rd, 2 * n + 2
            n -= 2
            if n < MOE_SLOTS:
                return wlo_rd, 2 * n + 2
            n -= MOE_SLOTS
            if n < ADA_EARLY:
                return ada_ps, ADA_EARLY + ADA_LATE + n + 1
            n -= ADA_EARLY
            if n < OD_IN:
                return (inlo_rd, EV_STEPS + 2 * n + 2) if n < OD_IN - 1 else (p1_ps, 21)
            n -= OD_IN
            if n < ADA_LATE:
                return ada_ps, 2 * ADA_EARLY + ADA_LATE + n + 1
            return outlo_rd, OUT_STEPS + 2 * (n - ADA_LATE) + 2

        def expert_slot(layer, m):
            n = (L0_SLOTS, L1_MOE)[layer] + m
            return n % RING, n // RING

        def norm_tiles(n):
            return 2 if n == 3 else 4

        def mixed_ks(layer, j):
            return ((slice(0, 4), slice(4, 6), slice(6, 8)), (slice(0, 4), slice(4, 8)))[layer][j]

        def mixed_low(layer, ks):
            return m_lo[layer][ks.start // 4][:, ks.start % 4:ks.start % 4 + ks.stop - ks.start, :]

        def out_slot(layer, i):
            return (L0_SLOTS, L1_MOE)[layer] - 2 + i // 2

        def out_weights(layer, i):
            return slot(out_slot(layer, i))[:, (i % 2) * HALF:(i % 2 + 1) * HALF]

        def in_slot(layer, i):
            return (ADA_EARLY, L1_BASE + ADA_EARLY)[layer] + i // 2

        def in_weights(layer, i):
            return slot(in_slot(layer, i))[:, (i % 2) * HALF:(i % 2 + 1) * HALF]

        def in_step(layer, i):
            return EV_STEPS * layer + i + 1

        def in_done(layer, i):
            if i % 2 == 0:
                return even_ps, (0, 3)[layer] + i // 2 + 1
            return (proj_ps, 4 * (i // 2) + 4) if layer == 0 else (p1_ps, (4, 8, 12, 16, 18, 20)[i // 2])

        @block.sync
        def _(sp_eng):
            def load(n, dst, src):
                if n >= RING:
                    sp_eng.wait_ge(*last_use(n - RING))
                sp_eng.dma_start(dst, src).then_inc(slot_full[n % RING], 16)

            def ada(layer, first, count, n):
                for j in range(count):
                    if (layer, first, j) == (1, 0, 1):
                        sp_eng.wait_ge(y_st, 16 * N_EXPERTS)
                    src = ada_w[layer, :, (first + j) * 512:(first + j + 1) * 512]
                    load(n + j, slot_kn(n + j), src.rearrange("(k p) n -> p k n", p=P))

            def columns(n, w, a, b):
                width = b - a
                dst = slot(n)[:, 0:KD * width].rearrange("p (k n) -> p k n", k=KD)
                load(n, dst, w[0, :, a:b].rearrange("(k p) n -> p k n", p=P))

            def rows(n, w, half):
                load(n, slot_kn(n, 4), w[0, half * 512:(half + 1) * 512, :].rearrange("(k p) n -> p k n", p=P))

            def expert(layer, e, m):
                w = (moe_w_gate, moe_w_up, moe_w_down)[m]
                src = w[layer, bass.ds(e, 1), :, :].rearrange("o (k p) n -> p (o k) n", p=P)
                dst = ring[:, expert_slot(layer, m)[0], :].rearrange("p (k n) -> p k n", k=8 if m < 2 else 4)
                return dst, src

            def experts(layer, base):
                for m in range(3):
                    load(base + m, *expert(layer, 0, m))
                with sp_eng.Fori(1, N_EXPERTS) as e:
                    for m in range(3):
                        sp_eng.wait_ge(wlo_rd, e * HALVES + (2 * m + 2 - HALVES + layer * N_EXPERTS * HALVES))
                        sp_eng.dma_start(*expert(layer, e, m)).then_inc(slot_full[expert_slot(layer, m)[0]], 16)
                sp_eng.wait_ge(wlo_rd, (layer + 1) * N_EXPERTS * HALVES)
                sp_eng.wait_ge(rt_rd, 2 * layer + 2)
                most = sp_eng.value_load(count_i[0:1, 0:1], min_val=0, max_val=CAPACITY)
                with sp_eng.If(most > P):
                    sp_eng.sem_inc(more_st[layer], 1)
                    with sp_eng.Fori(1, (4, 2)[layer]) as p:
                        with sp_eng.Fori(0, N_EXPERTS) as e:
                            g = p * N_EXPERTS + e
                            rows_at = y_dram[bass.ds(e * P + p * (N_EXPERTS * P), P), :]
                            sp_eng.wait_ge(more_pe[layer], g * 4 + (1 - 4 * N_EXPERTS))
                            sp_eng.wait_ge(more_st[layer], g * 16 + (1 - 16 * N_EXPERTS))
                            for m in range(3):
                                sp_eng.dma_start(*expert(layer, e, m)).then_inc(more_ld[layer], 16)
                            sp_eng.wait_ge(more_dve[layer], g * 5 + (5 - 5 * N_EXPERTS))
                            sp_eng.dma_start(rows_at, y_sb[:, :]).then_inc(more_st[layer], 16)
                    sp_eng.wait_ge(more_st[layer], 16 * N_EXPERTS * ((4, 2)[layer] - 1) + 1)
                sp_eng.sem_inc(all_done, 1)

            ada(0, 0, ADA_EARLY, 0)
            n = ADA_EARLY
            for a, b in ((0, 512), (512, 1024), (1024, 1536), (1536, 1792)):
                columns(n, ev_w_in, a, b)
                n += 1
            ada(0, ADA_EARLY, ADA_LATE, n)
            n += ADA_LATE
            rows(n, ev_w_out, 0)
            rows(n + 1, ev_w_out, 1)
            experts(0, L0_SLOTS)
            n = L1_BASE
            ada(1, 0, ADA_EARLY, n)
            n += ADA_EARLY
            for a in range(0, 3072, 512):
                columns(n, od_w_in, a, a + 512)
                n += 1
            columns(n, od_w_in, 3072, 3104)
            n += 1
            ada(1, ADA_EARLY, ADA_LATE, n)
            n += ADA_LATE
            rows(n, od_w_out, 0)
            rows(n + 1, od_w_out, 1)
            experts(1, L1_MOE)
            for t in range(2):
                sp_eng.wait_ge(res_rd, t + 1)
                sp_eng.dma_start(out[0, t * P:(t + 1) * P, :], h[:, t, :]).then_inc(s_out, 16)
            sp_eng.wait_ge(s_out, 32)

        @block.gpsimd
        def _(pool):
            step = Chain(pool, pool_step)
            pool.memset(region_b[:, :], 0.0).then_inc(s_bd0, 1)
            pool.memset(ident[:, :], 0.0).then_inc(pool_step, 1)
            pool.iota(slots_i[:, :], [[1, P]], base=0, channel_multiplier=0).then_inc(pool_step, 1)
            pool.iota(ekey_i[:, :], [[P, N_EXPERTS]], base=0, channel_multiplier=0).then_inc(pool_step, 1)
            pool.iota(first_of_i[:, :, :], [[1, 4], [-1, 4]], base=0, channel_multiplier=0).then_inc(pool_step, 1)
            pool.memset(before[:, :], 1.0).then_inc(pool_step, 1)
            pool.memset(gla_mask[:, :, :], 1.0).then_inc(pool_step, 1)
            pool.memset(wmask[:, :, :], 0.0).then_inc(pool_step, 1)
            pool.memset(gate_in[:, :, :], 0.0).then_inc(pool_step, 1)
            step.n = 8
            step.wait()
            pool.memset(ones[:, :], 1.0).then_inc(s_const, 1)
            pool.memset(eps_c[:, :], EPS).then_inc(s_const, 1)
            pool.tensor_copy(slots[:, :], slots_i[:, :]).then_inc(s_const, 1)
            pool.tensor_copy(ekey[:, :], ekey_i[:, :]).then_inc(s_const, 1)
            step(pool.tensor_copy(first_of[:, :, :], first_of_i[:, :, :]))
            pool.tensor_scalar(first_of[:, :, :], first_of[:, :, :], 1.0, None, ALU.is_ge).then_inc(s_const, 1)
            pool.affine_select(out=before[:, :], in_=before[:, :], compare_op=ALU.is_gt, fill=0.0,
                               base=0, pattern=[[1, P]], channel_multiplier=-1).then_inc(s_const, 1)
            pool.affine_select(out=ident[:, :], in_=ident[:, :], compare_op=ALU.not_equal, fill=1.0,
                               base=0, pattern=[[-1, P]], channel_multiplier=1).then_inc(s_const, 1)
            pool.affine_select(out=wmask[:, 0, :], in_=wmask[:, 0, :], compare_op=ALU.is_ge,
                               fill=NEG, base=0, pattern=[[-1, P]], channel_multiplier=1).then_inc(s_const, 1)
            pool.affine_select(out=wmask[:, 1, :], in_=wmask[:, 1, :], compare_op=ALU.is_ge,
                               fill=NEG, base=0, pattern=[[1, P]], channel_multiplier=-1).then_inc(s_const, 1)
            step(pool.affine_select(out=gla_mask[:, 0, :], in_=gla_mask[:, 0, :], compare_op=ALU.is_ge,
                                    fill=0.0, base=0, pattern=[[1, P]], channel_multiplier=-1))
            step(pool.affine_select(out=gla_mask[:, 1, :], in_=gla_mask[:, 1, :], compare_op=ALU.is_ge,
                                    fill=0.0, base=0, pattern=[[-1, P]], channel_multiplier=1))
            pool.memset(gla_mask[0:CHUNK, 0, CHUNK:P], 0.0).then_inc(s_const, 1)
            pool.memset(gla_mask[CHUNK:P, 1, 0:CHUNK], 0.0).then_inc(s_const, 1)
            pool.wait_ge(s_bd0, 1)
            for b2 in range(2):
                for gate, w in enumerate((ev_rg_w, ev_ig_w)):
                    for d in range(2):
                        dst = bd[b2 * 64:(b2 + 1) * 64, gate * 8 + d * 4:gate * 8 + d * 4 + 4, b2 * 64:(b2 + 1) * 64]
                        src = w[0, d].rearrange("(ct b) c e -> b c ct e", b=2)[b2]
                        pool.dma_start(dst, src).then_inc(s_bdl, 16)
            for layer in range(2):
                pool.wait_ge(rt_rd, 2 * layer + 2)
                pool.wait_ge(y_st, 16 * N_EXPERTS * (layer + 1))
                pool.wait_ge(all_done, layer + 1)

                def two_rows(written):
                    for t in range((4, 2)[layer]):
                        for two in range(2):
                            pool.indirect_dma_start(y_two[:, t, two, :], None, y_dram[0:written, :],
                                                    bass.IndirectOffsetOnAxis(ap=two_idx[:, two, t:t + 1], axis=0)
                                                    ).then_inc(two_ld[t], 16)

                most = pool.value_load(count_i[0:1, 0:1], min_val=0, max_val=CAPACITY)
                with pool.If(most > P):
                    two_rows((4, 2)[layer] * N_EXPERTS * P)
                with pool.Else():
                    two_rows(N_EXPERTS * P)

        @block.scalar
        def _(act):
            step = Chain(act, act_step)
            ra = [(0, ada_b[0].rearrange("(k p) -> k p", p=P)), (48, ada_b[1].rearrange("(k p) -> k p", p=P)),
                  (96, norm_mix_g.rearrange("l (k p) -> (l k) p", p=P)),
                  (112, norm_ffn_g.rearrange("l (k p) -> (l k) p", p=P))]
            rb = [(0, c[0].rearrange("(k p) -> k p", p=P)), (8, c_ctx.rearrange("(k p) -> k p", p=P)),
                  (16, ev_conv_w[0].rearrange("j (k p) -> (j k) p", p=P)),
                  (32, ev_conv_b[0].rearrange("(k p) -> k p", p=P)),
                  (36, ev_rg_b[0].rearrange("d (k p) -> (d k) p", p=P)),
                  (44, ev_ig_b[0].rearrange("d (k p) -> (d k) p", p=P)),
                  (52, ev_lambda[0].rearrange("d (k p) -> (d k) p", p=P)),
                  (60, od_gate_b[0].rearrange("d (k p) -> (d k) p", p=P))]
            for tile, parts in ((rows_b, rb), (rows_a, ra)):
                for at, src in parts:
                    act.dma_start(tile[at:at + src.shape[0], :], src).then_inc(s_rows, 16)
            for t in range(4):
                src = (x, ctx)[t // 2][0, (t % 2) * P:(t % 2 + 1) * P, :]
                act.dma_start(h[:, t, :], src).then_inc(s_h0, 16)
            for cs, table in enumerate((rope_cos, rope_sin)):
                act.dma_start(rope[:, cs, :, :], table.rearrange("(t p) n -> p t n", p=P)).then_inc(s_small, 16)
            act.dma_start(g_qk[:, 0, :], ev_q_norm_g[0].partition_broadcast(P)).then_inc(s_small, 16)
            act.dma_start(g_qk[:, 1, :], ev_k_norm_g[0].partition_broadcast(P)).then_inc(s_small, 16)
            act.dma_start(sink[:, 0, :], ev_sink[0].partition_broadcast(P)).then_inc(s_small, 16)
            act.dma_start(g_out[:, :], od_out_norm_g[0].partition_broadcast(P)).then_inc(s_small, 16)
            act.dma_start(bias_r[:, :], router_bias.partition_broadcast(P)).then_inc(s_small, 16)
            act.dma_start(rw[:, :, :], router_w.rearrange("(k p) e -> p k e", p=P)).then_inc(s_small, 16)

            act.wait_ge(vec_rd, 1)
            act.activation(cond[:, :, :].rearrange("p s k -> p (s k)"), vec_b[:, 0:16], ACT.Silu).then_inc(cond_rd, 1)

            def n_high(layer, j):
                act.wait_ge(nT_act, 16 * layer + 2 * j + 2)
                act.wait_ge(nT_dve, 16 * layer + 2 * j + 2)
                act.activation(n_hi[:, 2 * j:2 * j + 2, :], nT[:, 2 * j:2 * j + 2, :], ACT.Copy).then_inc(nhi_rd, 1)

            def in_high(layer, i):
                n = in_slot(layer, i)
                act.wait_ge(slot_full[n % RING], 16 * (n // RING + 1))
                if i >= 2:
                    act.wait_ge(*in_done(layer, i - 2))
                act.activation(in_hi[layer][i % 2][:, :], in_weights(layer, i), ACT.Copy).then_inc(inhi_rd, 1)

            def norm(n):
                tiles = norm_tiles(n)
                if n == 0:
                    act.wait_ge(s_h0, 64)
                    act.wait_ge(s_const, 11)
                act.activation(small[0:1, 40:41], eps_c[0:1, 0:1], ACT.Sqrt)
                for t in range(tiles):
                    if n:
                        act.wait_ge(h_rd, (0, 0, 4, 8)[n] + t + 1)
                    squares = xn[:, t, :] if n % 2 else nT_flat[:, t * D:(t + 1) * D]
                    step(act.activation(squares, h[:, t, :], ACT.Square, accum_out=ssq[:, n, t:t + 1]))
                act.activation(ssq[:, n, 4:4 + tiles], ssq[:, n, 0:tiles], ACT.Sqrt,
                               scale=1.0 / D, bias=eps_c[:, 0:1]).then_inc(std_rd, 1)
                act.wait_ge(rstd_rd, n + 1)
                for t in range(0, tiles, 2):
                    act.activation(xn[:, t, :], h[:, t, :], ACT.Copy, scale=rstd[:, n, t:t + 1]).then_inc(xn_rd, 1)
                if n % 2 == 0:
                    for i in range(2):
                        in_high(n // 2, i)
                for k in range(0, KD, 2):
                    act.wait_ge(tp_ps, KD * n + k + 1)
                    if k == 0:
                        act.wait_ge(mod_rd, (1, 2, 3, 4)[n])
                    for s in range(tiles // 2):
                        act.activation(nT[:, k, s * 256:(s + 1) * 256], ps[:, k % 4, s * 256:(s + 1) * 256],
                                       ACT.Identity, scale=affine[:, n, k, s:s + 1],
                                       bias=mod[:, n // 2, (0 if n % 2 == 0 else 24) + k, s:s + 1]).then_inc(nT_act, 1)
                    if n % 2 == 0 and k:
                        n_high(n // 2, k // 2 - 1)
                if n % 2 == 0:
                    n_high(n // 2, 3)

            def ada_copy(s, bank):
                act.wait_ge(ada_ps, s + 1)
                act.activation(mod_rows[1][0:2, s % 4, :], ps[0:2, bank, :], ACT.Copy).then_inc(ada_row, 1)

            norm(0)

            act.wait_ge(sp_x, 1)
            act.activation(sp[:, 1, :], sp[:, 0, :], ACT.Exp, scale=-1.0).then_inc(sp_e, 1)
            act.wait_ge(sp_x, 2)
            act.activation(sp[:, 3, :], sp[:, 2, :], ACT.Ln).then_inc(sp_l, 1)

            for i in range(2, 5):
                in_high(0, i)
            for t in range(4):
                act.wait_ge(proj_ps, 5 + t)
                act.activation(gg[:, t, :], ps[:, 4 + t, :], ACT.Gelu_apprx_tanh).then_inc(gelu_rd, 1)
            for i in range(5, EV_STEPS):
                in_high(0, i)
            act.wait_ge(proj_ps, 12)
            for t in range(4):
                act.activation(qk[:, t, 0:512].rearrange("p (g kv d) -> p g kv d", g=4, kv=2),
                               ps[:, t, :].rearrange("p (kv g d) -> p g kv d", kv=2, g=4), ACT.Copy).then_inc(qkv_rd, 1)
            for t in range(4):
                act.wait_ge(proj_ps, 13 + t)
                act.activation(qk[:, t, 512:640], ps[:, 4 + t, 0:128], ACT.Copy).then_inc(qkv_rd, 1)
                act.activation(v_sb[:, t, :], ps[:, 4 + t, 128:256], ACT.Copy).then_inc(qkv_rd, 1)
            act.wait_ge(qkss, 1)
            act.activation(qk_ss[:, 1, :], qk_ss[:, 0, :], ACT.Sqrt, scale=1.0 / 64, bias=eps_c[:, 0:1]).then_inc(qkstd, 1)

            for half in range(2):
                if half:
                    act.wait_ge(rg_ps, 16)
                for u in range(4):
                    ct, d = 2 * half + u // 2, u % 2
                    for gate in range(2):
                        act.wait_ge(rg_ps, half * 8 + 2 * u + gate + 1)
                        bias_at = 36 + gate * 8 + d * 4 + ct
                        act.activation((rg_r, rg_i)[gate][half][:, u, :], ps[:, 2 * u + gate, :], ACT.Sigmoid,
                                       bias=vec_b[:, bias_at:bias_at + 1]).then_inc(sg_rd, 1)
            act.wait_ge(sg_rd, 16)
            act.wait_ge(sp_rd, 2)
            for half in range(2):
                for u in range(4):
                    ct, d = 2 * half + u // 2, u % 2
                    col = d * 4 + ct
                    act.activation(rg_a[half][:, u, :], rg_r[half][:, u, :], ACT.Exp,
                                   scale=sp[:, 6, col:col + 1]).then_inc(at_rd, 1)
                    act.activation(rg_r[half][:, u, :], rg_r[half][:, u, :], ACT.Tanh,
                                   scale=sp[:, 7, col:col + 1]).then_inc(at_rd, 1)
            for half in range(2):
                ada_copy(4 + half, 6)
                act.wait_ge(va_rd, 4 * half + 4)
                act.activation(rg_r[half], rg_r[half], ACT.Sqrt).then_inc(sq_rd, 1)

            for j in range(5):
                act.wait_ge(qkt_ps, j + 1)
                act.activation(qkT[:, j, :], ps[:, j, :], ACT.Copy).then_inc(qkt_rd, 1)
            for s in range(6, 8):
                ada_copy(s, 6)

            def mixed_high(layer, j):
                ks = mixed_ks(layer, j)
                act.activation(m_hi[layer][:, ks, :], (mixT, oT)[layer][:, ks, :], ACT.Copy).then_inc(mhi_rd, 1)

            def out_high(layer, i):
                n = out_slot(layer, i)
                act.wait_ge(slot_full[n % RING], 16 * (n // RING + 1))
                if i >= 2:
                    act.wait_ge(outstep_ps, 3 * layer + i - 1)
                act.activation(out_hi[layer][i % 2][:, :], out_weights(layer, i), ACT.Copy).then_inc(outhi_rd, 1)

            for u in range(8):
                keys = 512 if u < 4 else 256
                b = u % 2
                act.wait_ge(nm_rd, u + 1)
                for g in range(4):
                    act.activation(prob[:, b, g, 0:keys], prob[:, b, g, 0:keys], ACT.Exp,
                                   bias=soft[:, b, 1, g:g + 1], accum_out=soft[:, b, 3, g:g + 1]).then_inc(ex_rd, 1)
                act.activation(soft[:, b, 2, :], soft[:, b, 2, :], ACT.Exp).then_inc(ex_rd, 1)
                if u < 4:
                    ada_copy(8 + u, 6)
                else:
                    act.wait_ge(gr_ps, u - 3)
                    act.activation(gate_row[:, u // 2 - 2, (u % 2) * 512:(u % 2 + 1) * 512], ps[:, 6, :],
                                   ACT.Copy).then_inc(gr_rd, 1)
                if u > 0:
                    act.wait_ge(pv_ps, u)
                for s in range(keys // P):
                    n = (4 * u if u < 4 else 16 + 2 * (u - 4)) + s
                    act.wait_ge(pt_ps, n + 1)
                    act.activation(probT[:, s, :], ps[:, 4 + n % 2, :], ACT.Copy).then_inc(pt_rd, 1)
                if u == 4:
                    act.wait_ge(half_rd, 2)
                    mixed_high(0, 0)
                elif u == 6:
                    act.wait_ge(mod_rd, 2)
                    out_high(0, 0)

            def gate_rows(n, streams):
                for s in range(streams):
                    for half in range(2):
                        act.wait_ge(gr_ps, n + 2 * s + half + 1)
                        act.activation(gate_row[:, s, half * 512:(half + 1) * 512], ps[:, 2 * s + half, :],
                                       ACT.Copy).then_inc(gr_rd, 1)

            for j in range(2):
                act.wait_ge(pv_rd, 14 + 2 * j)
                mixed_high(0, j + 1)
            act.wait_ge(pv_ps, 8)
            for i in range(1, OUT_STEPS):
                out_high(0, i)
            norm(1)

            def router(layer):
                tiles = (4, 2)[layer]
                act.wait_ge(rt_ps, layer + 1)
                act.activation(rt[:, 0, 0:16 * tiles], ps[:, 4, 0:16 * tiles], ACT.Sigmoid).then_inc(rt_sg, 1)

            def experts(layer):
                tiles = (4, 2)[layer]
                for k in range(KD):
                    act.wait_ge(back_ps, KD * layer + k + 1)
                    act.activation(x_hi[:, 0:tiles, k * P:(k + 1) * P],
                                   ps[:, k % 4, 0:tiles * P].rearrange("p (t n) -> p t n", t=tiles), ACT.Copy).then_inc(xhi_rd, 1)

                def first(e):
                    return e + layer * N_EXPERTS

                def high(e, j, i):
                    m, half = i // 2, i % 2
                    n = first(e) * HALVES + i
                    at, fills = expert_slot(layer, m)
                    act.wait_ge(slot_full[at], e * 16 + 16 * (1 + fills))
                    if not (isinstance(e, int) and first(e) * HALVES + i < SPLITS):
                        act.wait_ge(w_ps, n - (SPLITS - 1))
                    act.activation(w_hi[:, (j * HALVES + i) % SPLITS, :], ring[:, at, half * HALF:(half + 1) * HALF],
                                   ACT.Copy).then_inc(whi_rd, 1)

                def gathered(e, c):
                    act.wait_ge(pick_ps, first(e) * 2 + (c + 1))
                    act.activation(rows_e[:, c * 512:(c + 1) * 512], ps[:, c, :], ACT.Copy).then_inc(row_rd, 1)

                def turned(e, c):
                    act.wait_ge(xt_ps, first(e) * 2 + (c + 1))
                    act.activation(xg_hi[:, 4 * c:4 * c + 4, :].rearrange("p k n -> p (k n)"), ps[:, (4, 0)[c], :],
                                   ACT.Copy).then_inc(xgh_rd, 1)

                def body(e, j, last):
                    high(e, j, 3)
                    high(e, j, 4)
                    act.wait_ge(w_ps, first(e) * HALVES + 2)
                    act.activation(glu[:, :], ps[:, 2, :], ACT.Silu).then_inc(silu_rd, 1)
                    high(e, j, 5)
                    if not last:
                        high(e + 1, 1 - j, 0)
                        high(e + 1, 1 - j, 1)
                        gathered(e + 1, 0)
                    act.wait_ge(gt_ps, first(e) + 1)
                    act.activation(glu_hi[:, :, :].rearrange("p f n -> p (f n)"), ps[:, 7, :], ACT.Copy).then_inc(ghi_rd, 1)
                    if not last:
                        gathered(e + 1, 1)
                        turned(e + 1, 0)
                        turned(e + 1, 1)
                        high(e + 1, 1 - j, 2)
                    act.wait_ge(w_ps, first(e) * HALVES + 6)
                    if not (isinstance(e, int) and first(e) == 0):
                        act.wait_ge(y_st, first(e) * 16)
                    act.activation(y_sb[:, :].rearrange("p (a n) -> p a n", a=2), ps[:, 5:7, :], ACT.Copy).then_inc(y_sbrd, 1)
                    act.wait_ge(y_sbrd, first(e) + 1)
                    act.dma_start(y_dram[bass.ds(e * P, P), :], y_sb[:, :]).then_inc(y_st, 16)

                high(0, 0, 0)
                high(0, 0, 1)
                for c in range(2):
                    gathered(0, c)
                for c in range(2):
                    turned(0, c)
                high(0, 0, 2)
                body(0, 0, False)
                with act.Fori(0, N_EXPERTS // 2 - 1) as i:
                    body(i * 2 + 1, 1, False)
                    body(i * 2 + 2, 0, False)
                body(N_EXPERTS - 1, 1, True)
                most = act.value_load(count_i[0:1, 0:1], min_val=0, max_val=CAPACITY)
                with act.If(most > P):
                    with act.Fori(0, ((4, 2)[layer] - 1) * N_EXPERTS) as g:
                        act.wait_ge(more_pe[layer], g * 4 + 3)
                        act.activation(glu[:, :], ps[:, 2, :], ACT.Silu).then_inc(more_act[layer], 1)

            def add_experts(layer, t):
                act.wait_ge(two_ld[t], 32 * (layer + 1))
                act.activation(y_two[:, t, 0, :], y_two[:, t, 0, :], ACT.Copy, scale=two_w[:, 0, t:t + 1]).then_inc(two_rd, 1)

            router(0)
            experts(0)
            ada_copy(12, 7)
            gate_rows(4, 2)
            add_experts(0, 0)
            ada_copy(13, 7)
            add_experts(0, 1)
            add_experts(0, 2)
            ada_copy(14, 7)
            add_experts(0, 3)
            ada_copy(15, 7)
            norm(2)

            for d in range(2):
                act.dma_start(gate_up[32 * d:32 * d + 16, :], od_gate_up[0, d]).then_inc(s_gup, 16)
            for i in range(2, 4):
                in_high(1, i)
            for hd in range(4):
                act.wait_ge(p1_ps, hd + 1)
                act.activation(qT[:, hd, :], ps[:, hd, 0:256], ACT.Copy, scale=DK ** -0.5).then_inc(p1_act, 1)
            for i in range(4, OD_STEPS):
                in_high(1, i)
            n = L1_BASE + ADA_EARLY + OD_IN - 1
            act.wait_ge(slot_full[n % RING], 16 * (n // RING + 1))
            for d in range(2):
                act.activation(gate_in[:, :, 32 * d:32 * d + 16],
                               slot(n)[:, 0:KD * 32].rearrange("p (k n) -> p k n", k=KD)[:, :, 16 * d:16 * d + 16],
                               ACT.Copy).then_inc(gin_rd, 1)
            act.wait_ge(p1_ps, 20)
            for t in range(2):
                for half in range(2):
                    act.activation(r_sb[:, t, half * 512:(half + 1) * 512], ps[:, 4 + 2 * t + half, :],
                                   ACT.Silu).then_inc(p1_act, 1)
            act.wait_ge(p1_ps, 21)
            for d in range(2):
                part = slice(32 * d, 32 * d + 16)
                act.activation(aT[part, :], ps[part, 0, :], ACT.Copy).then_inc(p1_act, 1)

            for hd in range(HEADS):
                act.wait_ge(z_rd, 2 * hd + 2)
                step.add(act.activation(gates_abs[:, hd], gates[:, hd], ACT.Abs))
            step.wait()
            for pair in range(2):
                heads = slice(2 * pair, 2 * pair + 2)
                step.add(act.activation(gates_abs[:, heads], gates_abs[:, heads], ACT.Exp, scale=-1.0))
            step.wait()
            for pair in range(2):
                heads = slice(2 * pair, 2 * pair + 2)
                act.activation(gates_abs[:, heads], gates_abs[:, heads], ACT.Ln, bias=1.0).then_inc(zl_rd, 1)
            ada_copy(16, 3)

            for hd in range(HEADS):
                act.wait_ge(bc_rd, 2 * hd + 1)
                act.activation(ebuf[:, :, 0:256], bcum[:, :, 0:256], ACT.Exp, scale=1 / 16.0).then_inc(ee_rd, 1)
                act.activation(ebuf[:, :, 256:512], bcum[:, :, 0:256], ACT.Exp, scale=-1 / 16.0).then_inc(ee_rd, 1)
                act.wait_ge(bc_rd, 2 * hd + 2)
                act.activation(gla_small[:, hd % 2], gla_small[:, hd % 2], ACT.Exp, scale=1 / 16.0).then_inc(ee_rd, 1)
                act.activation(absz[:, :, :], lmin[:, :, :], ACT.Exp, scale=1 / 16.0).then_inc(ee_rd, 1)
                ada_copy((17, 18, 20, 22)[hd], 3)
                if hd in (1, 2):
                    ada_copy((19, 21)[hd - 1], 3)
                for d in range(2):
                    act.wait_ge(ke_ps, 2 * hd + d + 1)
                    act.activation(kend[:, d, :, :].rearrange("p t n -> p (t n)"), ps[:, d, :],
                                   ACT.Copy).then_inc(ke_rd, 1)
            ada_copy(23, 3)

            act.wait_ge(o_ps, HEADS)
            for t in range(2):
                for hd in range(4):
                    src = ps[:, 4 + 2 * t + hd // 2, (hd % 2) * DV:(hd % 2 + 1) * DV]
                    step(act.activation(ebuf[:, 0, 0:DV], src, ACT.Square, accum_out=small[:, t * 4 + hd:t * 4 + hd + 1]))
            act.activation(small[:, 8:16], small[:, 0:8], ACT.Sqrt, scale=1.0 / DV, bias=eps_c[:, 0:1]).then_inc(og_std, 1)
            act.wait_ge(mod_rd, 4)
            for i in range(2):
                out_high(1, i)
            for k in range(4):
                act.wait_ge(og_ps, k + 1)
                act.activation(oT[:, 2 * k:2 * k + 2, :], ps[:, k, :].rearrange("p (a t) -> p a t", a=2),
                               ACT.Copy).then_inc(oT_rd, 1)
            for j in range(2):
                act.wait_ge(oT_rd, 2 * j + 2)
                mixed_high(1, j)
            gate_rows(8, 1)
            for i in range(2, OUT_STEPS):
                out_high(1, i)
            norm(3)
            router(1)
            experts(1)
            gate_rows(10, 1)
            for t in range(2):
                add_experts(1, t)

        @block.tensor
        def _(pe):
            def wait_slot(n):
                pe.wait_ge(slot_full[n % RING], 16 * (n // RING + 1))

            pe.wait_ge(s_const, 11)
            pe.wait_ge(s_rows, 16 * 12)
            pe.transpose(ps[:, 0, 0:68], rows_b[:, :], ident[0:68, 0:68])
            pe.transpose(ps[:, 0, 128:256], rows_a[:, :], ident[:, :]).then_inc(vec_ps, 1)

            def ada_slot(n, bank, parts=range(KD)):
                for k in parts:
                    mm = pe.matmul(ps[0:2, bank, :], cond[:, :, k], slot_kn(n)[:, k, :], start=(k == 0), stop=(k == KD - 1))
                    if k == KD - 1:
                        mm.then_inc(ada_ps, 1)

            def ada_wait(n, s):
                if s >= 2:
                    pe.wait_ge(ada_row, s if s >= 4 else s - 1)
                    if s % 4 == 0:
                        pe.wait_ge(mod_add, s // 4)
                wait_slot(n)

            def ada_turn(group, bank):
                pe.wait_ge(ada_row, 4 * group + 4)
                for q in range(4):
                    for j in range(4):
                        at = (4 * q + j) * 2
                        tp = pe.transpose(ps[:, bank, at:at + 2], mod_rows[group > 0][0:2, q, j * P:(j + 1) * P], ident[0:2, 0:2])
                tp.then_inc(ada_tp, 1)

            def norm(n):
                tiles = norm_tiles(n)
                pe.wait_ge(xn_rd, 4 * n + tiles)
                for k in range(KD):
                    if k >= 4:
                        s2 = tiles // 2
                        if k % 2 == 0:
                            pe.wait_ge(nT_act, 8 * n + ((k - 4) // 2 + 1) * s2)
                        else:
                            pe.wait_ge(nT_dve, 8 * n + ((k - 4) // 2 + 1) * s2)
                    for t in range(tiles):
                        tp = pe.transpose(ps[:, k % 4, t * P:(t + 1) * P], xn[:, t, k * P:(k + 1) * P], ident[:, :])
                    tp.then_inc(tp_ps, 1)
                pe.wait_ge(nT_act, 8 * n + 4 * (tiles // 2))
                pe.wait_ge(nT_dve, 8 * n + 4 * (tiles // 2))

            pe.wait_ge(cond_rd, 1)
            for s in range(ADA_EARLY):
                ada_wait(s, s)
                ada_slot(s, 6 + s % 2)
            ada_turn(0, 7)
            norm(0)

            def in_product(out_ap, layer, i, k, units, tokens, tokens_first):
                kk = k if (layer, i) == (0, EV_STEPS - 1) else k % 4
                width = units[2]
                w = [m[layer][i % 2][:, :].rearrange("p (k n) -> p k n", n=width)[:, kk, units[0]:units[1]]
                     for m in (in_hi, in_lo)]
                x = [n_hi[:, k, tokens], n_lo[layer][:, k, tokens]]
                for a, b in ((0, 0), (0, 1), (1, 0)):
                    sides = (x[a], w[b]) if tokens_first else (w[a], x[b])
                    mm = pe.matmul(out_ap, *sides, start=(k == 0 and (a, b) == (0, 0)),
                                   stop=(k == KD - 1 and (a, b) == (1, 0)))
                return mm

            for i in range(EV_STEPS - 1):
                grp, half = i // 2, i % 2
                pe.wait_ge(inlo_rd, in_step(0, i))
                for ct in range(4):
                    if i == 4:
                        pe.wait_ge(uc_rd, ct + 1)
                    for k in range(4 * half, 4 * half + 4):
                        if i < 2 and ct == 0 and k % 2 == 0:
                            pe.wait_ge(nlo_rd, k // 2 + 1)
                        units, tokens = (ct * P, (ct + 1) * P, 512), slice(0, 512)
                        if grp == 2:
                            units, tokens = (0, 512, 512), slice(ct * P, (ct + 1) * P)
                        mm = in_product(ps[:, (0, 4, 0)[grp] + ct, :], 0, i, k, units, tokens, grp == 2)
                    if half:
                        mm.then_inc(proj_ps, 1)
                    elif ct == 3:
                        mm.then_inc(even_ps, 1)
            pe.wait_ge(inlo_rd, in_step(0, EV_STEPS - 1))
            for t in range(4):
                pe.wait_ge(gelu_rd, t + 1)
                for k in range(KD):
                    mm = in_product(ps[:, 4 + t, 0:256], 0, EV_STEPS - 1, k, (0, 256, 256), slice(t * P, (t + 1) * P), True)
                mm.then_inc(proj_ps, 1)
            n = ADA_EARLY + EV_IN

            pe.wait_ge(s_bdl, 16 * 8)
            pe.wait_ge(qkv_rd, 12)
            for half in range(2):
                for u in range(4):
                    ct, d = 2 * half + u // 2, u % 2
                    for gate in range(2):
                        if half:
                            pe.wait_ge(sg_rd, 2 * u + gate + 1)
                        mm = pe.matmul(ps[:, 2 * u + gate, :], bd[:, gate * 8 + d * 4 + ct, :], uc[:, ct, :],
                                       start=True, stop=True)
                        mm.then_inc(rg_ps, 1)
            pe.wait_ge(sg_rd, 16)
            ada_wait(n, 4)
            ada_slot(n, 6)
            pe.wait_ge(qkn_rd, 1)
            for j in range(5):
                for t in range(4):
                    tp = pe.transpose(ps[:, j, t * P:(t + 1) * P], qk[:, t, j * P:(j + 1) * P], ident[:, :])
                tp.then_inc(qkt_ps, 1)
            for s in range(1, 4):
                ada_wait(n + s, 4 + s)
                ada_slot(n + s, 6)
            ada_turn(1, 6)
            n += 4

            pe.wait_ge(qkt_rd, 5)

            def scores(u):
                i, kv = u // 2, u % 2
                a, b = (0, 512) if u < 4 else (256, 512)
                if u > 0:
                    pe.wait_ge(sc_rd, u)
                rows = slice(kv * 64, kv * 64 + 64)
                for g in range(4):
                    mm = pe.matmul(ps[:, g, 0:b - a], qkT[rows, g, i * P:(i + 1) * P], qkT[rows, 4, a:b],
                                   start=True, stop=True)
                mm.then_inc(sc_ps, 1)

            scores(0)
            for u in range(8):
                if u < 7:
                    scores(u + 1)
                if u < 4:
                    ada_wait(n + u, 8 + u)
                    ada_slot(n + u, 6)
                else:
                    pe.wait_ge(dg_rd, 1)
                    if u == 4:
                        pe.wait_ge(mod_add, 3)
                    else:
                        pe.wait_ge(gr_rd, u - 4)
                    pe.matmul(ps[:, 6, :], ones[:, :], diag[:, u // 2 - 2, 4 * (u % 2):4 * (u % 2) + 4, :],
                              start=True, stop=True).then_inc(gr_ps, 1)
                if u == 3:
                    ada_turn(2, 6)
                kv = u % 2
                tiles = 4 if u < 4 else 2
                pe.wait_ge(pn_rd, u + 1)
                for s in range(tiles):
                    m = (4 * u if u < 4 else 16 + 2 * (u - 4)) + s
                    if m >= 2:
                        pe.wait_ge(pt_rd, m - 1)
                    for g in range(4):
                        tp = pe.transpose(ps[:, 4 + m % 2, g * P:(g + 1) * P], prob[:, u % 2, g, s * P:(s + 1) * P],
                                          ident[:, :])
                    tp.then_inc(pt_ps, 1)
                if u > 0:
                    pe.wait_ge(pv_rd, 2 * u)
                for s in range(tiles):
                    m = (4 * u if u < 4 else 16 + 2 * (u - 4)) + s
                    pe.wait_ge(pt_rd, m + 1)
                    vt = s if u < 4 else 2 + s
                    mm = pe.matmul(ps[0:64, 7, :], v_sb[:, vt, kv * 64:kv * 64 + 64], probT[:, s, :],
                                   start=(s == 0), stop=(s == tiles - 1))
                mm.then_inc(pv_ps, 1)

            def gate_rows(count, streams):
                pe.wait_ge(dg_rd, count)
                for s in range(streams):
                    for half in range(2):
                        pe.matmul(ps[:, 2 * s + half, :], ones[:, :], diag[:, s, 4 * half:4 * half + 4, :],
                                  start=True, stop=True).then_inc(gr_ps, 1)

            pe.wait_ge(pv_rd, 16)
            pe.wait_ge(pt_rd, 24)
            n += 4
            def out_product(layer, bank):
                for i in range(OUT_STEPS):
                    pe.wait_ge(outlo_rd, OUT_STEPS * layer + i + 1)
                    whi, wlo = (m[layer][i % 2][:, :].rearrange("p (k n) -> p k n", k=2) for m in (out_hi, out_lo))
                    if layer == 0:
                        pe.wait_ge(mlo_rd, (1, 1, 2, 3)[i])
                    else:
                        pe.wait_ge(mlo_rd, 4 + i // 2)
                    for m in range((8, 4)[layer]):
                        tokens = slice(m // 2 * P, m // 2 * P + P)
                        cols = slice(m % 2 * 512, m % 2 * 512 + 512)
                        for q in range(2):
                            k = 2 * i + q
                            xhi, xlo = m_hi[layer][:, k, tokens], m_lo[layer][k // 4][:, k % 4, tokens]
                            pe.matmul(ps[:, bank + m, :], xhi, whi[:, q, cols], start=(k == 0), stop=False)
                            pe.matmul(ps[:, bank + m, :], xhi, wlo[:, q, cols], start=False, stop=False)
                            mm = pe.matmul(ps[:, bank + m, :], xlo, whi[:, q, cols], start=False, stop=(k == KD - 1))
                        if i == OUT_STEPS - 1:
                            mm.then_inc(y_ps, 1)
                    if i < OUT_STEPS - 1:
                        mm.then_inc(outstep_ps, 1)

            pe.wait_ge(gr_rd, 4)
            pe.wait_ge(mod_rd, 2)
            out_product(0, 0)
            n += 2

            def router(layer):
                tiles = (4, 2)[layer]
                for t in range(tiles):
                    for k in range(KD):
                        mm = pe.matmul(ps[:, 4, t * 16:(t + 1) * 16], nT[:, k, t * P:(t + 1) * P], rw[:, k, :],
                                       start=(k == 0), stop=(k == KD - 1))
                mm.then_inc(rt_ps, 1)
                pe.wait_ge(rt_sg, layer + 1)

            def experts(layer):
                tiles = (4, 2)[layer]
                for k in range(KD):
                    if k >= 4:
                        pe.wait_ge(xlo_rd, KD * layer + k - 3)
                    for t in range(tiles):
                        tp = pe.transpose(ps[:, k % 4, t * P:(t + 1) * P], nT[:, k, t * P:(t + 1) * P], ident[:, :])
                    tp.then_inc(back_ps, 1)
                pe.wait_ge(rt_rd, 2 * layer + 1)
                for t in range(tiles):
                    for b in range(t + 1):
                        pe.matmul(ps[:, 5, t * 16:(t + 1) * 16], ones[:, :] if b < t else before[:, :], routed[:, b, :],
                                  start=(b == 0), stop=(b == t))
                for b in range(tiles):
                    mm = pe.matmul(ps[:, 5, 64:80], ones[:, :], routed[:, b, :], start=(b == 0), stop=(b == tiles - 1))
                mm.then_inc(rank_ps, 1)
                pe.wait_ge(xlo_rd, KD * layer + KD)

                def first(e):
                    return e + layer * N_EXPERTS

                def gather(e, c):
                    if c == 0:
                        pe.wait_ge(pick_rd, first(e) + 1)
                    for t in range(tiles):
                        for part, src in enumerate((x_hi, x_lo)):
                            mm = pe.matmul(ps[:, c, :], pick[:, t, :], src[:, t, c * 512:(c + 1) * 512],
                                           start=(t == 0 and part == 0), stop=(t == tiles - 1 and part == 1))
                    mm.then_inc(pick_ps, 1)

                def turn(e, c):
                    pe.wait_ge(row_rd, first(e) * 2 + (c + 1))
                    for k in range(4):
                        tp = pe.transpose(ps[:, (4, 0)[c], k * P:(k + 1) * P], rows_e[:, (4 * c + k) * P:(4 * c + k + 1) * P],
                                          ident[:, :])
                    tp.then_inc(xt_ps, 1)

                def body(e, j, last):
                    n0 = first(e) * HALVES
                    for m in range(2):
                        for half in range(2):
                            if m == 0:
                                pe.wait_ge(xgh_rd, first(e) * 2 + (half + 1))
                                pe.wait_ge(xgl_rd, first(e) * 2 + (half + 1))
                            i = 2 * m + half
                            pe.wait_ge(wlo_rd, n0 + i + 1)
                            b = (j * HALVES + i) % SPLITS
                            whi = w_hi[:, b, :].rearrange("p (k n) -> p k n", k=4)
                            wlo = w_lo[:, b, :].rearrange("p (k n) -> p k n", k=4)
                            for q in range(4):
                                k = 4 * half + q
                                out_ap = ps[:, 2 + m, :]
                                pe.matmul(out_ap, xg_hi[:, k, :], whi[:, q, :], start=(k == 0), stop=False)
                                pe.matmul(out_ap, xg_hi[:, k, :], wlo[:, q, :], start=False, stop=False)
                                mm = pe.matmul(out_ap, xg_lo[:, k, :], whi[:, q, :], start=False, stop=(k == KD - 1))
                            mm.then_inc(w_ps, 1)
                    if not last:
                        gather(e + 1, 0)
                    pe.wait_ge(glu_rd, first(e) + 1)
                    for f in range(FT):
                        tp = pe.transpose(ps[:, 7, f * P:(f + 1) * P], glu[:, f * P:(f + 1) * P], ident[:, :])
                    tp.then_inc(gt_ps, 1)
                    if not last:
                        gather(e + 1, 1)
                        turn(e + 1, 0)
                    pe.wait_ge(glo_rd, first(e) + 1)
                    if not (isinstance(e, int) and first(e) == 0):
                        pe.wait_ge(y_sbrd, first(e))
                    for half in range(2):
                        i = 4 + half
                        pe.wait_ge(wlo_rd, n0 + i + 1)
                        b = (j * HALVES + i) % SPLITS
                        whi = w_hi[:, b, :].rearrange("p (k n) -> p k n", k=2)
                        wlo = w_lo[:, b, :].rearrange("p (k n) -> p k n", k=2)
                        for q in range(2):
                            f = 2 * half + q
                            for c in range(2):
                                cols = slice(c * 512, (c + 1) * 512)
                                out_ap = ps[:, 5 + c, :]
                                pe.matmul(out_ap, glu_hi[:, f, :], whi[:, q, cols], start=(f == 0), stop=False)
                                pe.matmul(out_ap, glu_hi[:, f, :], wlo[:, q, cols], start=False, stop=False)
                                mm = pe.matmul(out_ap, glu_lo[:, f, :], whi[:, q, cols], start=False, stop=(f == FT - 1))
                        mm.then_inc(w_ps, 1)
                        if half == 0 and not last:
                            turn(e + 1, 1)

                for c in range(2):
                    gather(0, c)
                for c in range(2):
                    turn(0, c)
                body(0, 0, False)
                with pe.Fori(0, N_EXPERTS // 2 - 1) as i:
                    body(i * 2 + 1, 1, False)
                    body(i * 2 + 2, 0, False)
                body(N_EXPERTS - 1, 1, True)

                most = pe.value_load(count_i[0:1, 0:1], min_val=0, max_val=CAPACITY)
                with pe.If(most > P):
                    pe.wait_ge(y_sbrd, (layer + 1) * N_EXPERTS)
                    pe.sem_inc(more_pe[layer], 1)
                    with pe.Fori(0, ((4, 2)[layer] - 1) * N_EXPERTS) as g:
                        pe.wait_ge(more_dve[layer], g * 5 + 1)
                        for k in range(KD):
                            for part, src in enumerate((x_hi, x_lo)):
                                for t in range(tiles):
                                    mm = pe.matmul(ps[:, k // 4, (k % 4) * P:(k % 4 + 1) * P], src[:, t, k * P:(k + 1) * P],
                                                   pick[:, t, :], start=(part == 0 and t == 0),
                                                   stop=(part == 1 and t == tiles - 1))
                        mm.then_inc(more_pe[layer], 1)
                        pe.wait_ge(more_dve[layer], g * 5 + 2)
                        pe.wait_ge(more_ld[layer], g * 48 + 48)
                        for m in range(2):
                            w = ring[:, expert_slot(layer, m)[0], :].rearrange("p (k n) -> p k n", k=8)
                            for k in range(KD):
                                mm = pe.matmul(ps[:, 2 + m, :], xg_f[:, k, :], w[:, k, :], start=(k == 0), stop=(k == KD - 1))
                        mm.then_inc(more_pe[layer], 1)
                        pe.wait_ge(more_dve[layer], g * 5 + 3)
                        for f in range(FT):
                            tp = pe.transpose(ps[:, 7, f * P:(f + 1) * P], glu[:, f * P:(f + 1) * P], ident[:, :])
                        tp.then_inc(more_pe[layer], 1)
                        pe.wait_ge(more_dve[layer], g * 5 + 4)
                        w = ring[:, expert_slot(layer, 2)[0], :].rearrange("p (k n) -> p k n", k=4)
                        for c in range(2):
                            for f in range(FT):
                                mm = pe.matmul(ps[:, 5 + c, :], glu_t[:, f, :], w[:, f, c * 512:(c + 1) * 512],
                                               start=(f == 0), stop=(f == FT - 1))
                        mm.then_inc(more_pe[layer], 1)

            pe.wait_ge(gr_rd, 4)
            norm(1)
            router(0)
            experts(0)
            n = L1_BASE
            for s in range(4):
                ada_wait(n + s, 12 + s)
                if s == 0:
                    pe.wait_ge(y_sbrd, N_EXPERTS)
                ada_slot(n + s, 7)
                if s == 0:
                    gate_rows(2, 2)
            n += ADA_EARLY
            ada_turn(3, 7)
            pe.wait_ge(gr_rd, 8)
            norm(2)

            for i in range(OD_STEPS):
                grp, half = i // 2, i % 2
                pe.wait_ge(inlo_rd, in_step(1, i))
                count = 2 if grp >= 4 else 4
                for u in range(count):
                    if half == 0:
                        if grp == 2:
                            pe.wait_ge(p1_act, u + 1)
                        elif grp == 3:
                            pe.wait_ge(p1_dve, u + 1)
                        elif grp == 4:
                            pe.wait_ge(p1_dve, 12)
                    for k in range(4 * half, 4 * half + 4):
                        if i < 2 and u == 0 and k % 2 == 0:
                            pe.wait_ge(nlo_rd, 4 + k // 2 + 1)
                        units, tokens = (0, 512, 512), slice(u * P, (u + 1) * P)
                        if grp < 2:
                            units, tokens = (u * P, (u + 1) * P, 512), slice(0, (256, 512)[grp])
                        bank = (u, 4 + u, u, 4 + u, 4 + 2 * u, 5 + 2 * u)[grp]
                        mm = in_product(ps[:, bank, 0:256] if grp == 0 else ps[:, bank, :], 1, i, k, units, tokens, grp >= 2)
                    if half:
                        mm.then_inc(p1_ps, 1)
                    elif u == count - 1:
                        mm.then_inc(even_ps, 1)
            n += OD_IN - 1
            pe.wait_ge(gin_rd, 2)
            for k in range(KD):
                mm = pe.matmul(ps[0:48, 0, :], gate_in[:, k, :], nT[:, k, :], start=(k == 0), stop=(k == KD - 1))
            mm.then_inc(p1_ps, 1)
            n += 1
            pe.wait_ge(p1_act, 10)

            pe.wait_ge(s_gup, 32)
            for hd in range(HEADS):
                bank = (0, 4, 6, 0)[hd]
                if hd == 3:
                    pe.wait_ge(z_rd, 2)
                for d in range(2):
                    part = slice(32 * d, 32 * d + 16)
                    mm = pe.matmul(ps[:, bank + d, :], gate_up[part, hd * P:(hd + 1) * P], aT[part, :],
                                   start=True, stop=True)
                mm.then_inc(z_ps, 1)
            for s in (16, 17):
                ada_wait(n + s - 16, s)
                ada_slot(n + s - 16, 3)
            pe.wait_ge(z_rd, 2 * HEADS)
            for hd in range(HEADS):
                if hd in (1, 2):
                    s = (19, 21)[hd - 1]
                    ada_wait(n + s - 16, s)
                    ada_slot(n + s - 16, 3)
                if hd == 1:
                    ada_turn(4, 3)
                pe.wait_ge(qd_rd, 2 * hd + 2)
                if hd:
                    pe.wait_ge(att_rd, hd)
                for d in range(2):
                    for t in range(2):
                        mm = pe.matmul(ps[:, 2, (2 * d + t) * P:(2 * d + t + 1) * P], kinc[:, d, t * P:(t + 1) * P],
                                       qdec[:, d, t * P:(t + 1) * P], start=True, stop=True)
                mm.then_inc(at_ps, 1)
                pe.wait_ge(ee_us, hd + 1)
                if hd:
                    pe.wait_ge(st_rd, 14 * hd)
                for d in range(2):
                    for t in range(4):
                        tp = pe.transpose(ps[:, d, t * P:(t + 1) * P], kendT[:, d, t * P:(t + 1) * P], ident[:, :])
                    tp.then_inc(ke_ps, 1)

                def head_out(t):
                    return ps[:, 4 + 2 * t + hd // 2, (hd % 2) * DV:(hd % 2 + 1) * DV]

                pe.wait_ge(att_rd, hd + 1)
                for t in range(2):
                    for d in range(2):
                        pe.matmul(head_out(t), att[:, d, t, :], v1[:, t, hd * DV:(hd + 1) * DV],
                                  start=(d == 0), stop=False, skip_group_check=True)
                pe.wait_ge(ke_rd, 2 * hd + 2)
                for q in range(8):
                    for d in range(2):
                        ch = (4 + q if q < 4 else q - 4) if d == 0 else 7 - q
                        t, lo = ch // 2, (ch % 2) * CHUNK
                        if q:
                            pe.wait_ge(st_rd, 14 * hd + 2 * (q - 1) + d + 1)
                        if q >= 4:
                            mm = pe.matmul(head_out(t)[lo:lo + CHUNK, :], qdec[:, d, ch * CHUNK:(ch + 1) * CHUNK],
                                           state[:, (q - 1) % 2, d, :], start=False, stop=(q >= 6),
                                           skip_group_check=True)
                        if q < 7:
                            pe.matmul(ps[:, d, 0:DV], kend[lo:lo + CHUNK, d, t, :],
                                      v1[lo:lo + CHUNK, t, hd * DV:(hd + 1) * DV],
                                      start=True, stop=True).then_inc(ds_ps, 1)
                    s = (18, 20, 22, 23)[hd]
                    if q == 0:
                        ada_wait(n + s - 16, s)
                    ada_slot(n + s - 16, 3, (q,))
                mm.then_inc(o_ps, 1)
            ada_turn(5, 3)

            n += ADA_LATE
            pe.wait_ge(og_rd, 2)
            pe.wait_ge(mod_rd, 4)
            for k in range(4):
                for a in range(2):
                    for t in range(2):
                        tp = pe.transpose(ps[:, k, a * 256 + t * P:a * 256 + (t + 1) * P],
                                          og[:, t, (2 * k + a) * P:(2 * k + a + 1) * P], ident[:, :])
                tp.then_inc(og_ps, 1)
            pe.wait_ge(oT_rd, 4)
            gate_rows(3, 1)
            out_product(1, 4)
            pe.wait_ge(gr_rd, 10)
            norm(3)
            router(1)
            experts(1)
            gate_rows(4, 1)

        @block.vector
        def _(dve):
            step = Chain(dve, dve_step)

            dve.wait_ge(vec_ps, 1)
            dve.tensor_copy(vec_b[:, :], ps[:, 0, 0:68]).then_inc(vec_rd, 1)
            dve.tensor_copy(vec_a[:, :], ps[:, 0, 128:256]).then_inc(vec_rd, 1)
            dve.wait_ge(vec_rd, 2)

            def n_low(layer, j):
                dve.wait_ge(nhi_rd, 4 * layer + j + 1)
                ks = slice(2 * j, 2 * j + 2)
                dve.tensor_tensor(n_lo[layer][:, ks, :], nT[:, ks, :], n_hi[:, ks, :].bitcast(F32),
                                  ALU.subtract).then_inc(nlo_rd, 1)

            def in_low(layer, i):
                dve.wait_ge(inhi_rd, in_step(layer, i))
                dve.tensor_tensor(in_lo[layer][i % 2][:, :], in_weights(layer, i), in_hi[layer][i % 2][:, :].bitcast(F32),
                                  ALU.subtract).then_inc(inlo_rd, 1)

            def normed(n):
                tiles = norm_tiles(n)
                dve.wait_ge(std_rd, n + 1)
                dve.reciprocal(rstd[:, n, 0:tiles], ssq[:, n, 4:4 + tiles]).then_inc(rstd_rd, 1)
                dve.wait_ge(rstd_rd, n + 1)
                for t in range(1, tiles, 2):
                    dve.tensor_scalar(xn[:, t, :], h[:, t, :], rstd[:, n, t:t + 1], None, ALU.mult).then_inc(xn_rd, 1)

            def norm(n):
                tiles = norm_tiles(n)
                if n:
                    normed(n)
                if n == 2:
                    for i in range(2):
                        in_low(1, i)
                dve.wait_ge(mod_rd, (1, 2, 3, 4)[n])
                for k in range(1, KD, 2):
                    dve.wait_ge(tp_ps, KD * n + k + 1)
                    for s in range(tiles // 2):
                        dve.tensor_scalar(nT[:, k, s * 256:(s + 1) * 256], ps[:, k % 4, s * 256:(s + 1) * 256],
                                          affine[:, n, k, s:s + 1],
                                          mod[:, n // 2, (0 if n % 2 == 0 else 24) + k, s:s + 1],
                                          ALU.mult, ALU.add).then_inc(nT_dve, 1)
                    if n == 2 and k > 1:
                        n_low(1, k // 2 - 1)
                if n == 0:
                    for j in range(3):
                        n_low(0, j)
                if n % 2 == 0:
                    n_low(n // 2, 3)

            def ada(group, bank):
                layer, third = group // 3, group % 3
                dve.wait_ge(ada_tp, group + 1)
                bias = vec_a[:, 16 * group:16 * (group + 1)].unsqueeze(2).to_broadcast([P, 16, 2])
                dve.tensor_tensor(mod[:, layer, 16 * third:16 * (third + 1), :],
                                  ps[:, bank, 0:32].rearrange("p (j s) -> p j s", s=2), bias, ALU.add).then_inc(mod_add, 1)
                if third != 1:
                    part = third // 2
                    dve.wait_ge(mod_add, group + 1)
                    gain_at = 96 + 16 * part + 8 * layer
                    gain = vec_a[:, gain_at:gain_at + 8].unsqueeze(2).to_broadcast([P, 8, 2])
                    dve.scalar_tensor_tensor(affine[:, 2 * layer + part, :, :],
                                             mod[:, layer, 8 + 24 * part:16 + 24 * part, :], 1.0, gain,
                                             ALU.add, ALU.mult).then_inc(mod_rd, 1)

            for s in range(ADA_EARLY):
                if s == 1:
                    normed(0)
                elif s == 3:
                    for i in range(2):
                        in_low(0, i)
                dve.wait_ge(ada_ps, s + 1)
                dve.tensor_copy(mod_rows[0][0:2, s, :], ps[0:2, 6 + s % 2, :]).then_inc(ada_row, 1)
            ada(0, 7)
            norm(0)

            lam = vec_b[:, 52:60]
            dve.scalar_tensor_tensor(sp[:, 0, :], lam, -1.0, lam, ALU.mult, ALU.max).then_inc(sp_x, 1)
            dve.wait_ge(sp_e, 1)
            dve.tensor_scalar(sp[:, 2, :], sp[:, 1, :], 1.0, None, ALU.add).then_inc(sp_x, 1)
            dve.wait_ge(sp_x, 2)
            step(dve.tensor_scalar(sp[:, 4, :], sp[:, 2, :], 1.0, None, ALU.subtract))
            step(dve.tensor_scalar(sp[:, 5, :], sp[:, 4, :], 0.0, None, ALU.is_equal))
            step(dve.tensor_tensor(sp[:, 4, :], sp[:, 4, :], sp[:, 5, :], ALU.add))
            dve.wait_ge(sp_l, 1)
            step(dve.tensor_tensor(sp[:, 3, :], sp[:, 3, :], sp[:, 5, :], ALU.add))
            step(dve.reciprocal(sp[:, 5, :], sp[:, 4, :]))
            step(dve.tensor_tensor(sp[:, 3, :], sp[:, 3, :], sp[:, 5, :], ALU.mult))
            step(dve.tensor_tensor(sp[:, 3, :], sp[:, 3, :], sp[:, 1, :], ALU.mult))
            step(dve.tensor_scalar(sp[:, 4, :], lam, -1.0, 0.0, ALU.mult, ALU.max))
            step(dve.tensor_tensor(sp[:, 3, :], sp[:, 3, :], sp[:, 4, :], ALU.add))
            dve.tensor_scalar(sp[:, 6, :], sp[:, 3, :], -8.0, None, ALU.mult).then_inc(sp_rd, 1)
            dve.tensor_scalar(sp[:, 7, :], sp[:, 3, :], 8.0, None, ALU.mult).then_inc(sp_rd, 1)

            in_low(0, 2)
            for ct in range(4):
                if ct == 2:
                    in_low(0, 3)
                dve.wait_ge(proj_ps, ct + 1)
                u2 = ps[:, ct, :].rearrange("p (s t) -> p s t", s=2)
                y2 = uc[:, ct, :].rearrange("p (s t) -> p s t", s=2)

                def tap(j):
                    return vec_b[:, 16 + 4 * j + ct:17 + 4 * j + ct]

                step(dve.tensor_scalar(y2, u2, tap(1), vec_b[:, 32 + ct:33 + ct], ALU.mult, ALU.add))
                step(dve.scalar_tensor_tensor(y2[:, :, 1:256], u2[:, :, 0:255], tap(0), y2[:, :, 1:256], ALU.mult, ALU.add))
                step(dve.scalar_tensor_tensor(y2[:, :, 0:255], u2[:, :, 1:256], tap(2), y2[:, :, 0:255], ALU.mult, ALU.add))
                dve.scalar_tensor_tensor(y2[:, :, 0:254], u2[:, :, 2:256], tap(3), y2[:, :, 0:254],
                                         ALU.mult, ALU.add).then_inc(uc_rd, 1)

            for i in range(4, EV_STEPS):
                in_low(0, i)
            dve.wait_ge(qkv_rd, 12)
            dve.wait_ge(s_small, 16 * 8)
            flat = region_q[:, :]
            qsq = region_t[:, :]
            heads = flat.rearrange("p (n d) -> p n d", d=64)
            step(dve.tensor_tensor(qsq, flat, flat, ALU.mult))
            dve.tensor_reduce(qk_ss[:, 0, :], qsq.rearrange("p (n d) -> p n d", d=64), AX_X, ALU.add).then_inc(qkss, 1)
            dve.wait_ge(qkstd, 1)
            step(dve.reciprocal(qk_ss[:, 2, :], qk_ss[:, 1, :]))
            step(dve.tensor_tensor(heads, heads, qk_ss[:, 2, :].unsqueeze(2).to_broadcast([P, 40, 64]), ALU.mult))
            for w, (a, b) in enumerate(((0, 512), (512, 640))):
                part = qk[:, :, a:b].rearrange("p t (n d) -> p t n d", d=64)
                gain = g_qk[:, w, :].unsqueeze(1).unsqueeze(1).to_broadcast([P, 4, (b - a) // 64, 64])
                step.add(dve.tensor_tensor(part, part, gain, ALU.mult))
            step.wait()
            for t in range(2):
                hv = qk[:, t, :].rearrange("p (n a x f) -> p n a x f", n=10, a=2, x=2)
                x1, x2 = hv[:, :, :, 0, :], hv[:, :, :, 1, :]
                shape = [P, 10, 2, 16]
                cos = rope[:, 0, t, :].rearrange("p (a f) -> p a f", a=2).unsqueeze(1).to_broadcast(shape)
                sin = rope[:, 1, t, :].rearrange("p (a f) -> p a f", a=2).unsqueeze(1).to_broadcast(shape)
                scratch = region_t[:, 0:1280].rearrange("p (w n a f) -> p w n a f", w=4, n=10, a=2)
                step.add(dve.tensor_tensor(scratch[:, 0], x1, cos, ALU.mult))
                step.add(dve.tensor_tensor(scratch[:, 1], x2, sin, ALU.mult))
                step.add(dve.tensor_tensor(scratch[:, 2], x2, cos, ALU.mult))
                step(dve.tensor_tensor(scratch[:, 3], x1, sin, ALU.mult))
                step.add(dve.tensor_tensor(x1, scratch[:, 0], scratch[:, 1], ALU.subtract))
                step(dve.tensor_tensor(x2, scratch[:, 2], scratch[:, 3], ALU.add))
            dve.tensor_scalar(sink[:, 1, :], sink[:, 0, :], -1.0, None, ALU.mult).then_inc(qkn_rd, 1)
            dve.wait_ge(qkn_rd, 1)

            for half in range(2):
                for u in range(4):
                    ct = 2 * half + u // 2
                    dve.wait_ge(at_rd, 8 * half + 2 * u + 2)
                    step.add(dve.tensor_tensor(tmp[:, u % 2, :], rg_a[half][:, u, :], rg_a[half][:, u, :], ALU.mult))
                    step(dve.tensor_tensor(rg_i[half][:, u, :], rg_i[half][:, u, :], uc[:, ct, :], ALU.mult))
                    dve.scalar_tensor_tensor(rg_r[half][:, u, :], tmp[:, u % 2, :], 1.0, rg_r[half][:, u, :],
                                             ALU.add, ALU.mult).then_inc(va_rd, 1)
            dve.wait_ge(va_rd, 8)
            for half in range(2):
                dve.wait_ge(sq_rd, half + 1)
                step(dve.tensor_tensor(rg_i[half], rg_i[half], rg_r[half], ALU.mult))
                for u in range(4):
                    a, b, o = rg_a[half][:, u, :], rg_i[half][:, u, :], rg_r[half][:, u, :]
                    if u % 2 == 0:
                        step(dve.tensor_tensor_scan(o[:, 256:512], a[:, 256:512], b[:, 256:512], 0.0, ALU.mult, ALU.add))
                        step(dve.tensor_tensor_scan(o[:, 0:256], a[:, 0:256], b[:, 0:256], o[:, 511:512], ALU.mult, ALU.add))
                    else:
                        step(dve.tensor_tensor_scan(o[:, ::-1], a[:, ::-1], b[:, ::-1], 0.0, ALU.mult, ALU.add))
                for c2 in range(2):
                    ct = 2 * half + c2
                    dve.wait_ge(gelu_rd, ct + 1)
                    step(dve.tensor_tensor(tmp[:, 0, :], rg_r[half][:, 2 * c2, :], rg_r[half][:, 2 * c2 + 1, :], ALU.add))
                    ins = dve.tensor_tensor(mixT[:, ct, :], tmp[:, 0, :], gg[:, ct, :], ALU.mult)
                    if c2 == 0:
                        step(ins)
                    else:
                        ins.then_inc(half_rd, 1)
                        dve.wait_ge(half_rd, half + 1)


            ada(1, 6)

            def diagonals(layer, m, streams):
                for s in range(streams):
                    ins = dve.tensor_tensor(diag[:, s, :, :], ident[:, :].unsqueeze(1).to_broadcast([P, 8, P]),
                                            mod[:, layer, 8 * m:8 * m + 8, s:s + 1].to_broadcast([P, 8, P]), ALU.mult)
                    if s == streams - 1:
                        step(ins)
                    else:
                        step.add(ins)
                dve.tensor_copy(small[0:1, 32:33], ident[0:1, 0:1]).then_inc(dg_rd, 1)

            def mixed_lows(layer, j):
                dve.wait_ge(mhi_rd, 3 * layer + j + 1)
                ks = mixed_ks(layer, j)
                dve.tensor_tensor(mixed_low(layer, ks), (mixT, oT)[layer][:, ks, :], m_hi[layer][:, ks, :].bitcast(F32),
                                  ALU.subtract).then_inc(mlo_rd, 1)

            def out_lows(layer, i):
                dve.wait_ge(outhi_rd, OUT_STEPS * layer + i + 1)
                dve.tensor_tensor(out_lo[layer][i % 2][:, :], out_weights(layer, i), out_hi[layer][i % 2][:, :].bitcast(F32),
                                  ALU.subtract).then_inc(outlo_rd, 1)

            def scaled_scores(u):
                i, kv = u // 2, u % 2
                keys = 512 if u < 4 else 256
                b = u % 2
                dve.wait_ge(sc_ps, u + 1)
                if u >= 2:
                    dve.wait_ge(pv_ps, u - 1)
                if u < 4:
                    step(dve.tensor_scalar(prob[:, b, :, :], ps[:, 0:4, :], ATT_SCALE, None, ALU.mult))
                    far = prob[:, b, :, (1 - i) * P:(2 - i) * P]
                    ins = dve.tensor_tensor(far, far, wmask[:, i, :].unsqueeze(1).to_broadcast([P, 4, P]), ALU.add)
                else:
                    ins = dve.tensor_scalar(prob[:, b, :, 0:256], ps[:, 0:4, 0:256], ATT_SCALE, None, ALU.mult)
                ins.then_inc(sc_rd, 1)
                dve.wait_ge(sc_rd, u + 1)
                step(dve.tensor_reduce(soft[:, b, 0, :], prob[:, b, :, 0:keys], AX_X, ALU.max))
                step(dve.scalar_tensor_tensor(soft[:, b, 1, :], soft[:, b, 0, :], -1.0, sink[:, 1, kv * 4:kv * 4 + 4],
                                              ALU.mult, ALU.min))
                dve.tensor_tensor(soft[:, b, 2, :], soft[:, b, 1, :], sink[:, 0, kv * 4:kv * 4 + 4],
                                  ALU.add).then_inc(nm_rd, 1)

            scaled_scores(0)
            for u in range(8):
                i, kv = u // 2, u % 2
                keys = 512 if u < 4 else 256
                b = u % 2
                dve.wait_ge(ex_rd, 5 * u + 5)
                step(dve.tensor_tensor(soft[:, b, 3, :], soft[:, b, 3, :], soft[:, b, 2, :], ALU.add))
                step(dve.reciprocal(soft[:, b, 4, :], soft[:, b, 3, :]))
                dve.tensor_tensor(prob[:, b, :, 0:keys], prob[:, b, :, 0:keys],
                                  soft[:, b, 4, :].unsqueeze(2).to_broadcast([P, 4, keys]), ALU.mult).then_inc(pn_rd, 1)
                if u < 7:
                    scaled_scores(u + 1)
                if u == 3:
                    ada(2, 6)
                    diagonals(0, 2, 2)
                elif u == 5:
                    mixed_lows(0, 0)
                elif u == 7:
                    out_lows(0, 0)
                dve.wait_ge(pv_ps, u + 1)
                for odd in range(2):
                    src = ps[0:64, 7, :].rearrange("p (a o t) -> p a o t", a=2, o=2)[:, :, odd, :]
                    dve.tensor_copy(mixT[64 * odd:64 * odd + 64, 4 + 2 * kv:6 + 2 * kv, i * P:(i + 1) * P],
                                    src).then_inc(pv_rd, 1)

            def residual(layer, products, rows):
                tiles = (4, 2)[layer]
                dve.wait_ge(gr_rd, rows)
                for t in range(tiles):
                    for half in range(2):
                        m = 2 * t + half
                        dve.wait_ge(y_ps, products + m + 1)
                        bank = 4 * layer + m
                        cols = slice(half * 512, half * 512 + 512)
                        if m >= 1:
                            step.wait()
                        dve.tensor_tensor(tmp[:, m % 2, :], ps[:, bank, :], gate_row[:, t // 2, cols],
                                          ALU.mult).then_inc(y_rd, 1)
                        dve.wait_ge(y_rd, products + m + 1)
                        ins = dve.tensor_tensor(h[:, t, cols], h[:, t, cols], tmp[:, m % 2, :], ALU.add)
                        if half == 0:
                            step.add(ins)
                        else:
                            ins.then_inc(h_rd, 1)

            for j in range(1, 3):
                mixed_lows(0, j)
            for i in range(1, OUT_STEPS):
                out_lows(0, i)
            residual(0, 0, 4)
            norm(1)

            def router(layer):
                tiles = (4, 2)[layer]
                G = 4 * tiles
                dve.wait_ge(rt_sg, layer + 1)
                score = rt[:, 0, 0:4 * G]
                sel = rt[:, 1, 0:4 * G]
                s3 = score.rearrange("p (t e) -> p t e", t=tiles)
                step(dve.tensor_tensor(sel.rearrange("p (t e) -> p t e", t=tiles), s3,
                                       bias_r[:, :].unsqueeze(1).to_broadcast([P, tiles, 16]), ALU.add))

                def rank(values, n, res):
                    v = values.rearrange("p (n e) -> p n e", e=4)
                    res3 = res.rearrange("p (n e) -> p n e", e=4)
                    shape = [P, n, 4, 4]
                    other, me = v.unsqueeze(2).to_broadcast(shape), v.unsqueeze(3).to_broadcast(shape)
                    over, same = (cmp[:, w, 0:16 * n].rearrange("p (n e o) -> p n e o", e=4, o=4) for w in range(2))
                    earlier = first_of[:, :, :].unsqueeze(1).to_broadcast(shape)
                    step.add(dve.tensor_tensor(over, other, me, ALU.is_gt))
                    step(dve.tensor_tensor(same, other, me, ALU.is_equal))
                    step(dve.tensor_tensor(same, same, earlier, ALU.mult))
                    step(dve.tensor_tensor(over, over, same, ALU.add))
                    step(dve.tensor_reduce(res3, over, AX_X, ALU.add))

                r4 = rt[:, 2, 0:4 * G]
                rank(sel, G, r4)
                top2 = rt[:, 3, 0:4 * G]
                step(dve.tensor_scalar(top2, r4, 2.0, None, ALU.is_lt))
                both = rt[:, 4, 0:4 * G]
                step(dve.tensor_tensor(both, top2, sel, ALU.mult))
                gs = rt[:, 5, 0:G]
                step(dve.tensor_reduce(gs, both.rearrange("p (n e) -> p n e", e=4), AX_X, ALU.add))
                gr = rt[:, 6, 0:G]
                rank(gs, tiles, gr)
                best = rt[:, 7, 0:G]
                step(dve.tensor_scalar(best, gr, 0.0, None, ALU.is_equal))
                mine = routed[:, 0:tiles, :].rearrange("p t e -> p (t e)")
                dve.tensor_tensor(mine.rearrange("p (n e) -> p n e", e=4), top2.rearrange("p (n e) -> p n e", e=4),
                                  best.unsqueeze(2).to_broadcast([P, G, 4]), ALU.mult).then_inc(rt_rd, 1)
                dve.wait_ge(rt_rd, 2 * layer + 1)
                step(dve.tensor_tensor(both, mine, score, ALU.mult))
                tot = rt[:, 8, 0:tiles]
                step(dve.tensor_reduce(tot, both.rearrange("p (t e) -> p t e", t=tiles), AX_X, ALU.add))
                step(dve.reciprocal(rt[:, 8, 8:8 + tiles], tot))
                step(dve.tensor_tensor(comb[:, 0:tiles, :], both.rearrange("p (t e) -> p t e", t=tiles),
                                       rt[:, 8, 8:8 + tiles].unsqueeze(2).to_broadcast([P, tiles, 16]), ALU.mult))

                for k in range(KD):
                    dve.wait_ge(xhi_rd, KD * layer + k + 1)
                    cols = slice(k * P, (k + 1) * P)
                    dve.tensor_tensor(x_lo[:, 0:tiles, cols], ps[:, k % 4, 0:tiles * P].rearrange("p (t n) -> p t n", t=tiles),
                                      x_hi[:, 0:tiles, cols].bitcast(F32), ALU.subtract).then_inc(xlo_rd, 1)

                dve.wait_ge(rank_ps, layer + 1)
                rank = ps[:, 5, 0:4 * G].rearrange("p (t e) -> p t e", t=tiles)
                mine = routed[:, 0:tiles, :]
                step(dve.scalar_tensor_tensor(rank_e[:, 0:tiles, :], rank, 1.0, mine, ALU.add, ALU.mult))
                step(dve.tensor_scalar(rank_e[:, 0:tiles, :], rank_e[:, 0:tiles, :], 1.0, None, ALU.subtract))
                step.add(dve.tensor_reduce(small[:, 48:49], ps[:, 5, 64:80], AX_X, ALU.max))
                key = [rt[:, 2 + n, 0:4 * G].rearrange("p (t e) -> p t e", t=tiles) for n in range(2)]
                place = rt[:, 4, 0:4 * G].rearrange("p (t e) -> p t e", t=tiles)
                step(dve.tensor_tensor(place, rank_e[:, 0:tiles, :], ekey[:, :].unsqueeze(1).to_broadcast([P, tiles, 16]),
                                       ALU.add))
                step(dve.tensor_copy(count_i[:, :], small[:, 48:49]))
                for p in range(1, tiles):
                    step(dve.tensor_scalar(key[0], rank_e[:, 0:tiles, :], float(P * p), float((N_EXPERTS - 1) * P),
                                           ALU.is_ge, ALU.mult))
                    step(dve.tensor_tensor(place, place, key[0], ALU.add))
                for two, far in enumerate((FAR, -1.0)):
                    step(dve.scalar_tensor_tensor(key[two], place, far, mine, ALU.subtract, ALU.mult))
                    step(dve.tensor_scalar(key[two], key[two], far, None, ALU.add))
                    step(dve.tensor_reduce(two_at[:, two, 0:tiles], key[two], AX_X, (ALU.min, ALU.max)[two]))
                    step.add(dve.tensor_copy(two_idx[:, two, 0:tiles], two_at[:, two, 0:tiles]))
                    step(dve.tensor_tensor(key[two], key[two], two_at[:, two, 0:tiles].unsqueeze(2).to_broadcast([P, tiles, 16]),
                                           ALU.is_equal))
                    step(dve.tensor_tensor(key[two], key[two], comb[:, 0:tiles, :], ALU.mult))
                    ins = dve.tensor_reduce(two_w[:, two, 0:tiles], key[two], AX_X, ALU.add)
                    if two == 0:
                        step(ins)
                    else:
                        ins.then_inc(rt_rd, 1)

            def experts(layer):
                tiles = (4, 2)[layer]

                def first(e):
                    return e + layer * N_EXPERTS

                def choose(e, where):
                    for t in range(tiles):
                        ins = dve.tensor_scalar(pick[:, t, :], slots[:, :], rank_e[:, t, bass.ds(e, 1)], None, ALU.is_equal)
                    ins.then_inc(where, 1)

                def pick_rows(e):
                    if not (isinstance(e, int) and first(e) == 0):
                        dve.wait_ge(pick_ps, first(e) * 2)
                    choose(e, pick_rd)

                def low(e, j, i):
                    m, half = i // 2, i % 2
                    dve.wait_ge(whi_rd, first(e) * HALVES + (i + 1))
                    b = (j * HALVES + i) % SPLITS
                    dve.tensor_tensor(w_lo[:, b, :], ring[:, expert_slot(layer, m)[0], half * HALF:(half + 1) * HALF],
                                      w_hi[:, b, :].bitcast(F32), ALU.subtract).then_inc(wlo_rd, 1)

                def turned(e, c):
                    dve.wait_ge(xgh_rd, first(e) * 2 + (c + 1))
                    dve.tensor_tensor(xg_lo[:, 4 * c:4 * c + 4, :].rearrange("p k n -> p (k n)"), ps[:, (4, 0)[c], :],
                                      xg_hi[:, 4 * c:4 * c + 4, :].bitcast(F32).rearrange("p k n -> p (k n)"),
                                      ALU.subtract).then_inc(xgl_rd, 1)

                def body(e, j, last):
                    if not last:
                        pick_rows(e + 1)
                    for i in range(3, HALVES):
                        low(e, j, i)
                    dve.wait_ge(silu_rd, first(e) + 1)
                    dve.wait_ge(w_ps, first(e) * HALVES + 4)
                    dve.tensor_tensor(glu[:, :], glu[:, :], ps[:, 3, :], ALU.mult).then_inc(glu_rd, 1)
                    if not last:
                        low(e + 1, 1 - j, 0)
                    dve.wait_ge(ghi_rd, first(e) + 1)
                    dve.tensor_tensor(glu_lo[:, :, :].rearrange("p f n -> p (f n)"), ps[:, 7, :],
                                      glu_hi[:, :, :].bitcast(F32).rearrange("p f n -> p (f n)"), ALU.subtract).then_inc(glo_rd, 1)
                    if not last:
                        low(e + 1, 1 - j, 1)
                        turned(e + 1, 0)
                        turned(e + 1, 1)
                        low(e + 1, 1 - j, 2)

                pick_rows(0)
                low(0, 0, 0)
                low(0, 0, 1)
                for c in range(2):
                    turned(0, c)
                low(0, 0, 2)
                body(0, 0, False)
                with dve.Fori(0, N_EXPERTS // 2 - 1) as i:
                    body(i * 2 + 1, 1, False)
                    body(i * 2 + 2, 0, False)
                body(N_EXPERTS - 1, 1, True)
                dve.wait_ge(w_ps, (layer + 1) * N_EXPERTS * HALVES)
                dve.wait_ge(y_st, (layer + 1) * N_EXPERTS * 16)

                most = dve.value_load(count_i[0:1, 0:1], min_val=0, max_val=CAPACITY)
                with dve.If(most > P):
                    with dve.Fori(0, (4, 2)[layer] - 1) as p:
                        dve.tensor_scalar(rank_e[:, 0:tiles, :], rank_e[:, 0:tiles, :], float(P), None,
                                          ALU.subtract).then_inc(more_rank[layer], 1)
                        with dve.Fori(0, N_EXPERTS) as e:
                            g = p * N_EXPERTS + e
                            dve.wait_ge(more_rank[layer], p + 1)
                            choose(e, more_dve[layer])
                            dve.wait_ge(more_pe[layer], g * 4 + 2)
                            dve.tensor_copy(xg_f[:, :, :].rearrange("p (a k) n -> p a (k n)", a=2), ps[:, 0:2, :]
                                            ).then_inc(more_dve[layer], 1)
                            dve.wait_ge(more_act[layer], g + 1)
                            dve.tensor_tensor(glu[:, :], glu[:, :], ps[:, 3, :], ALU.mult).then_inc(more_dve[layer], 1)
                            dve.wait_ge(more_pe[layer], g * 4 + 4)
                            dve.tensor_copy(glu_t[:, :, :].rearrange("p f n -> p (f n)"), ps[:, 7, :]
                                            ).then_inc(more_dve[layer], 1)
                            dve.wait_ge(more_pe[layer], g * 4 + 5)
                            dve.tensor_copy(y_sb[:, :].rearrange("p (a n) -> p a n", a=2), ps[:, 5:7, :]
                                            ).then_inc(more_dve[layer], 1)

            def add_experts(layer, rows):
                dve.wait_ge(gr_rd, rows)
                for t in range((4, 2)[layer]):
                    one, other = y_two[:, t, 0, :], y_two[:, t, 1, :]
                    dve.wait_ge(two_rd, (0, 4)[layer] + t + 1)
                    step(dve.scalar_tensor_tensor(one, other, two_w[:, 1, t:t + 1], one, ALU.mult, ALU.add))
                    step(dve.tensor_tensor(one, one, gate_row[:, t // 2, :], ALU.mult))
                    dve.tensor_tensor(h[:, t, :], h[:, t, :], one, ALU.add).then_inc((h_rd, res_rd)[layer], 1)

            router(0)
            experts(0)
            diagonals(0, 5, 2)
            add_experts(0, 8)
            ada(3, 7)
            norm(2)

            for i in range(2, 5):
                in_low(1, i)
            for hd in range(4):
                dve.wait_ge(p1_ps, 5 + hd)
                dve.tensor_copy(kT[:, hd, :], ps[:, 4 + hd, :]).then_inc(p1_dve, 1)
            for half in range(2):
                for i in range(5 + 2 * half, 7 + 2 * half):
                    in_low(1, i)
                for t in range(4):
                    m = half * 4 + t
                    dve.wait_ge(p1_ps, 9 + m)
                    dve.tensor_copy(v1[:, t, half * 512:(half + 1) * 512], ps[:, m, :]).then_inc(p1_dve, 1)
            for i in range(9, OD_STEPS):
                in_low(1, i)
            dve.wait_ge(p1_ps, 20)
            step(dve.memset(reset, 1.0))
            step(dve.memset(reset.rearrange("p (n t) -> p n t", t=CHUNK)[:, :, 0:1], 0.0))

            for hd in range(HEADS):
                bank = (0, 4, 6, 0)[hd]
                dve.wait_ge(z_ps, hd + 1)
                for d in range(2):
                    gb = vec_b[:, 60 + 4 * d + hd:61 + 4 * d + hd]
                    dve.tensor_scalar(gates[:, hd, d, :], ps[:, bank + d, :], gb, None, ALU.add).then_inc(z_rd, 1)
            for pair in range(2):
                heads = slice(2 * pair, 2 * pair + 2)
                dve.wait_ge(zl_rd, pair + 1)
                step(dve.scalar_tensor_tensor(gates[:, heads], gates[:, heads], 0.0, gates_abs[:, heads],
                                              ALU.min, ALU.subtract))

            b3 = [bcum[:, d, :].rearrange("p (n t) -> p n t", t=CHUNK) for d in range(2)]
            l3 = [lmin[:, d, :].rearrange("p (n t) -> p n t", t=CHUNK) for d in range(2)]
            ends = [b3[0][:, :, CHUNK - 1:CHUNK], b3[1][:, :, 0:1]]

            def gate_sums(hd):
                step.add(dve.tensor_tensor_scan(bcum[:, 0, :], reset, gates[:, hd, 0, :], 0.0, ALU.mult, ALU.add))
                step(dve.tensor_tensor_scan(bcum[:, 1, ::-1], reset, gates[:, hd, 1, ::-1], 0.0, ALU.mult, ALU.add))

            def gate_rests(hd):
                dve.tensor_copy(gla_small[:, hd % 2, 0, :].unsqueeze(2), ends[0]).then_inc(bc_rd, 1)
                step.add(dve.tensor_copy(gla_small[:, hd % 2, 1, :].unsqueeze(2), ends[1]))
                for d in range(2):
                    ins = dve.tensor_tensor(l3[d], ends[d].to_broadcast([P, 8, CHUNK]), b3[d], ALU.subtract)
                    if d:
                        step.wait()
                        ins.then_inc(bc_rd, 1)
                    else:
                        step.add(ins)

            gate_sums(0)
            gate_rests(0)
            for hd in range(HEADS):
                dve.wait_ge(ee_rd, 4 * hd + 2)
                q2 = qT[:, hd, :].unsqueeze(1).to_broadcast([P, 2, 256])
                k2 = kT[:, hd, 0:256].unsqueeze(1).to_broadcast([P, 2, 256])
                dve.tensor_tensor(qdec[:, :, :], ebuf[:, :, 0:256], q2, ALU.mult).then_inc(qd_rd, 1)
                dve.tensor_tensor(kinc[:, :, :], ebuf[:, :, 256:512], k2, ALU.mult).then_inc(qd_rd, 1)
                dve.wait_ge(ee_rd, 4 * hd + 4)
                dve.tensor_tensor(kendT[:, :, :], absz[:, :, :], kT[:, hd, :].unsqueeze(1).to_broadcast([P, 2, 512]),
                                  ALU.mult).then_inc(ee_us, 1)
                dve.wait_ge(at_ps, hd + 1)
                dve.tensor_tensor(att[:, :, :, :], ps[:, 2, :].rearrange("p (d t n) -> p d t n", d=2, t=2),
                                  gla_mask[:, :, :].unsqueeze(2).to_broadcast([P, 2, 2, P]), ALU.mult).then_inc(att_rd, 1)
                if hd == 1:
                    ada(4, 3)
                for q in range(7):
                    if q == 2 and hd < HEADS - 1:
                        gate_sums(hd + 1)
                    elif q == 4 and hd < HEADS - 1:
                        gate_rests(hd + 1)
                    for d in range(2):
                        ch = (4 + q if q < 4 else q - 4) if d == 0 else 7 - q
                        dve.wait_ge(ds_ps, 14 * hd + 2 * q + d + 1)
                        if q == 0:
                            dve.tensor_copy(state[:, 0, d, :], ps[:, d, 0:DV]).then_inc(st_rd, 1)
                        else:
                            dve.wait_ge(st_rd, 14 * hd + 2 * (q - 1) + d + 1)
                            dve.scalar_tensor_tensor(state[:, q % 2, d, :], state[:, (q - 1) % 2, d, :],
                                                     gla_small[:, hd % 2, d, ch:ch + 1], ps[:, d, 0:DV],
                                                     ALU.mult, ALU.add).then_inc(st_rd, 1)
                dve.wait_ge(o_ps, hd + 1)

            ada(5, 3)
            dve.wait_ge(og_std, 1)
            step(dve.reciprocal(small[:, 16:24], small[:, 8:16]))
            for t in range(2):
                for hd in range(4):
                    src = ps[:, 4 + 2 * t + hd // 2, (hd % 2) * DV:(hd % 2 + 1) * DV]
                    step.add(dve.scalar_tensor_tensor(og[:, t, hd * DV:(hd + 1) * DV], src,
                                                      small[:, 16 + t * 4 + hd:17 + t * 4 + hd], g_out[:, :],
                                                      ALU.mult, ALU.mult))
                step.wait()
                dve.tensor_tensor(og[:, t, :], og[:, t, :], r_sb[:, t, :], ALU.mult).then_inc(og_rd, 1)
            dve.wait_ge(og_rd, 2)
            out_lows(1, 0)
            diagonals(1, 2, 1)
            out_lows(1, 1)
            for j in range(2):
                mixed_lows(1, j)
            for i in range(2, OUT_STEPS):
                out_lows(1, i)
            residual(1, 8, 10)
            norm(3)
            router(1)
            experts(1)
            diagonals(1, 5, 1)
            add_experts(1, 12)


_INS = ['x', 'c', 'ctx', 'c_ctx', 'router_w', 'router_bias', 'ada_w', 'ada_b', 'norm_mix_g', 'norm_ffn_g',
        'moe_w_gate', 'moe_w_up', 'moe_w_down', 'ev_w_in', 'ev_w_out', 'ev_conv_w', 'ev_conv_b',
        'ev_rg_w', 'ev_rg_b', 'ev_ig_w', 'ev_ig_b', 'ev_lambda', 'ev_q_norm_g', 'ev_k_norm_g', 'ev_sink',
        'od_w_in', 'od_w_out', 'od_gate_up', 'od_gate_b', 'od_out_norm_g']


def rope_tables(tokens, grid, head_dim):
    import numpy as np
    freqs = head_dim // 4
    inv = np.float32(10000.0) ** (-np.arange(freqs, dtype=np.float32) / np.float32(freqs))
    pos = np.arange(tokens)
    row = (pos // grid).astype(np.float32)[:, None] * inv
    col = (pos % grid).astype(np.float32)[:, None] * inv
    angle = np.concatenate([row, col], axis=1)
    return np.cos(angle).astype(np.float32), np.sin(angle).astype(np.float32)


def kernel(**inputs):
    import numpy as _np
    import concourse.bacc as _bacc
    from concourse import mybir as _mybir
    from concourse.bass_utils import run_bass_kernel_spmd as _run

    nc = _bacc.Bacc("TRN2", target_bir_lowering=False, num_devices=1)
    arrays, args = {}, []
    for name in _INS:
        a = _np.ascontiguousarray(inputs[name])
        arrays[f"in_{name}_dram"] = a
        args.append(nc.dram_tensor(f"in_{name}_dram", a.shape, _mybir.dt.from_np(a.dtype), kind="ExternalInput").ap())
    for name, a in zip(("rope_cos", "rope_sin"), rope_tables(256, 64, 64)):
        arrays[f"in_{name}_dram"] = a
        args.append(nc.dram_tensor(f"in_{name}_dram", a.shape, _mybir.dt.float32, kind="ExternalInput").ap())
    args.append(nc.dram_tensor("out_0_dram", (1, 256, 1024), _mybir.dt.float32, kind="ExternalOutput").ap())
    build(nc, *args)
    r = _run(nc, [arrays], core_ids=[0])
    return r.results[0]["out_0_dram"]
```
